# Optimizing a Trainium2 kernel written in Bass

```python
import math
import jax, jax.numpy as jnp
from jax import lax
import numpy as np

D_MODEL = 2048
BATCH = 1
SEQ = 256
DEPTH = 1

CHUNK = 64
Q_BLOCK = 128
TOKEN_BLOCK = 128

SSM_WIDTH = 1024
SSM_GROUP = 16
SSM_GROUPS = SSM_WIDTH // SSM_GROUP
SSM_STATE = 64
DT_MIN = 1e-3
DT_MAX = 1e-1

N_HEADS = 16
Q_LORA = 512
KV_LORA = 512
QK_NOPE = 128
QK_ROPE = 64
V_HEAD = 128
QK_HEAD = QK_NOPE + QK_ROPE
ROPE_THETA = 10000.0

PEER_HEADS = 8
N_KEYS = 128
N_EXPERTS = N_KEYS * N_KEYS
PEER_KEY_HALF = 128
PEER_TOPK = 16

LN_EPS = 1e-5
RMS_EPS = 1e-6
DEEPNORM_ALPHA = (2.0 * DEPTH) ** 0.25
DEEPNORM_BETA = (8.0 * DEPTH) ** -0.25

OFF_SSM = 0
OFF_Q = OFF_SSM + SSM_WIDTH
OFF_KV = OFF_Q + Q_LORA
OFF_KR = OFF_KV + KV_LORA
OFF_GA = OFF_KR + QK_ROPE
OFF_GS = OFF_GA + D_MODEL
IN_WIDTH = OFF_GS + D_MODEL

kernel_name = "hybrid_s5_mla_peer_deepnorm"

def layer_norm(x, g, b):
    xf = x.astype(jnp.float32)
    mu = jnp.mean(xf, axis=-1, keepdims=True)
    var = jnp.mean(jnp.square(xf - mu), axis=-1, keepdims=True)
    y = (xf - mu) * lax.rsqrt(var + LN_EPS) * g.astype(jnp.float32) + b.astype(jnp.float32)
    return y.astype(x.dtype)

def rms_norm(x, g):
    xf = x.astype(jnp.float32)
    y = xf * lax.rsqrt(jnp.mean(jnp.square(xf), axis=-1, keepdims=True) + RMS_EPS) * g.astype(jnp.float32)
    return y.astype(x.dtype)

def apply_rope(x):
    S = x.shape[1]
    half = QK_ROPE // 2
    inv_freq = 1.0 / (ROPE_THETA ** (jnp.arange(half, dtype=jnp.float32) / half))
    ang = jnp.arange(S, dtype=jnp.float32)[:, None] * inv_freq[None, :]
    cos = jnp.cos(ang)[None, :, None, :]
    sin = jnp.sin(ang)[None, :, None, :]
    xf = x.astype(jnp.float32)
    x1, x2 = xf[..., :half], xf[..., half:]
    out = jnp.concatenate([x1 * cos - x2 * sin, x1 * sin + x2 * cos], axis=-1)
    return out.astype(x.dtype)

def chunk_causal_attention(q, k, v):
    Bsz, S, H, Dq = q.shape
    nb = S // Q_BLOCK
    scale = 1.0 / math.sqrt(QK_HEAD)
    q_blocks = q.reshape(Bsz, nb, Q_BLOCK, H, Dq).transpose(1, 0, 2, 3, 4)
    k_chunk = jnp.arange(S) // CHUNK
    neg = jnp.finfo(jnp.float32).min

    def one_block(args):
        qi, bi = args
        s = jnp.einsum('bqhd,bkhd->bhqk', qi, k).astype(jnp.float32) * scale
        q_chunk = (bi * Q_BLOCK + jnp.arange(Q_BLOCK)) // CHUNK
        mask = k_chunk[None, :] <= q_chunk[:, None]
        p = jax.nn.softmax(jnp.where(mask[None, None], s, neg), axis=-1)
        return jnp.einsum('bhqk,bkhd->bqhd', p.astype(v.dtype), v)

    out = lax.map(one_block, (q_blocks, jnp.arange(nb)))
    return out.transpose(1, 0, 2, 3, 4).reshape(Bsz, S, H, v.shape[-1])

def s5_ssm(u, lam_re, lam_im, log_dt, b_re, b_im, c_re, c_im, d_skip):
    Bsz, S, _ = u.shape
    G, P, Hg = SSM_GROUPS, SSM_STATE, SSM_GROUP
    uf = u.astype(jnp.float32).reshape(Bsz, S, G, Hg)
    dt = jnp.exp(log_dt.astype(jnp.float32))[:, None]
    lr = lam_re.astype(jnp.float32)
    li = lam_im.astype(jnp.float32)
    mag = jnp.exp(lr * dt)
    ab_re = mag * jnp.cos(li * dt)
    ab_im = mag * jnp.sin(li * dt)
    den = lr * lr + li * li
    nr = ab_re - 1.0
    ni = ab_im
    coef_re = (nr * lr + ni * li) / den
    coef_im = (ni * lr - nr * li) / den
    br = b_re.astype(jnp.float32)
    bi = b_im.astype(jnp.float32)
    bb_re = coef_re[..., None] * br - coef_im[..., None] * bi
    bb_im = coef_re[..., None] * bi + coef_im[..., None] * br
    bu_re = jnp.einsum('bsgh,gph->bsgp', uf, bb_re)
    bu_im = jnp.einsum('bsgh,gph->bsgp', uf, bb_im)
    a_re = jnp.broadcast_to(ab_re[None, None], (1, S, G, P))
    a_im = jnp.broadcast_to(ab_im[None, None], (1, S, G, P))

    def combine(e1, e2):
        a1r, a1i, b1r, b1i = e1
        a2r, a2i, b2r, b2i = e2
        return (a2r * a1r - a2i * a1i,
                a2r * a1i + a2i * a1r,
                a2r * b1r - a2i * b1i + b2r,
                a2r * b1i + a2i * b1r + b2i)

    _, _, x_re, x_im = lax.associative_scan(combine, (a_re, a_im, bu_re, bu_im), axis=1)
    y = (jnp.einsum('bsgp,ghp->bsgh', x_re, c_re.astype(jnp.float32))
         - jnp.einsum('bsgp,ghp->bsgh', x_im, c_im.astype(jnp.float32)))
    y = y + d_skip.astype(jnp.float32).reshape(G, Hg) * uf
    return y.reshape(Bsz, S, SSM_WIDTH).astype(u.dtype)

def hybrid_mixer(h, w_in, q_norm_g, w_uq, kv_norm_g, w_ukv, lam_re, lam_im, log_dt,
                 b_re, b_im, c_re, c_im, d_skip, w_glu, w_proj_attn, w_proj_ssm, w_out):
    Bsz, S, _ = h.shape
    z = h @ w_in
    u_ssm = z[..., OFF_SSM:OFF_Q]
    c_q = z[..., OFF_Q:OFF_KV]
    c_kv = z[..., OFF_KV:OFF_KR]
    k_r = z[..., OFF_KR:OFF_GA]
    g_attn = z[..., OFF_GA:OFF_GS]
    g_ssm = z[..., OFF_GS:IN_WIDTH]

    q = (rms_norm(c_q, q_norm_g) @ w_uq).reshape(Bsz, S, N_HEADS, QK_HEAD)
    q = jnp.concatenate([q[..., :QK_NOPE], apply_rope(q[..., QK_NOPE:])], axis=-1)
    kv = (rms_norm(c_kv, kv_norm_g) @ w_ukv).reshape(Bsz, S, N_HEADS, QK_NOPE + V_HEAD)
    k_rope = apply_rope(k_r[:, :, None, :])
    k = jnp.concatenate([kv[..., :QK_NOPE],
                         jnp.broadcast_to(k_rope, (Bsz, S, N_HEADS, QK_ROPE))], axis=-1)
    v = kv[..., QK_NOPE:]
    attn = chunk_causal_attention(q, k, v).reshape(Bsz, S, N_HEADS * V_HEAD)

    y = jax.nn.gelu(s5_ssm(u_ssm, lam_re, lam_im, log_dt, b_re, b_im, c_re, c_im, d_skip))
    ssm = y * jax.nn.sigmoid(y @ w_glu)

    merged = jax.nn.sigmoid(g_attn) * (attn @ w_proj_attn) + jax.nn.sigmoid(g_ssm) * (ssm @ w_proj_ssm)
    return merged @ w_out

def peer_ffn(h, w_pq, sub_keys, u_tab, v_tab):
    Bsz, S, D = h.shape
    K = PEER_TOPK
    q = (h @ w_pq).reshape(Bsz, S, PEER_HEADS, 2, PEER_KEY_HALF)
    s = jnp.einsum('bshcd,hcnd->bshcn', q, sub_keys).astype(jnp.float32)
    v1, i1 = lax.top_k(s[..., 0, :], K)
    v2, i2 = lax.top_k(s[..., 1, :], K)
    cand = (v1[..., :, None] + v2[..., None, :]).reshape(Bsz, S, PEER_HEADS, K * K)
    top, pos = lax.top_k(cand, K)
    expert = (jnp.take_along_axis(i1, pos // K, axis=-1) * N_KEYS
              + jnp.take_along_axis(i2, pos % K, axis=-1))
    gate = jax.nn.softmax(top, axis=-1)

    n_blk = (Bsz * S) // TOKEN_BLOCK
    hb = h.reshape(n_blk, TOKEN_BLOCK, D)
    eb = expert.reshape(n_blk, TOKEN_BLOCK, PEER_HEADS * K)
    gb = gate.reshape(n_blk, TOKEN_BLOCK, PEER_HEADS * K).astype(h.dtype)

    def one_block(args):
        xt, et, gt = args
        u = u_tab[et]
        act = jax.nn.gelu(jnp.einsum('td,tkd->tk', xt, u))
        return jnp.einsum('tk,tkd->td', gt * act, v_tab[et])

    out = lax.map(one_block, (hb, eb, gb))
    return out.reshape(Bsz, S, D)

def setup_inputs(seed: int = 0) -> dict:
    key = jax.random.key(seed)
    ks = jax.random.split(key, 40)
    f32 = jnp.float32
    L = DEPTH

    def nrm(k, shape, scale):
        return jax.random.normal(k, shape, f32) * scale

    n_idx = jnp.arange(SSM_STATE, dtype=f32)
    return {
        "x": nrm(ks[0], (BATCH, SEQ, D_MODEL), 1.0),
        "ln_in_g": 1.0 + nrm(ks[1], (D_MODEL,), 0.02),
        "ln_in_b": nrm(ks[2], (D_MODEL,), 0.02),
        "w_in": nrm(ks[3], (L, D_MODEL, IN_WIDTH), D_MODEL ** -0.5),
        "q_norm_g": 1.0 + nrm(ks[4], (L, Q_LORA), 0.02),
        "w_uq": nrm(ks[5], (L, Q_LORA, N_HEADS * QK_HEAD), Q_LORA ** -0.5),
        "kv_norm_g": 1.0 + nrm(ks[6], (L, KV_LORA), 0.02),
        "w_ukv": nrm(ks[7], (L, KV_LORA, N_HEADS * (QK_NOPE + V_HEAD)), KV_LORA ** -0.5),
        "ssm_lam_re": -0.5 + nrm(ks[8], (L, SSM_GROUPS, SSM_STATE), 0.01),
        "ssm_lam_im": math.pi * n_idx + nrm(ks[9], (L, SSM_GROUPS, SSM_STATE), 0.01),
        "ssm_log_dt": jax.random.uniform(ks[10], (L, SSM_GROUPS), f32, math.log(DT_MIN), math.log(DT_MAX)),
        "ssm_b_re": nrm(ks[11], (L, SSM_GROUPS, SSM_STATE, SSM_GROUP), (2.0 * SSM_GROUP) ** -0.5),
        "ssm_b_im": nrm(ks[12], (L, SSM_GROUPS, SSM_STATE, SSM_GROUP), (2.0 * SSM_GROUP) ** -0.5),
        "ssm_c_re": nrm(ks[13], (L, SSM_GROUPS, SSM_GROUP, SSM_STATE), SSM_STATE ** -0.5),
        "ssm_c_im": nrm(ks[14], (L, SSM_GROUPS, SSM_GROUP, SSM_STATE), SSM_STATE ** -0.5),
        "ssm_d": nrm(ks[15], (L, SSM_WIDTH), 1.0),
        "w_glu": nrm(ks[16], (L, SSM_WIDTH, SSM_WIDTH), SSM_WIDTH ** -0.5),
        "w_proj_attn": nrm(ks[17], (L, N_HEADS * V_HEAD, D_MODEL), (N_HEADS * V_HEAD) ** -0.5),
        "w_proj_ssm": nrm(ks[18], (L, SSM_WIDTH, D_MODEL), SSM_WIDTH ** -0.5),
        "w_out": nrm(ks[19], (L, D_MODEL, D_MODEL), DEEPNORM_BETA * D_MODEL ** -0.5),
        "ln_mix_g": 1.0 + nrm(ks[20], (L, D_MODEL), 0.02),
        "ln_mix_b": nrm(ks[21], (L, D_MODEL), 0.02),
        "w_peer_q": nrm(ks[22], (L, D_MODEL, PEER_HEADS * 2 * PEER_KEY_HALF), D_MODEL ** -0.5),
        "peer_sub_keys": nrm(ks[23], (L, PEER_HEADS, 2, N_KEYS, PEER_KEY_HALF), PEER_KEY_HALF ** -0.5),
        "peer_u": nrm(ks[24], (L, N_EXPERTS, D_MODEL), D_MODEL ** -0.5),
        "peer_v": nrm(ks[25], (L, N_EXPERTS, D_MODEL), DEEPNORM_BETA),
        "ln_ffn_g": 1.0 + nrm(ks[26], (L, D_MODEL), 0.02),
        "ln_ffn_b": nrm(ks[27], (L, D_MODEL), 0.02),
    }

def reference(x, ln_in_g, ln_in_b, w_in, q_norm_g, w_uq, kv_norm_g, w_ukv,
              ssm_lam_re, ssm_lam_im, ssm_log_dt, ssm_b_re, ssm_b_im, ssm_c_re, ssm_c_im, ssm_d,
              w_glu, w_proj_attn, w_proj_ssm, w_out, ln_mix_g, ln_mix_b,
              w_peer_q, peer_sub_keys, peer_u, peer_v, ln_ffn_g, ln_ffn_b):
    h = layer_norm(x, ln_in_g, ln_in_b)
    for l in range(DEPTH):
        y = hybrid_mixer(h, w_in[l], q_norm_g[l], w_uq[l], kv_norm_g[l], w_ukv[l],
                         ssm_lam_re[l], ssm_lam_im[l], ssm_log_dt[l], ssm_b_re[l], ssm_b_im[l],
                         ssm_c_re[l], ssm_c_im[l], ssm_d[l], w_glu[l],
                         w_proj_attn[l], w_proj_ssm[l], w_out[l])
        h = layer_norm(DEEPNORM_ALPHA * h + y, ln_mix_g[l], ln_mix_b[l])
        y = peer_ffn(h, w_peer_q[l], peer_sub_keys[l], peer_u[l], peer_v[l])
        h = layer_norm(DEEPNORM_ALPHA * h + y, ln_ffn_g[l], ln_ffn_b[l])
    return h


_drawn_inputs = setup_inputs


def setup_inputs(seed=0):
    import zlib

    import numpy as np

    out = dict(_drawn_inputs(seed))
    spreads = {}
    factors = {'q_norm_g': 6.972,
     'kv_norm_g': 5.275,
     'ssm_lam_re': 8.0,
     'ssm_b_re': 2.813,
     'ssm_b_im': 2.68,
     'ssm_c_re': 2.823,
     'ssm_c_im': 2.914,
     'ln_ffn_g': 2.895,
     'ln_ffn_b': 2.826}
    for name, (base, spread) in spreads.items():
        noise = np.random.default_rng([zlib.crc32(name.encode()), seed]).standard_normal(out[name].shape)
        drawn = base * np.exp(spread * noise) if base else spread * noise
        out[name] = __import__('jax').numpy.asarray(drawn.astype(out[name].dtype))
    for name, factor in factors.items():
        out[name] = (out[name] * factor).astype(out[name].dtype)
    return out
```

```python
import math
from contextlib import ExitStack

import numpy as np
import concourse.bass as bass
import concourse.mybir as mybir

F32 = mybir.dt.float32
F32R = mybir.dt.float32r
U32 = mybir.dt.uint32
ACT = mybir.ActivationFunctionType
ALU = mybir.AluOpType
AX_X = mybir.AxisListType.X

P = 128
T = 256
TT = T // P
D = 2048
KC = D // P
SSM = 1024
QL = 512
ROPE = 64
HEADS = 16
NOPE = 128
NKEY = 128
PH = 8
TOPK = 16
NE = NKEY * NKEY
SW = 2048
UW = SW // 2
STILES = 32
TH = 128
LN_EPS, RMS_EPS = 1e-5, 1e-6
ALPHA = 2.0 ** 0.25
SCALE = 1.0 / math.sqrt(NOPE + ROPE)
MASKED = -3.0e38
LOWEST = -3.4028235e38
BASE = 640
HALF = NKEY // 2

STAGES = [("ssm_in", 8), ("gates", 32), ("latent", 9), ("glu", 4), ("proj_ssm", 8), ("q_nope", 4), ("q_rope", 2),
          ("k_nope", 4), ("value", 4), ("proj_attn", 16), ("out", 16), ("peer_q", 16),
          ("u0", HALF), ("v0", HALF), ("u1", HALF), ("v1", HALF)]
GROUPS = [("t_in", 8, "D"), ("t_bb", 4, "A"), ("ssm_in", 8, "D"), ("gates", 16, "A"), ("latent", 6, "A"),
          ("glu", 8, "D"), ("proj_ssm", 8, "D"), ("t_lat", 5, "D"), ("q_nope", 16, "D"), ("q_rope", 4, "A"),
          ("t_qr", 4, "A"), ("k_nope", 16, "D"), ("value", 8, "A"), ("attn", 16, "D"), ("proj_attn", 8, "D"),
          ("t_mix", 8, "D"), ("out", 8, "D"), ("t_h", 8, "D"), ("peer_q", 16, "D"), ("scores", 8, "A"),
          ("u0", HALF, "D"), ("v0", 8, "D"), ("u1", HALF, "D"), ("v1", 8, "D")]
COLUMN_FORM = ["ssm_in", "glu", "q_nope", "k_nope", "peer_q", "u0", "u1"]
TRANSPOSED = ["t_in", "t_bb", "t_lat", "t_qr", "t_mix", "t_h"]
SPLIT_TRANSPOSED = ["t_in", "t_lat", "t_mix", "t_h"]


def starts(pairs):
    at, out = 0, {}
    for name, n in pairs:
        out[name] = at
        at += n
    return out, at


BLOCK0, NBLOCK = starts(STAGES)
GROUP0, _ = starts([(n, k) for n, k, _ in GROUPS])
SIZE = {n: k for n, k, _ in GROUPS}
EMPTIER = {n: e for n, _, e in GROUPS}
EMPTIED0 = {e: starts([(n, k) for n, k, x in GROUPS if x == e])[0] for e in "DA"}
TMP0, _ = starts([(n, SIZE[n]) for n in COLUMN_FORM])
TP0, _ = starts([(n, SIZE[n]) for n in TRANSPOSED])
TH0, _ = starts([(n, 4 if n == "t_lat" else SIZE[n]) for n in SPLIT_TRANSPOSED])
FLAT = [(n, k) for n, size, _ in GROUPS for k in range(size)]
NUNIT = 2 * NBLOCK


def build(nc, a, out):
    with ExitStack() as ctx:
        def sem(name):
            return ctx.enter_context(nc.semaphore(name))

        def at(name, kib, shape, dt=F32, more=0):
            return nc.alloc_sbuf_tensor_at(name, shape, dt, offset=BASE + int(kib * 1024) + more)

        bank = [ctx.enter_context(nc.psum_tensor(f"bank{i}", [P, 512], F32)) for i in range(8)]

        raw = [at(f"raw{i}", 8 * i, [P, SW]) for i in range(4)]
        hi = [at(f"hi{i}", 32 + 4 * i, [P, UW], F32R) for i in range(4)]
        lo = [at(f"lo{i}", 48 + 4 * i, [P, UW], F32R) for i in range(4)]
        actT = at("actT", 64, [P, KC, 2, T], F32R)
        glu_s = at("glu_s", 64, [P, 8, T])
        qr_rows = at("qr_rows", 64, [P, TT, 1024])
        qr_rot = at("qr_rot", 72, [P, TT, 1024])
        rope_m = at("rope_m", 80, [P, 2, 1024])
        ln_out_gb = at("ln_out_gb", 64, [P, 2, D])
        res = at("res", 96, [P, TT, D])
        ln_in_gb = at("ln_in_gb", 112, [P, 2, D])
        gates = at("gates", 112, [P, 8, TT, 512])
        bb_rows = at("bb_rows", 128, [P, 2, 8, P])
        b_in = at("b_in", 136, [P, 2, STILES, 16])
        c_in = at("c_in", 140, [P, 2, STILES, 16])
        W = at("W", 112, [P, HALF, T])
        table = at("table", 144, [P, STILES, 2, TH])
        yT = at("yT", 144, [P, 8, 2, T], F32R)
        ssmT = at("ssmT", 160, [P, 8, 2, T], F32R)
        qT = at("qT", 144, [P, HEADS, T])
        kT = at("kT", 160, [P, HEADS, T])
        uT = at("uT", 176, [P, 8, T])
        qrT = at("qrT", 176, [P, 8, T])
        keysT = at("keysT", 176, [P, 16, NKEY])
        bbT = at("bbT", 184, [P, 16, P])
        c_blk = at("c_blk", 192, [P, STILES, 2, 32])
        lat = at("lat", 184, [P, TT, 1088])
        latT = at("latT", 192.5, [P, 8, 2, T], F32R)
        kr_rows = at("kr_rows", 215, [P, TT, P])
        lat_g = at("lat_g", 208.5, [P, 2, QL])
        v0 = at("v0", 184, [P, D])
        v1 = at("v1", 208.5, [P, D])
        sm_p = [at(f"sm_p{i}", 193 + 1.5 * i, [P, 384]) for i in range(2)]
        sm_pT = [at(f"sm_pT{i}", 196 + 1.5 * i, [P, 384]) for i in range(2)]
        ln_mix_gb = at("ln_mix_gb", 184, [P, 2, D])
        s_all = at("s_all", 184, [P, 16, 2, NKEY])
        pqT = at("pqT", 200, [P, 16, T])
        rot_m = [at(f"rot_m{i}", 200 + 2 * i, [P, 2, T]) for i in range(2)]
        z = [at(f"z{i}", 204 + 2 * i, [P, 2, T]) for i in range(2)]
        xs = [at(f"xs{i}", 208 + 2 * i, [P, 2, T]) for i in range(2)]
        xs_m = at("xs_m", 212, [P, 2, T])
        prm = at("prm", 200, [P, 32, STILES])
        pw = at("pw", 212, [P, 8, 2, STILES])
        tab_m = [at(f"tab_m{i}", 204 + 4 * i, [P, 16, 64]) for i in range(2)]
        bb_m = [at(f"bb_m{i}", 184 + 2 * i, [P, STILES, 16]) for i in range(2)]
        tk_s = at("tk_s", 200, [P, 2, NKEY])
        tk_s2 = at("tk_s2", 201, [P, 2, NKEY])
        tk_cand = at("tk_cand", 202, [P, 16, 16])
        tk_cand2 = at("tk_cand2", 203, [P, 16, 16])
        tk_eq = at("tk_eq", 204, [P, 16, 16])
        tk_v = at("tk_v", 205, [P, 2, 16])
        tk_i = at("tk_i", 205, [P, 2, 16], U32, 128)
        tk_if = at("tk_if", 205, [P, 2, 16], F32, 256)
        tk_top = at("tk_top", 205, [P, 16], F32, 384)
        tk_pos = at("tk_pos", 205, [P, 16], U32, 448)
        tk_pu = at("tk_pu", 205, [P, 2, 16], U32, 512)
        tk_pf = at("tk_pf", 205, [P, 2, 16], F32, 640)
        tk_sel = at("tk_sel", 205, [P, 2, 16], F32, 768)
        picked = at("picked", 206, [P, 3, 16, 16])
        gsum = at("gsum", 209, [P, 4, 16])
        hkT = at("hkT", 210, [P, 3, T])
        iota = at("iota", 213, [P, NKEY])
        tok = [at(f"tok{i}", 213.5, [P, 3, 8], F32, 96 * i) for i in range(2)]
        oneA = [at(f"oneA{i}", 184 + 4 * i, [P, 8, NKEY]) for i in range(2)]
        oneB = [at(f"oneB{i}", 192 + 2 * i, [P, 8, HALF]) for i in range(2)]
        wh = [at(f"wh{i}", 196 + i, [P, T], F32R) for i in range(2)]
        wl = [at(f"wl{i}", 198 + i, [P, T], F32R) for i in range(2)]
        C0 = 216.5
        ident = at("ident", C0, [P, P])
        tmp = [at(f"tmp{i}", C0, [P, T], F32, 512 + 1024 * i) for i in range(2)]
        rope = at("rope", C0, [P, TT, 2, 32], F32, 2560)
        mag = at("mag", C0, [P, STILES], F32, 3072)
        wTH = at("wTH", C0, [P, 2, STILES], F32, 3200)
        dskip = at("dskip", C0, [P, 8], F32, 3456)
        stats = at("stats", C0, [P, TT, 4, 6], F32, 3488)
        mv = at("mv", C0, [P, TT, 2], F32, 3680)
        rs = at("rs", C0, [P, 8], F32, 3712)
        krT = at("krT", C0, [P, T], F32, 3744)
        mask = at("mask", C0, [P, 384], F32, 4768)
        iota16 = at("iota16", C0, [P, 16], F32, 6304)
        ini = at("ini", C0, [P, 8], F32, 6368)
        smx = [at(f"smx{i}", C0, [P, 8], F32, 6400 + 32 * i) for i in range(2)]
        v01 = [v0, v1]

        s_raw = [sem(f"raw_landed{i}") for i in range(4)]
        s_hi, s_lo, s_mm = sem("hi_made"), sem("lo_made"), sem("unit_multiplied")
        s_ev = {"D": sem("bank_emptied_by_vector"), "A": sem("bank_emptied_by_scalar")}
        s_tmp = sem("second_half_copied")
        s_tp, s_th = sem("transposed"), sem("transposed_hi_made")
        s_x, s_par, s_gb, s_id = sem("x_landed"), sem("ssm_params_landed"), sem("ln_gb_landed"), sem("ident_landed")
        s_const = sem("constants_landed")
        s_dve, s_act, s_pool = sem("vector_step"), sem("scalar_step"), sem("pool_step")
        s_var, s_std = sem("variance_made"), sem("deviation_made")
        s_rows, s_rowfree = sem("rows_ready"), sem("norm_rows_used")
        s_prm, s_prmA = sem("ssm_prm_by_vector"), sem("ssm_prm_by_scalar")
        s_pw, s_tab, s_bb = sem("powers_ready"), sem("tables_ready"), sem("bb_ready")
        s_bu, s_bufree, s_z, s_xr, s_cy, s_y, s_gel = (sem("bu_made"), sem("bu_used"), sem("z_made"), sem("x_made"),
                                                       sem("cx_made"), sem("y_made"), sem("y_gelu"))
        s_yh, s_yl = sem("y_hi_made"), sem("y_lo_made")
        s_sig, s_glu, s_sh, s_sl = sem("glu_sigmoid"), sem("glu_product"), sem("ssm_hi_made"), sem("ssm_lo_made")
        s_sq, s_latg = sem("squares_made"), sem("latent_gain_landed")
        s_qr, s_krot = sem("q_rotated"), sem("k_rotated")
        s_S, s_P, s_E, s_Pn, s_PT, s_PTs, s_PV, s_pvh = (sem("scores_made"), sem("scores_masked"), sem("exp_made"),
                                                         sem("probs_ready"), sem("probs_transposed"),
                                                         sem("probsT_copied"), sem("head_multiplied"), sem("head_hi_made"))
        s_keys, s_topped, s_gexp, s_picked = sem("keys_landed"), sem("top_ready"), sem("gate_exp"), sem("picked_ready")
        s_hk, s_hkT, s_one, s_G, s_Gev = (sem("hk_transposed"), sem("hkT_copied"), sem("one_hots"),
                                                  sem("gate_matrix"), sem("gates_applied"))
        s_gel2, s_whm, s_wlm, s_tok = sem("expert_gelu"), sem("w_hi_made"), sem("w_lo_made"), sem("tokens_copied")
        s_top = sem("top_step")
        s_iota, s_outd = sem("iota_made"), sem("out_written")
        block = ctx.enter_context(nc.Block())

        def emptied(stage, k):
            e = EMPTIER[stage]
            return s_ev[e], EMPTIED0[e][stage] + k + 1

        def bank_of(stage, k):
            return bank[(GROUP0[stage] + k) % 4]

        def wait_bank_free(pe, stage, k):
            n = GROUP0[stage] + k
            if n >= 4:
                pe.wait_ge(*emptied(*FLAT[n - 4]))

        def unit0(stage):
            return 2 * BLOCK0[stage]

        class Chain:

            def __init__(self, eng, s):
                self.eng, self.s, self.n, self.extra = eng, s, 0, 0

            def __call__(self, ins):
                self.n += 1
                ins.then_inc(self.s, 1)
                self.eng.wait_ge(self.s, self.n + self.extra)

            def enter(self, i, per):
                self.at, self.per, self.extra = self.n, per, i * per

            def leave(self, count):
                assert self.n - self.at == self.per, (self.n - self.at, self.per)
                self.n, self.extra = self.at + self.per * count, 0

        @block.sync
        def _(sp):
            x_rows = a["x"].rearrange("(t p) d -> t p d", p=P)
            for t in range(TT):
                sp.dma_start(res[:, t, :], x_rows[t]).then_inc(s_x, 16)

            def load(b, i=None):
                n = b if i is None else i * 4 + b
                if b >= 4:
                    sp.wait_ge(s_lo, n * 2 - 6)
                sp.dma_start(raw[b % 4][:], a["stream"][n]).then_inc(s_raw[b % 4], 16)

            for b in range(4):
                load(b)
            loops = (NBLOCK - 4) // 4
            with sp.Fori(0, loops) as i:
                for j in range(4):
                    load(4 + j, i)
            for b in range(4 + 4 * loops, NBLOCK):
                load(b)
            for t in range(TT):
                sp.wait_ge(s_rows, 2 * TT + t + 1)
                sp.dma_start(out.rearrange("(t p) d -> t p d", p=P)[t], res[:, t, :]).then_inc(s_outd, 16)
            sp.wait_ge(s_outd, 16 * TT)

        @block.scalar
        def _(act):
            step = Chain(act, s_act)
            act.dma_start(prm[:, 0, :], a["lam_re"]).then_inc(s_par, 16)
            act.dma_start(prm[:, 1, :], a["lam_im"]).then_inc(s_par, 16)
            for g in range(2):
                act.dma_start(prm[64 * g:64 * g + 64, 2, :],
                               a["log_dt"][g:g + 1, :].broadcast_to([64, STILES])).then_inc(s_par, 16)
            act.dma_start(b_in[:, 0], a["b_re"]).then_inc(s_par, 16)
            act.dma_start(b_in[:, 1], a["b_im"]).then_inc(s_par, 16)
            act.dma_start(c_in[:, 0], a["c_re"]).then_inc(s_par, 16)
            act.dma_start(c_in[:, 1], a["c_im"]).then_inc(s_par, 16)
            act.dma_start(ident[:], a["ident"]).then_inc(s_id, 16)
            act.dma_start(ln_in_gb[:, 0, :], a["ln_in_g"].broadcast_to([P, D])).then_inc(s_gb, 16)
            act.dma_start(ln_in_gb[:, 1, :], a["ln_in_b"].broadcast_to([P, D])).then_inc(s_gb, 16)
            act.dma_start(rope[:], a["rope"]).then_inc(s_const, 16)
            act.dma_start(dskip[:], a["dskip"]).then_inc(s_const, 16)

            def split(u, i=None, per=0):
                n = u if i is None else i * per + u
                b = u // 2
                if u % 2 == 0:
                    landed = 16 * (b // 4 + 1)
                    act.wait_ge(s_raw[b % 4], landed if i is None else i * (2 * per) + landed)
                if u >= 4:
                    act.wait_ge(s_mm, n - 3)
                act.activation(hi[u % 4][:], raw[b % 4][:, (u % 2) * UW:(u % 2 + 1) * UW], ACT.Copy).then_inc(s_hi, 1)

            def second_half(stage, k, i=None, per=0, ahead=0):
                f = TMP0[stage] + k
                if f >= 2:
                    prev = emptied(*[(n, m) for n in COLUMN_FORM for m in range(SIZE[n])][f - 2])
                    act.wait_ge(prev[0], prev[1] if i is None else i * per + (emptied(stage, k)[1] - 2))
                act.activation(tmp[f % 2][:], bank_of(stage, k)[:, T:2 * T], ACT.Copy).then_inc(s_tmp, 1)

            def transposed_hi(stage, k, dst):
                act.wait_ge(s_tp, TP0[stage] + k + 1)
                src = bank_of(stage, k)[:].rearrange("p (c t) -> p c t", c=2)
                act.activation(dst, src, ACT.Copy).then_inc(s_th, 1)

            def deviation(n, count):
                act.wait_ge(s_var, n)
                act.activation(rs[:, 0:count], rs[:, 4:4 + count], ACT.Sqrt).then_inc(s_std, 1)

            act.wait_ge(s_par, 16 * 8)
            act.activation(prm[:, 2, :], prm[:, 2, :], ACT.Exp).then_inc(s_prmA, 1)
            act.wait_ge(s_prm, 1)
            act.activation(mag[:], prm[:, 3, :], ACT.Exp).then_inc(s_prmA, 1)
            act.activation(prm[:, 5, :], prm[:, 4, :], ACT.Sin).then_inc(s_prmA, 1)
            act.activation(prm[:, 6, :], prm[:, 4, :], ACT.Sin, scale=0.5).then_inc(s_prmA, 1)
            deviation(1, TT)
            for u in range(4):
                split(u)
            for k in range(8):
                transposed_hi("t_in", k, actT[:, 2 * k:2 * k + 2, 0, :])
            for k in range(4):
                act.wait_ge(s_tp, TP0["t_bb"] + k + 1)
                act.activation(bbT[:, 4 * k:4 * k + 4, :], bank_of("t_bb", k)[:].rearrange("p (c s) -> p c s", c=4),
                               ACT.Copy).then_inc(s_ev["A"], 1)
            for k in range(8):
                u = unit0("ssm_in") + 2 * k
                split(u + 4)
                split(u + 5)
                act.wait_ge(s_mm, u + 2)
                second_half("ssm_in", k)

            for b in range(32):
                u = unit0("gates") + 2 * b
                split(u + 4)
                split(u + 5)
                if b % 4 == 3:
                    act.wait_ge(s_mm, u + 2)
                    for t in range(TT):
                        g = 2 * (b // 4) + t
                        act.activation(gates[:, b // 4, t, :], bank_of("gates", g)[:],
                                       ACT.Sigmoid).then_inc(s_ev["A"], 1)
                if b >= 7 and b % 4 == 3:
                    q = (b - 7) // 4
                    act.wait_ge(s_y, q + 1)
                    act.activation(uT[:, q, :], uT[:, q, :], ACT.Gelu_apprx_tanh).then_inc(s_gel, 1)

            for b in range(9):
                u = unit0("latent") + 2 * b
                split(u + 4)
                split(u + 5)
                if b == 1:
                    act.wait_ge(s_y, 8)
                    act.activation(uT[:, 7, :], uT[:, 7, :], ACT.Gelu_apprx_tanh).then_inc(s_gel, 1)
                    act.wait_ge(s_gel, 8)
                    act.activation(yT[:, :, 0, :], uT[:], ACT.Copy).then_inc(s_yh, 1)
                    act.dma_start(lat_g[:, 0, :], a["q_norm_g"].broadcast_to([P, QL])).then_inc(s_latg, 16)
                    act.dma_start(lat_g[:, 1, :], a["kv_norm_g"].broadcast_to([P, QL])).then_inc(s_latg, 16)
                if b in (3, 7, 8):
                    act.wait_ge(s_mm, u + 2)
                    c = (3, 7, 8).index(b)
                    n = ROPE if c == 2 else QL
                    for t in range(TT):
                        g = 2 * c + t
                        act.activation(lat[:, t, QL * c:QL * c + n], bank_of("latent", g)[:, 0:n],
                                       ACT.Copy).then_inc(s_ev["A"], 1)
            act.wait_ge(*emptied("latent", 5))
            for n in range(4):
                t, c = n // 2, n % 2
                step(act.activation(rope_m[:, 0, 0:QL], lat[:, t, QL * c:QL * (c + 1)], ACT.Square,
                                    accum_out=mv[:, t, c:c + 1]))
            act.sem_inc(s_sq, 1)
            deviation(2, 4)

            for k in range(8):
                u = unit0("glu") + k
                split(u + 4)
                act.wait_ge(s_mm, u + 1)
                second_half("glu", k)
                act.wait_ge(*emptied("glu", k))
                act.activation(glu_s[:, k, :], glu_s[:, k, :], ACT.Sigmoid).then_inc(s_sig, 1)
            act.wait_ge(s_glu, 1)
            act.activation(ssmT[:, :, 0, :], glu_s[:], ACT.Copy).then_inc(s_sh, 1)
            for k in range(16):
                split(unit0("proj_ssm") + k + 4)
            for k in range(4):
                transposed_hi("t_lat", k, latT[:, 2 * k:2 * k + 2, 0, :])

            def heads_columns(stage):
                for m in range(8):
                    u = unit0(stage) + m
                    split(u + 4)
                    act.wait_ge(s_mm, u + 1)
                    for k in (2 * m, 2 * m + 1):
                        second_half(stage, k)

            heads_columns("q_nope")
            for b in range(2):
                u = unit0("q_rope") + 2 * b
                split(u + 4)
                split(u + 5)
                act.wait_ge(s_mm, u + 2)
                for t in range(TT):
                    act.activation(qr_rows[:, t, 512 * b:512 * (b + 1)], bank_of("q_rope", 2 * b + t)[:],
                                   ACT.Copy).then_inc(s_ev["A"], 1)
            for k in range(4):
                act.wait_ge(s_tp, TP0["t_qr"] + k + 1)
                act.activation(qrT[:, 2 * k:2 * k + 2, :], bank_of("t_qr", k)[:].rearrange("p (c t) -> p c t", c=2),
                               ACT.Copy).then_inc(s_ev["A"], 1)
            heads_columns("k_nope")
            for b in range(4):
                u = unit0("value") + 2 * b
                split(u + 4)
                split(u + 5)
                act.wait_ge(s_mm, u + 2)
                for t in range(TT):
                    act.activation(v01[t][:, 512 * b:512 * (b + 1)], bank_of("value", 2 * b + t)[:],
                                   ACT.Copy).then_inc(s_ev["A"], 1)
            for h in range(HEADS):
                act.wait_ge(s_P, h + 1)
                act.activation(sm_p[h % 2][:, 0:P], sm_p[h % 2][:, 0:P], ACT.Exp, bias=smx[h % 2][:, 0:1],
                               accum_out=smx[h % 2][:, 2:3])
                act.activation(sm_p[h % 2][:, P:384], sm_p[h % 2][:, P:384], ACT.Exp, bias=smx[h % 2][:, 1:2],
                               accum_out=smx[h % 2][:, 3:4]).then_inc(s_E, 1)
                act.wait_ge(s_PT, h + 1)
                act.activation(sm_pT[h % 2][:], bank[6 + h % 2][:, 0:384], ACT.Copy).then_inc(s_PTs, 1)
                act.wait_ge(s_PV, h + 1)
                act.activation(actT[:, h, 0, :], bank_of("attn", h)[:, 0:T], ACT.Copy).then_inc(s_pvh, 1)
            act.dma_start(ln_mix_gb[:, 0, :], a["ln_mix_g"].broadcast_to([P, D])).then_inc(s_gb, 16)
            act.dma_start(ln_mix_gb[:, 1, :], a["ln_mix_b"].broadcast_to([P, D])).then_inc(s_gb, 16)
            act.dma_start(keysT[:], a["keysT"]).then_inc(s_keys, 16)
            for k in range(32):
                split(unit0("proj_attn") + k + 4)
            for k in range(8):
                transposed_hi("t_mix", k, actT[:, 2 * k:2 * k + 2, 0, :])
            for k in range(32):
                split(unit0("out") + k + 4)
            deviation(3, TT)
            for k in range(8):
                transposed_hi("t_h", k, actT[:, 2 * k:2 * k + 2, 0, :])
            for k in range(16):
                u = unit0("peer_q") + 2 * k
                split(u + 4)
                split(u + 5)
                act.wait_ge(s_mm, u + 2)
                second_half("peer_q", k)
            for k in range(8):
                act.wait_ge(s_keys, 16 + k + 1)
                act.activation(s_all[:, 2 * k:2 * k + 2, :, :],
                               bank_of("scores", k)[:].rearrange("p (a c n) -> p a c n", a=2, c=2),
                               ACT.Copy).then_inc(s_ev["A"], 1)

            def expert_in(stage, half):
                with act.Fori(0, HALF // 4) as i:
                    for j in range(4):
                        u = unit0(stage) + 2 * j
                        split(u + 4, i, 8)
                        split(u + 5, i, 8)
                        act.wait_ge(s_mm, i * 8 + (u + 2))
                        second_half(stage, j, i, 4)
                        act.wait_ge(s_ev["D"], i * 4 + emptied(stage, j)[1])
                        w = W[:, bass.ds(i * 4 + j, 1), :]
                        act.activation(w, w, ACT.Gelu_apprx_tanh).then_inc(s_gel2, 1)

            def w_hi(half, v, i=None):
                n = v if i is None else i * 4 + v
                act.activation(wh[v % 2][:], W[:, v, :] if i is None else W[:, bass.ds(n, 1), :],
                               ACT.Copy).then_inc(s_whm, 1)

            def expert_out(stage, half):
                act.wait_ge(s_Gev, 32 * (half + 1))
                for v in range(2):
                    w_hi(half, v)

                def steps(v, i=None):
                    u = unit0(stage) + 2 * v
                    for q in range(2):
                        if i is not None or u + q + 4 < NUNIT:
                            split(u + q + 4, i, 8)
                    if i is not None or v + 2 < HALF:
                        act.wait_ge(s_mm, (u + 2) if i is None else i * 8 + (u + 2))
                        w_hi(half, v + 2, i)

                with act.Fori(0, HALF // 4 - 1) as i:
                    for j in range(4):
                        steps(j, i)
                for v in range(HALF - 4, HALF):
                    steps(v)

            expert_in("u0", 0)
            act.wait_ge(s_topped, 1)
            act.activation(picked[:, 0], picked[:, 0], ACT.Exp).then_inc(s_gexp, 1)
            for t in range(TT):
                act.wait_ge(s_hk, t + 1)
                act.activation(hkT[:, :, t * P:(t + 1) * P], bank[4 + t][:, 0:384].rearrange("p (a t) -> p a t", a=3),
                               ACT.Copy).then_inc(s_hkT, 1)
            expert_out("v0", 0)
            expert_in("u1", 1)
            act.wait_ge(s_mm, unit0("v1"))
            act.dma_start(ln_out_gb[:, 0, :], a["ln_ffn_g"].broadcast_to([P, D])).then_inc(s_gb, 16)
            act.dma_start(ln_out_gb[:, 1, :], a["ln_ffn_b"].broadcast_to([P, D])).then_inc(s_gb, 16)
            expert_out("v1", 1)
            deviation(4, TT)

        @block.gpsimd
        def _(pool):
            step = Chain(pool, s_pool)
            pool.iota(iota16[:], [[1, 16]], 0, 0, allow_small_or_imprecise_dtypes=True).then_inc(s_iota, 1)

            pool.wait_ge(s_pw, 1)
            for half in range(2):
                st = slice(16 * half, 16 * half + 16)
                step(pool.memset(table[:, st, 0, 0:1], 1.0))
                step(pool.memset(table[:, st, 1, 0:1], 0.0))
                for k in range(7):
                    n = 1 << k
                    c, s = table[:, st, 0, 0:n], table[:, st, 1, 0:n]
                    pc = pw[:, k, 0, st].unsqueeze(2).broadcast_to([P, 16, n])
                    ps = pw[:, k, 1, st].unsqueeze(2).broadcast_to([P, 16, n])
                    m0, m1 = tab_m[0][:, :, 0:n], tab_m[1][:, :, 0:n]
                    pool.tensor_tensor(m0, c, pc, ALU.mult)
                    step(pool.tensor_tensor(m1, s, ps, ALU.mult))
                    step(pool.tensor_tensor(table[:, st, 0, n:2 * n], m0, m1, ALU.subtract))
                    pool.tensor_tensor(m0, c, ps, ALU.mult)
                    step(pool.tensor_tensor(m1, s, pc, ALU.mult))
                    step(pool.tensor_tensor(table[:, st, 1, n:2 * n], m0, m1, ALU.add))
            pool.sem_inc(s_tab, 1)

            for s in range(STILES):
                pool.wait_ge(s_z, s + 1)
                if s >= 1:
                    pool.wait_ge(s_xr, s)
                if s >= 2:
                    pool.wait_ge(s_cy, s - 1)
                x = xs[s % 2]
                for h in range(2):
                    tt = slice(TH * h, TH * h + TH)
                    c = table[:, s, 0:1, :].broadcast_to([P, 2, TH])
                    n = table[:, s, 1:2, :].broadcast_to([P, 2, TH])
                    pool.tensor_tensor(x[:, :, tt], z[s % 2][:, :, tt], c, ALU.mult)
                    last = pool.tensor_tensor(xs_m[:, :, tt], z[s % 2][:, :, tt], n, ALU.mult)
                step(last)
                pool.tensor_tensor(x[:, 0, :], x[:, 0, :], xs_m[:, 1, :], ALU.subtract)
                pool.tensor_tensor(x[:, 1, :], x[:, 1, :], xs_m[:, 0, :], ALU.add).then_inc(s_xr, 1)

            pool.wait_ge(s_ev["A"], emptied("scores", 7)[1])
            pool.iota(iota[:], [[1, NKEY]], 0, 0, allow_small_or_imprecise_dtypes=True).then_inc(s_iota, 1)

        @block.vector
        def _(dve):
            step = Chain(dve, s_dve)

            def split(u, i=None, per=0):
                n = u if i is None else i * per + u
                dve.wait_ge(s_hi, n + 1)
                dve.tensor_tensor(lo[u % 4][:], raw[(u // 2) % 4][:, (u % 2) * UW:(u % 2 + 1) * UW],
                                  hi[u % 4][:].bitcast(F32), ALU.subtract).then_inc(s_lo, 1)

            def add_halves(stage, k, dst, i=None, per=0):
                f = TMP0[stage] + k
                dve.wait_ge(s_tmp, f + 1 if i is None else i * per + (f + 1))
                dve.tensor_tensor(dst, bank_of(stage, k)[:, 0:T], tmp[f % 2][:], ALU.add).then_inc(s_ev["D"], 1)

            def transposed_lo(stage, k, dst_hi, dst_lo):
                dve.wait_ge(s_th, TH0[stage] + k + 1)
                src = bank_of(stage, k)[:].rearrange("p (c t) -> p c t", c=2)
                dve.tensor_tensor(dst_lo, src, dst_hi.bitcast(F32), ALU.subtract).then_inc(s_ev["D"], 1)

            def inverse_deviation(n, count):
                r, t, v = rs[:, 0:count], mv[:, :, :].rearrange("p a b -> p (a b)")[:, 0:count], rs[:, 4:4 + count]
                dve.wait_ge(s_std, n)
                step(dve.reciprocal(r, r))
                step(dve.tensor_tensor(ini[:, 0:count], r, r, ALU.mult))
                step(dve.tensor_tensor(ini[:, 0:count], ini[:, 0:count], v, ALU.mult))
                step(dve.tensor_scalar(ini[:, 0:count], ini[:, 0:count], -0.5, 1.5, ALU.mult, ALU.add))
                step(dve.tensor_tensor(r, r, ini[:, 0:count], ALU.mult))

            def layer_norm(n, nth, gb):
                for t in range(TT):
                    if nth == 1:
                        dve.wait_ge(s_x, 16 * TT)
                    for c in range(4):
                        last = dve.bn_stats(stats[:, t, c, :], res[:, t, 512 * c:512 * (c + 1)])
                    step(last)
                    step(dve.bn_aggr(mv[:, t, :], stats[:, t].rearrange("p c s -> p (c s)")))
                dve.tensor_scalar(rs[:, 4:4 + TT], mv[:, :, 1], LN_EPS, None, ALU.add).then_inc(s_var, 1)
                inverse_deviation(n, TT)
                dve.wait_ge(s_gb, 32 * nth)
                for t in range(TT):
                    step(dve.tensor_scalar(res[:, t, :], res[:, t, :], mv[:, t, 0:1], rs[:, t:t + 1],
                                           ALU.subtract, ALU.mult))
                    step(dve.tensor_tensor(res[:, t, :], res[:, t, :], gb[:, 0, :], ALU.mult))
                    dve.tensor_tensor(res[:, t, :], res[:, t, :], gb[:, 1, :], ALU.add).then_inc(s_rows, 1)

            (LR, LI, DT, LRDT, PHI, SIN, SINH, K2, DEN, NR, NI, CR, CI, M0, M1, COS) = range(16)

            def pr(n):
                return prm[:, n, :]

            def tt(o, x, y, op):
                step(dve.tensor_tensor(o, x, y, op))

            dve.memset(mask[:], 0.0)
            step(dve.memset(bb_rows[:], 0.0))
            step(dve.memset(c_blk[:], 0.0))
            step(dve.memset(mask[0:64, 64:128], MASKED))
            step(dve.memset(mask[0:64, 320:384], MASKED))
            dve.wait_ge(s_par, 16 * 8)
            dve.wait_ge(s_prmA, 1)
            tt(pr(PHI), pr(LI), pr(DT), ALU.mult)
            MAGIC = 12582912.0
            step(dve.tensor_scalar(pr(K2), pr(PHI), 1.0 / (2 * math.pi), MAGIC, ALU.mult, ALU.add))
            step(dve.tensor_scalar(pr(K2), pr(K2), MAGIC, None, ALU.subtract))
            for part in (6.28125, 0.0019350051879882812, 3.0199157663446332e-07):
                step(dve.scalar_tensor_tensor(pr(PHI), pr(K2), -part, pr(PHI), ALU.mult, ALU.add))
            step(dve.tensor_scalar(pr(PHI), pr(PHI), 3.1415925, -3.1415925, ALU.min, ALU.max))
            dve.tensor_tensor(pr(LRDT), pr(LR), pr(DT), ALU.mult).then_inc(s_prm, 1)
            dve.wait_ge(s_prmA, 4)
            tt(pr(M0), pr(SINH), pr(SINH), ALU.mult)
            step(dve.tensor_scalar(pr(COS), pr(M0), -2.0, 1.0, ALU.mult, ALU.add))
            step(dve.tensor_copy(pw[:, 0, 0, :], pr(COS)))
            step(dve.tensor_copy(pw[:, 0, 1, :], pr(SIN)))
            for k in range(7):
                c, s = pw[:, k, 0, :], pw[:, k, 1, :]
                tt(pr(M0), c, c, ALU.mult)
                tt(pr(M1), s, s, ALU.mult)
                tt(pw[:, k + 1, 0, :], pr(M0), pr(M1), ALU.subtract)
                step(dve.scalar_tensor_tensor(pw[:, k + 1, 1, :], c, 2.0, s, ALU.mult, ALU.mult))
            dve.tensor_copy(wTH[:], pw[:, 7]).then_inc(s_pw, 1)
            tt(pr(NR), mag[:], pr(COS), ALU.mult)
            step(dve.tensor_scalar(pr(NR), pr(NR), -1.0, None, ALU.add))
            tt(pr(NI), mag[:], pr(SIN), ALU.mult)
            tt(pr(M0), pr(LR), pr(LR), ALU.mult)
            tt(pr(M1), pr(LI), pr(LI), ALU.mult)
            tt(pr(DEN), pr(M0), pr(M1), ALU.add)
            step(dve.reciprocal(pr(DEN), pr(DEN)))
            for o, x, y, op in ((CR, NR, NI, ALU.add), (CI, NI, NR, ALU.subtract)):
                tt(pr(M0), pr(x), pr(LR), ALU.mult)
                tt(pr(M1), pr(y), pr(LI), ALU.mult)
                tt(pr(M0), pr(M0), pr(M1), op)
                tt(pr(o), pr(M0), pr(DEN), ALU.mult)
            cr, ci = (pr(x).unsqueeze(2).broadcast_to([P, STILES, 16]) for x in (CR, CI))
            mb = [bb_m[0][:], bb_m[1][:]]
            for ri, (x0, x1, op) in enumerate(((0, 1, ALU.subtract), (1, 0, ALU.add))):
                tt(mb[0], b_in[:, x0], cr, ALU.mult)
                tt(mb[1], b_in[:, x1], ci, ALU.mult)
                for g in range(2):
                    r = slice(64 * g, 64 * g + 64)
                    o = bb_rows[r, ri].rearrange("p q (j h) -> p (q j) h", h=32)[:, :, 16 * g:16 * g + 16]
                    tt(o, mb[0][r], mb[1][r], op)
            for ri, sign in ((0, 1.0), (1, -1.0)):
                for g in range(2):
                    r = slice(64 * g, 64 * g + 64)
                    last = dve.tensor_scalar(c_blk[r, :, ri, 16 * g:16 * g + 16], c_in[r, ri], sign, None, ALU.mult)
            last.then_inc(s_bb, 1)

            layer_norm(1, 1, ln_in_gb)
            for u in range(4):
                split(u)
            for k in range(8):
                c = slice(2 * k, 2 * k + 2)
                transposed_lo("t_in", k, actT[:, c, 0, :], actT[:, c, 1, :])
            for k in range(8):
                u = unit0("ssm_in") + 2 * k
                split(u + 4)
                split(u + 5)
                add_halves("ssm_in", k, uT[:, k, :])

            def scan_tile(s):
                m0, m1, zz = rot_m[0], rot_m[1], z[s % 2]
                if s == 0:
                    dve.wait_ge(s_tab, 1)
                else:
                    dve.wait_ge(s_z, s)
                dve.wait_ge(s_bu, s + 1)
                c = table[:, s, 0:1, :].broadcast_to([P, 2, TH])
                n = table[:, s, 1:2, :].broadcast_to([P, 2, TH])
                bu = bank[4 + s % 2][:].rearrange("p (a t) -> p a t", a=2)
                for h in range(2):
                    x = slice(TH * h, TH * h + TH)
                    dve.tensor_tensor(m0[:, :, x], bu[:, :, x], c, ALU.mult)
                    last = dve.tensor_tensor(m1[:, :, x], bu[:, :, x], n, ALU.mult)
                last.then_inc(s_bufree, 1)
                dve.wait_ge(s_bufree, s + 1)
                dve.tensor_tensor(m0[:, 0, :], m0[:, 0, :], m1[:, 1, :], ALU.add)
                step(dve.tensor_tensor(m0[:, 1, :], m0[:, 1, :], m1[:, 0, :], ALU.subtract))
                if s >= 2:
                    dve.wait_ge(s_xr, s - 1)
                r = mag[:, s:s + 1].broadcast_to([P, TH])
                dve.tensor_tensor_scan(zz[:, 0, 0:TH], r, m0[:, 0, 0:TH], 0.0, ALU.mult, ALU.add)
                step(dve.tensor_tensor_scan(zz[:, 1, 0:TH], r, m0[:, 1, 0:TH], 0.0, ALU.mult, ALU.add))
                zr, zi = zz[:, 0, TH - 1:TH], zz[:, 1, TH - 1:TH]
                wc, ws = wTH[:, 0, s:s + 1], wTH[:, 1, s:s + 1]
                dve.tensor_tensor(ini[:, 0:1], zi, ws, ALU.mult)
                step(dve.tensor_tensor(ini[:, 1:2], zr, ws, ALU.mult))
                dve.scalar_tensor_tensor(ini[:, 2:3], zr, wc, ini[:, 0:1], ALU.mult, ALU.subtract)
                step(dve.scalar_tensor_tensor(ini[:, 3:4], zi, wc, ini[:, 1:2], ALU.mult, ALU.add))
                dve.tensor_tensor_scan(zz[:, 0, TH:], r, m0[:, 0, TH:], ini[:, 2:3], ALU.mult, ALU.add)
                dve.tensor_tensor_scan(zz[:, 1, TH:], r, m0[:, 1, TH:], ini[:, 3:4], ALU.mult,
                                       ALU.add).then_inc(s_z, 1)

            def y_chunk(q):
                dve.wait_ge(s_cy, 4 * q + 4)
                dve.scalar_tensor_tensor(uT[:, q, :], uT[:, q, :], dskip[:, q:q + 1], bank[6 + q % 2][:, 0:T],
                                         ALU.mult, ALU.add).then_inc(s_y, 1)

            dve.wait_ge(s_const, 32)
            for b in range(32):
                u = unit0("gates") + 2 * b
                split(u + 4)
                split(u + 5)
                scan_tile(b)
                if b >= 6 and (b - 6) % 4 == 0:
                    y_chunk((b - 6) // 4)
            for b in range(9):
                u = unit0("latent") + 2 * b
                split(u + 4)
                split(u + 5)
                if b == 1:
                    y_chunk(7)
                if b == 2:
                    dve.wait_ge(s_yh, 1)
                    dve.tensor_tensor(yT[:, :, 1, :], uT[:], yT[:, :, 0, :].bitcast(F32),
                                      ALU.subtract).then_inc(s_yl, 1)
            dve.wait_ge(s_sq, 1)
            dve.tensor_scalar(rs[:, 4:8], mv[:].rearrange("p a b -> p (a b)"), 1.0 / QL, RMS_EPS,
                              ALU.mult, ALU.add).then_inc(s_var, 1)
            inverse_deviation(2, 4)
            dve.wait_ge(s_latg, 32)
            for t in range(TT):
                for c in range(2):
                    x = lat[:, t, QL * c:QL * (c + 1)]
                    n = 2 * t + c
                    dve.scalar_tensor_tensor(x, x, rs[:, n:n + 1], lat_g[:, c, :], ALU.mult, ALU.mult)
            cos, sin = rope[:, :, 0, :], rope[:, :, 1, :]
            x1, x2 = lat[:, :, 2 * QL:2 * QL + 32], lat[:, :, 2 * QL + 32:2 * QL + 64]
            km = [rope_m[:, 1, 64 * n:64 * n + 64].rearrange("p (a b) -> p a b", a=TT) for n in range(4)]
            dve.tensor_tensor(km[0], x1, cos, ALU.mult)
            dve.tensor_tensor(km[1], x2, sin, ALU.mult)
            dve.tensor_tensor(km[2], x1, sin, ALU.mult)
            step(dve.tensor_tensor(km[3], x2, cos, ALU.mult))
            for d in range(2):
                dve.tensor_tensor(kr_rows[:, :, 64 * d:64 * d + 32], km[0], km[1], ALU.subtract)
                last = dve.tensor_tensor(kr_rows[:, :, 64 * d + 32:64 * d + 64], km[2], km[3], ALU.add)
            last.then_inc(s_krot, 1)

            for k in range(8):
                split(unit0("glu") + k + 4)
                add_halves("glu", k, glu_s[:, k, :])
            dve.wait_ge(s_sig, 8)
            dve.tensor_tensor(glu_s[:], glu_s[:], uT[:], ALU.mult).then_inc(s_glu, 1)
            dve.wait_ge(s_sh, 1)
            dve.tensor_tensor(ssmT[:, :, 1, :], glu_s[:], ssmT[:, :, 0, :].bitcast(F32),
                              ALU.subtract).then_inc(s_sl, 1)
            for b in range(8):
                u = unit0("proj_ssm") + 2 * b
                split(u + 4)
                split(u + 5)
                if b % 2:
                    dve.wait_ge(s_mm, u + 2)
                    for t in range(TT):
                        g = gates[:, 4 + b // 2, t, :]
                        dve.tensor_tensor(g, g, bank_of("proj_ssm", b - 1 + t)[:], ALU.mult).then_inc(s_ev["D"], 1)
            for k in range(4):
                c = slice(2 * k, 2 * k + 2)
                transposed_lo("t_lat", k, latT[:, c, 0, :], latT[:, c, 1, :])
            dve.wait_ge(s_tp, TP0["t_lat"] + 5)
            dve.tensor_copy(krT[:], bank_of("t_lat", 4)[:, 0:T]).then_inc(s_ev["D"], 1)

            def heads_columns(stage, dst):
                for m in range(8):
                    split(unit0(stage) + m + 4)
                    for k in (2 * m, 2 * m + 1):
                        add_halves(stage, k, dst[:, k, :])

            heads_columns("q_nope", qT)
            for k in range(4):
                split(unit0("q_rope") + k + 4)
            dve.wait_ge(*emptied("q_rope", 3))
            for t in range(TT):
                rows = qr_rows[:, t, :].rearrange("p (h x) -> p h x", h=HEADS)
                rot = qr_rot[:, t, :].rearrange("p (h x) -> p h x", h=HEADS)
                m = [rope_m[:, n // 2, 512 * (n % 2):512 * (n % 2) + 512].rearrange("p (h x) -> p h x", h=HEADS)
                     for n in range(4)]
                cos = rope[:, t, 0:1, :].broadcast_to([P, HEADS, 32])
                sin = rope[:, t, 1:2, :].broadcast_to([P, HEADS, 32])
                dve.tensor_tensor(m[0], rows[:, :, 0:32], cos, ALU.mult)
                dve.tensor_tensor(m[1], rows[:, :, 32:64], sin, ALU.mult)
                dve.tensor_tensor(m[2], rows[:, :, 0:32], sin, ALU.mult)
                step(dve.tensor_tensor(m[3], rows[:, :, 32:64], cos, ALU.mult))
                dve.tensor_tensor(rot[:, :, 0:32], m[0], m[1], ALU.subtract)
                dve.tensor_tensor(rot[:, :, 32:64], m[2], m[3], ALU.add).then_inc(s_qr, 1)
                dve.wait_ge(s_qr, t + 1)
            heads_columns("k_nope", kT)
            for k in range(8):
                split(unit0("value") + k + 4)

            def mask_scores(h):
                p = sm_p[h % 2]
                dve.wait_ge(s_S, h + 1)
                if h >= 2:
                    dve.wait_ge(s_PT, h - 1)
                step(dve.scalar_tensor_tensor(p[:], bank[4 + h % 2][:, 0:384], SCALE, mask[:], ALU.mult, ALU.add))
                dve.tensor_reduce(smx[h % 2][:, 0:1], p[:, 0:P], AX_X, ALU.max, negate=True)
                dve.tensor_reduce(smx[h % 2][:, 1:2], p[:, P:384], AX_X, ALU.max, negate=True).then_inc(s_P, 1)

            mask_scores(0)
            for h in range(HEADS):
                if h + 1 < HEADS:
                    mask_scores(h + 1)
                p, mx = sm_p[h % 2], smx[h % 2]
                dve.wait_ge(s_E, h + 1)
                step(dve.reciprocal(mx[:, 4:6], mx[:, 2:4]))
                dve.tensor_scalar(p[:, 0:P], p[:, 0:P], mx[:, 4:5], None, ALU.mult)
                dve.tensor_scalar(p[:, P:384], p[:, P:384], mx[:, 5:6], None, ALU.mult).then_inc(s_Pn, 1)
                dve.wait_ge(s_pvh, h + 1)
                dve.tensor_tensor(actT[:, h, 1, :], bank_of("attn", h)[:, 0:T], actT[:, h, 0, :].bitcast(F32),
                                  ALU.subtract).then_inc(s_ev["D"], 1)
            for b in range(16):
                u = unit0("proj_attn") + 2 * b
                split(u + 4)
                split(u + 5)
                if b % 4 == 3:
                    dve.wait_ge(s_mm, u + 2)
                    for t in range(TT):
                        g, gs = gates[:, b // 4, t, :], gates[:, 4 + b // 4, t, :]
                        k = 2 * (b // 4) + t
                        dve.tensor_tensor(g, g, bank_of("proj_attn", k)[:], ALU.mult).then_inc(s_ev["D"], 1)
                        dve.wait_ge(*emptied("proj_attn", k))
                        step(dve.tensor_tensor(gs, gs, g, ALU.add))
            dve.sem_inc(s_picked, 1)
            for k in range(8):
                c = slice(2 * k, 2 * k + 2)
                transposed_lo("t_mix", k, actT[:, c, 0, :], actT[:, c, 1, :])
            for b in range(16):
                u = unit0("out") + 2 * b
                split(u + 4)
                split(u + 5)
                if b % 4 == 3:
                    dve.wait_ge(s_mm, u + 2)
                    for t in range(TT):
                        k = 2 * (b // 4) + t
                        r = res[:, t, 512 * (b // 4):512 * (b // 4 + 1)]
                        dve.scalar_tensor_tensor(r, r, ALPHA, bank_of("out", k)[:], ALU.mult,
                                                 ALU.add).then_inc(s_ev["D"], 1)
            dve.wait_ge(*emptied("out", 7))
            layer_norm(3, 2, ln_mix_gb)
            for k in range(8):
                c = slice(2 * k, 2 * k + 2)
                transposed_lo("t_h", k, actT[:, c, 0, :], actT[:, c, 1, :])
            for k in range(16):
                u = unit0("peer_q") + 2 * k
                split(u + 4)
                split(u + 5)
                add_halves("peer_q", k, pqT[:, k, :])
            dve.wait_ge(*emptied("scores", 7))

            top_steps = [0]

            def top_step(ins):
                top_steps[0] += 1
                ins.then_inc(s_top, 1)
                dve.wait_ge(s_top, top_steps[0])

            def ranks(values, indices, src, spare):
                top_step(dve.max(values[:, 0:8], src))
                dve.max_index(indices[:, 0:8], values[:, 0:8], src)
                top_step(dve.match_replace(spare, values[:, 0:8], src, LOWEST))
                top_step(dve.max(values[:, 8:16], spare))
                top_step(dve.max_index(indices[:, 8:16], values[:, 8:16], spare))

            def pick(c):
                eq = tk_eq[:]
                top_step(dve.tensor_tensor(eq, tk_pf[:, c, :].unsqueeze(2).broadcast_to([P, 16, 16]),
                                       iota16[:].unsqueeze(1).broadcast_to([P, 16, 16]), ALU.is_equal))
                top_step(dve.tensor_tensor(eq, eq, tk_if[:, c, :].unsqueeze(1).broadcast_to([P, 16, 16]), ALU.mult))
                top_step(dve.tensor_reduce(tk_sel[:, c, :], eq, AX_X, ALU.add))

            def top_part(part, i):
                if part == 0:
                    top_step(dve.tensor_copy(tk_s[:], s_all[:, bass.ds(i, 1)].rearrange("p o c n -> p (o c) n")))
                elif part in (1, 2):
                    c = part - 1
                    ranks(tk_v[:, c, :], tk_i[:, c, :], tk_s[:, c, :], tk_s2[:, c, :])
                elif part == 3:
                    top_step(dve.tensor_copy(tk_if[:], tk_i[:]))
                    top_step(dve.tensor_tensor(tk_cand[:], tk_v[:, 0, :].unsqueeze(2).broadcast_to([P, 16, 16]),
                                           tk_v[:, 1, :].unsqueeze(1).broadcast_to([P, 16, 16]), ALU.add))
                elif part == 4:
                    ranks(tk_top, tk_pos, tk_cand[:].rearrange("p a b -> p (a b)"),
                          tk_cand2[:].rearrange("p a b -> p (a b)"))
                elif part == 5:
                    top_step(dve.tensor_scalar(tk_pu[:, 0, :], tk_pos[:], 4, None, ALU.logical_shift_right))
                    top_step(dve.tensor_scalar(tk_pu[:, 1, :], tk_pos[:], 15, None, ALU.bitwise_and))
                    top_step(dve.tensor_copy(tk_pf[:], tk_pu[:]))
                    pick(0)
                elif part == 6:
                    pick(1)
                else:
                    top_step(dve.tensor_scalar(tk_top[:], tk_top[:], tk_top[:, 0:1], None, ALU.subtract))
                    top_step(dve.tensor_copy(picked[:, 0, bass.ds(i, 1), :].rearrange("p o k -> p (o k)"), tk_top[:]))
                    top_step(dve.tensor_copy(picked[:, 1:3, bass.ds(i, 1), :].rearrange("p a o k -> p (a o) k"),
                                         tk_sel[:]))

            def expert_in(stage, top):
                with dve.Fori(0, HALF // 4) as i:
                    for j in range(4):
                        u = unit0(stage) + 2 * j
                        for q in range(2):
                            split(u + q + 4, i, 8)
                            if top:
                                top_part(2 * j + q, i)
                        add_halves(stage, j, W[:, bass.ds(i * 4 + j, 1), :].rearrange("p o t -> p (o t)"), i, 4)
                    if top:
                        dve.sem_clear(s_top)

            def apply_gates(half):
                dve.wait_ge(s_gel2, HALF * (half + 1))
                with dve.Fori(0, 16) as i:
                    for g in range(2):
                        n = 32 * half + g
                        t0 = i * 16 + 8 * g
                        if not (half == 0):
                            dve.wait_ge(s_G, i * 2 + (n - 1))
                        else:
                            dve.wait_ge(s_G, i * 2 + g)
                        dve.tensor_copy(tok[g][:], hkT[:, :, bass.ds(t0, 8)]).then_inc(s_tok, 1)
                        dve.wait_ge(s_tok, i * 2 + (n + 1))
                        for t in range(8):
                            last = dve.tensor_scalar(oneA[g][:, t, :], iota[:], tok[g][:, 1, t:t + 1],
                                                     tok[g][:, 0, t:t + 1], ALU.is_equal, ALU.mult)
                            last = dve.tensor_scalar(oneB[g][:, t, :], iota[:, HALF * half:HALF * half + HALF],
                                                     tok[g][:, 2, t:t + 1], None, ALU.is_equal)
                        last.then_inc(s_one, 1)
                        dve.wait_ge(s_G, i * 2 + (n + 1))
                        w = W[:, :, bass.ds(t0, 8)]
                        dve.tensor_tensor(w, w, bank[4 + g][:].rearrange("p (t n) -> p n t", t=8),
                                          ALU.mult).then_inc(s_Gev, 1)

            def w_lo(half, v, i=None):
                n = v if i is None else i * 4 + v
                dve.wait_ge(s_whm, HALF * half + 1 + v if i is None else i * 4 + (HALF * half + 1 + v))
                w = W[:, v, :] if i is None else W[:, bass.ds(n, 1), :].rearrange("p o t -> p (o t)")
                dve.tensor_tensor(wl[v % 2][:], w, wh[v % 2][:].bitcast(F32), ALU.subtract).then_inc(s_wlm, 1)

            def expert_out(stage, half):
                for v in range(2):
                    w_lo(half, v)

                def steps(v, i=None):
                    u = unit0(stage) + 2 * v
                    for q in range(2):
                        if i is not None or u + q + 4 < NUNIT:
                            split(u + q + 4, i, 8)
                    if i is not None or v + 2 < HALF:
                        w_lo(half, v + 2, i)

                with dve.Fori(0, HALF // 4 - 1) as i:
                    for j in range(4):
                        steps(j, i)
                for v in range(HALF - 4, HALF):
                    steps(v)
                dve.wait_ge(s_mm, unit0(stage) + 2 * HALF)
                for k in range(8):
                    t, c = k // 4, k % 4
                    r = res[:, t, 512 * c:512 * (c + 1)]
                    if half == 0:
                        ins = dve.scalar_tensor_tensor(r, r, ALPHA, bank[k][:], ALU.mult, ALU.add)
                    else:
                        ins = dve.tensor_tensor(r, r, bank[k][:], ALU.add)
                    ins.then_inc(s_ev["D"], 1)
                dve.wait_ge(*emptied(stage, 7))

            expert_in("u0", True)
            dve.sem_inc(s_topped, 1)
            dve.wait_ge(s_gexp, 1)
            step(dve.tensor_reduce(gsum[:, 0, :], picked[:, 0], AX_X, ALU.add))
            step(dve.reciprocal(gsum[:, 1, :], gsum[:, 0, :]))
            dve.tensor_tensor(picked[:, 0], picked[:, 0], gsum[:, 1, :].unsqueeze(2).broadcast_to([P, 16, 16]),
                              ALU.mult).then_inc(s_picked, 1)
            dve.wait_ge(s_hkT, TT)
            dve.wait_ge(s_iota, 2)
            apply_gates(0)
            expert_out("v0", 0)
            expert_in("u1", False)
            apply_gates(1)
            expert_out("v1", 1)
            layer_norm(4, 3, ln_out_gb)

        @block.tensor
        def _(pe):
            def mm_done(ins):
                ins.then_inc(s_mm, 1)

            def wait_unit(u, i=None, per=0):
                pe.wait_ge(s_lo, u + 1 if i is None else i * per + (u + 1))

            def columns(dst, u, first, x, n, kc0, start, stop):
                for k in range(n):
                    w = slice((first + k) * P, (first + k + 1) * P)
                    pe.matmul(dst[:, :], hi[u % 4][:, w], x[:, kc0 + k, :, :].rearrange("p a t -> p (a t)"),
                              start=start and k == 0, stop=False)
                    last = pe.matmul(dst[:, 0:T], lo[u % 4][:, w], x[:, kc0 + k, 0, :], start=False,
                                     stop=stop and k == n - 1)
                return last

            def rows(dsts, u, x, kc0, start, stop, nk=2, width=512, tiles=range(TT)):
                for t in tiles:
                    tok_ = slice(t * P, (t + 1) * P)
                    for k in range(nk):
                        w = slice(k * width, (k + 1) * width)
                        o = dsts[t][:, 0:width]
                        pe.matmul(o, x[:, kc0 + k, 0, tok_], hi[u % 4][:, w], start=start and k == 0, stop=False)
                        pe.matmul(o, x[:, kc0 + k, 0, tok_], lo[u % 4][:, w], start=False, stop=False)
                        last = pe.matmul(o, x[:, kc0 + k, 1, tok_], hi[u % 4][:, w], start=False,
                                         stop=stop and k == nk - 1)
                return last

            def transposes(stage, k, sources):
                wait_bank_free(pe, stage, k)
                b = bank_of(stage, k)
                for n, src in enumerate(sources):
                    last = pe.transpose(b[:, n * P:(n + 1) * P], src, ident[:])
                last.then_inc(s_tp, 1)

            def row_chunk(src, k):
                return [src[:, t, c * P:(c + 1) * P] for c in (2 * k, 2 * k + 1) for t in range(TT)]

            def row_stage(stage, x, kcs, between=None):
                per = kcs // 2
                units = 2 * dict(STAGES)[stage]
                for n in range(units):
                    c, k = n // per, n % per
                    if k == 0:
                        for t in range(TT):
                            wait_bank_free(pe, stage, 2 * c + t)
                    wait_unit(unit0(stage) + n)
                    mm_done(rows([bank_of(stage, 2 * c + t) for t in range(TT)], unit0(stage) + n, x, 2 * k,
                                 k == 0, k == per - 1))
                    if between is not None:
                        between(n)

            pe.wait_ge(s_id, 16)
            pe.wait_ge(s_rows, TT)
            for k in range(8):
                transposes("t_in", k, row_chunk(res, k))
            pe.wait_ge(s_bb, 1)
            for k in range(4):
                transposes("t_bb", k, [bb_rows[:, ri, q, :] for q in (2 * k, 2 * k + 1) for ri in range(2)])
            pe.wait_ge(*emptied("t_in", 7))
            for k in range(8):
                u = unit0("ssm_in") + 2 * k
                wait_bank_free(pe, "ssm_in", k)
                for q in range(2):
                    wait_unit(u + q)
                    mm_done(columns(bank_of("ssm_in", k), u + q, 0, actT, 8, 8 * q, q == 0, q == 1))
            pe.wait_ge(*emptied("ssm_in", 7))
            pe.wait_ge(*emptied("t_bb", 3))

            def bu_tile(s):
                q, r = s // 4, slice(32 * (s % 4), 32 * (s % 4) + 32)
                if s >= 2:
                    pe.wait_ge(s_bufree, s - 1)
                for ri in range(2):
                    last = pe.matmul(bank[4 + s % 2][:, T * ri:T * ri + T], bbT[r, 2 * q + ri, :], uT[r, q, :],
                                     start=True, stop=True)
                last.then_inc(s_bu, 1)

            def cx_tile(s):
                q, r = s // 4, slice(32 * (s % 4), 32 * (s % 4) + 32)
                pe.wait_ge(s_xr, s + 1)
                if s % 4 == 0 and q >= 2:
                    pe.wait_ge(s_y, q - 1)
                for ri in range(2):
                    last = pe.matmul(bank[6 + q % 2][r, 0:T], c_blk[:, s, ri, :], xs[s % 2][:, ri, :],
                                     start=(ri == 0), stop=(ri == 1))
                last.then_inc(s_cy, 1)

            def ssm_beside(n):
                if n % 2:
                    bu_tile(n // 2)
                    if n // 2 >= 2:
                        cx_tile(n // 2 - 2)

            row_stage("gates", actT, KC, ssm_beside)

            for c in range(2):
                for n in range(8):
                    u = unit0("latent") + 8 * c + n
                    if n == 0:
                        for t in range(TT):
                            wait_bank_free(pe, "latent", 2 * c + t)
                    wait_unit(u)
                    mm_done(rows([bank_of("latent", 2 * c + t) for t in range(TT)], u, actT, 2 * n, n == 0, n == 7))
                    if c == 0 and n in (1, 3):
                        cx_tile(STILES - 2 + n // 2)
            for t in range(TT):
                wait_bank_free(pe, "latent", 4 + t)
            u = unit0("latent") + 16
            wait_unit(u)
            mm_done(rows([bank_of("latent", 4 + t) for t in range(TT)], u, actT, 0, True, True, nk=KC, width=ROPE))
            wait_unit(u + 1)
            pe.wait_ge(s_yl, 1)
            for k in range(8):
                if k == 0:
                    wait_bank_free(pe, "glu", k)
                    mm_done(pe.matmul(bank_of("glu", k)[:, 0:T], hi[(u + 1) % 4][:, 0:P], yT[:, 0, 0, :],
                                      start=True, stop=True))
                wait_bank_free(pe, "glu", k)
                wait_unit(unit0("glu") + k)
                mm_done(columns(bank_of("glu", k), unit0("glu") + k, 0, yT, 8, 0, True, True))
            pe.wait_ge(s_sl, 1)
            row_stage("proj_ssm", ssmT, 8)

            pe.wait_ge(s_krot, 1)
            for k in range(4):
                transposes("t_lat", k, row_chunk(lat, k))
            transposes("t_lat", 4, [kr_rows[:, t, :] for t in range(TT)])
            pe.wait_ge(*emptied("t_lat", 3))

            def heads_columns(stage, kc0):
                for m in range(8):
                    wait_unit(unit0(stage) + m)
                    for k in (2 * m, 2 * m + 1):
                        wait_bank_free(pe, stage, k)
                        last = columns(bank_of(stage, k), unit0(stage) + m, 4 * (k % 2), latT, 4, kc0, True, True)
                    mm_done(last)

            heads_columns("q_nope", 0)
            row_stage("q_rope", latT, 4)
            pe.wait_ge(s_qr, TT)
            for k in range(4):
                transposes("t_qr", k, row_chunk(qr_rot, k))
            heads_columns("k_nope", 4)
            lat_kv = latT[:, 4:8]
            for n in range(8):
                b, k = n // 2, n % 2
                if k == 0:
                    for t in range(TT):
                        wait_bank_free(pe, "value", 2 * b + t)
                wait_unit(unit0("value") + n)
                mm_done(rows([bank_of("value", 2 * b + t) for t in range(TT)], unit0("value") + n, latT, 4 + 2 * k,
                             k == 0, k == 1))

            def head_scores(h):
                if h >= 2:
                    pe.wait_ge(s_P, h - 1)
                r = slice(64 * (h % 2), 64 * (h % 2) + 64)
                for t, cols, keys in ((0, slice(0, P), slice(0, P)), (1, slice(P, 384), slice(0, T))):
                    q = slice(t * P, (t + 1) * P)
                    pe.matmul(bank[4 + h % 2][:, cols], qT[:, h, q], kT[:, h, keys], start=True, stop=False)
                    last = pe.matmul(bank[4 + h % 2][:, cols], qrT[r, h // 2, q], krT[r, keys],
                                     start=False, stop=True)
                last.then_inc(s_S, 1)

            pe.wait_ge(*emptied("k_nope", 15))
            pe.wait_ge(*emptied("value", 7))
            head_scores(0)
            for h in range(HEADS):
                if h + 1 < HEADS:
                    head_scores(h + 1)
                pe.wait_ge(s_Pn, h + 1)
                if h >= 2:
                    pe.wait_ge(s_PTs, h - 1)
                for n in range(3):
                    last = pe.transpose(bank[6 + h % 2][:, n * P:(n + 1) * P], sm_p[h % 2][:, n * P:(n + 1) * P],
                                        ident[:])
                last.then_inc(s_PT, 1)
                pe.wait_ge(s_PTs, h + 1)
                wait_bank_free(pe, "attn", h)
                hd = slice(h * P, (h + 1) * P)
                pe.matmul(bank_of("attn", h)[:, 0:T], v0[:, hd], sm_pT[h % 2][:, 0:T], start=True, stop=False)
                pe.matmul(bank_of("attn", h)[:, P:T], v1[:, hd], sm_pT[h % 2][:, T:384], start=False,
                          stop=True).then_inc(s_PV, 1)
            pe.wait_ge(*emptied("attn", 15))
            row_stage("proj_attn", actT, KC)
            pe.wait_ge(s_picked, 1)
            for k in range(8):
                transposes("t_mix", k, [gates[:, 4 + c // 4, t, (c % 4) * P:(c % 4 + 1) * P]
                                        for c in (2 * k, 2 * k + 1) for t in range(TT)])
            pe.wait_ge(*emptied("t_mix", 7))
            row_stage("out", actT, KC)
            pe.wait_ge(s_rows, 2 * TT)
            for k in range(8):
                transposes("t_h", k, row_chunk(res, k))
            pe.wait_ge(*emptied("t_h", 7))
            for k in range(16):
                wait_bank_free(pe, "peer_q", k)
                for q in range(2):
                    u = unit0("peer_q") + 2 * k + q
                    wait_unit(u)
                    mm_done(columns(bank_of("peer_q", k), u, 0, actT, 8, 8 * q, q == 0, q == 1))
            pe.wait_ge(*emptied("peer_q", 15))
            pe.wait_ge(s_keys, 16)
            for k in range(8):
                wait_bank_free(pe, "scores", k)
                for n in range(4):
                    t, hc = k // 4, 4 * (k % 4) + n
                    last = pe.matmul(bank_of("scores", k)[:, n * P:(n + 1) * P], pqT[:, hc, t * P:(t + 1) * P],
                                     keysT[:, hc, :], start=True, stop=True)
                last.then_inc(s_keys, 1)

            def expert_in(stage):
                with pe.Fori(0, HALF // 4) as i:
                    for j in range(4):
                        pe.wait_ge(s_ev["D"], i * 4 + (emptied(stage, j)[1] - 4))
                        for q in range(2):
                            u = unit0(stage) + 2 * j + q
                            wait_unit(u, i, 8)
                            mm_done(columns(bank_of(stage, j), u, 0, actT, 8, 8 * q, q == 0, q == 1))

            def gate_matrix(half):
                with pe.Fori(0, 16) as i:
                    for g in range(2):
                        n = 32 * half + g
                        if half == 0:
                            pe.wait_ge(s_Gev, i * 2 + g)
                        pe.wait_ge(s_one, i * 2 + (n + 1))
                        for t in range(8):
                            last = pe.matmul(bank[4 + g][:, HALF * t:HALF * t + HALF], oneA[g][:, t, :],
                                             oneB[g][:, t, :], start=True, stop=True)
                        last.then_inc(s_G, 1)

            def expert_out(stage, half):
                def steps(v, i=None, first=False, final=False):
                    if i is None:
                        pe.wait_ge(s_wlm, HALF * half + v + 1)
                    else:
                        pe.wait_ge(s_wlm, i * 4 + (HALF * half + v + 1))
                    for q in range(2):
                        u = unit0(stage) + 2 * v + q
                        wait_unit(u, i, 8)
                        for t in range(TT):
                            ts_ = slice(t * P, (t + 1) * P)
                            for w, v_ in ((wh, hi), (wh, lo), (wl, hi)):
                                for c in range(2):
                                    last = pe.matmul(bank[4 * t + 2 * q + c][:], w[v % 2][:, ts_],
                                                     v_[u % 4][:, 512 * c:512 * (c + 1)],
                                                     start=first and w is wh and v_ is hi,
                                                     stop=final and w is wl)
                        mm_done(last)

                pe.wait_ge(*emptied("u0" if half == 0 else "u1", HALF - 1))
                pe.wait_ge(s_Gev, 32 * (half + 1))
                for v in range(4):
                    steps(v, first=(v == 0))
                with pe.Fori(0, HALF // 4 - 2) as i:
                    for j in range(4):
                        steps(4 + j, i)
                for v in range(HALF - 4, HALF):
                    steps(v, final=(v == HALF - 1))

            pe.wait_ge(*emptied("scores", 7))
            expert_in("u0")
            pe.wait_ge(s_picked, 2)
            for t in range(TT):
                for n in range(3):
                    last = pe.transpose(bank[4 + t][:, n * P:(n + 1) * P],
                                        picked[:, n, 8 * t:8 * t + 8, :].rearrange("p h k -> p (h k)"), ident[:])
                last.then_inc(s_hk, 1)
            pe.wait_ge(s_hkT, TT)
            gate_matrix(0)
            expert_out("v0", 0)
            pe.wait_ge(*emptied("v0", 7))
            expert_in("u1")
            gate_matrix(1)
            expert_out("v1", 1)


def row_blocks(w):
    k, n = w.shape
    return w.reshape(k // 512, 4, P, n // 512, 512).transpose(3, 0, 2, 1, 4).reshape(-1, P, SW)


def column_blocks(w):
    k, m = w.shape
    kc = k // P
    return w.reshape(kc, P, m // P, P).transpose(2, 1, 0, 3).reshape(m // P // (16 // kc), 16 // kc, P, kc * P) \
        .transpose(0, 2, 1, 3).reshape(-1, P, SW)


def stream(w):
    w_in, w_uq, w_ukv = w["w_in"][0], w["w_uq"][0], w["w_ukv"][0]
    o_q = SSM
    o_kv, o_kr = o_q + QL, o_q + 2 * QL
    o_g = o_kr + ROPE
    kr = np.zeros((1, P, SW), np.float32)
    kr[0, :, :KC * ROPE] = w_in[:, o_kr:o_g].reshape(KC, P, ROPE).transpose(1, 0, 2).reshape(P, -1)
    uq = w_uq.reshape(QL, HEADS, NOPE + ROPE)
    ukv = w_ukv.reshape(QL, HEADS, 2 * NOPE)
    u = w["peer_u"][0].reshape(NKEY, NKEY, KC, P).transpose(1, 3, 2, 0).reshape(NKEY, P, SW)
    v = w["peer_v"][0].reshape(NKEY, NKEY, D).transpose(1, 0, 2)
    parts = [column_blocks(w_in[:, :SSM]), row_blocks(w_in[:, o_g:]), row_blocks(w_in[:, o_q:o_kr]), kr,
             column_blocks(w["w_glu"][0]), row_blocks(w["w_proj_ssm"][0]),
             column_blocks(uq[:, :, :NOPE].reshape(QL, -1)), row_blocks(uq[:, :, NOPE:].reshape(QL, -1)),
             column_blocks(ukv[:, :, :NOPE].reshape(QL, -1)), row_blocks(ukv[:, :, NOPE:].reshape(QL, -1)),
             row_blocks(w["w_proj_attn"][0]), row_blocks(w["w_out"][0]), column_blocks(w["w_peer_q"][0]),
             u[:HALF], v[:HALF], u[HALF:], v[HALF:]]
    return np.concatenate(parts)


def kernel(**inputs):
    import concourse.bacc as bacc
    from concourse.bass_utils import run_bass_kernel_spmd

    w = {k: np.asarray(v) for k, v in inputs.items()}
    half = ROPE // 2
    ang = np.arange(T, dtype=np.float32)[:, None] * (1.0 / (10000.0 ** (np.arange(half, dtype=np.float32) / half)))
    rope = np.stack([np.cos(ang), np.sin(ang)], 1).astype(np.float32)
    arrays = {
        "x": w["x"].reshape(T, D),
        "stream": stream(w),
        "rope": rope.reshape(TT, P, 2, half).transpose(1, 0, 2, 3),
        "ident": np.eye(P, dtype=np.float32),
        "lam_re": w["ssm_lam_re"][0].reshape(STILES, P).T,
        "lam_im": w["ssm_lam_im"][0].reshape(STILES, P).T,
        "log_dt": w["ssm_log_dt"][0].reshape(STILES, 2).T,
        "b_re": w["ssm_b_re"][0].reshape(STILES, P, 16).transpose(1, 0, 2),
        "b_im": w["ssm_b_im"][0].reshape(STILES, P, 16).transpose(1, 0, 2),
        "c_re": w["ssm_c_re"][0].reshape(STILES, 2, 16, 64).transpose(1, 3, 0, 2).reshape(P, STILES, 16),
        "c_im": w["ssm_c_im"][0].reshape(STILES, 2, 16, 64).transpose(1, 3, 0, 2).reshape(P, STILES, 16),
        "dskip": w["ssm_d"][0].reshape(8, P).T,
        "keysT": w["peer_sub_keys"][0].reshape(16, NKEY, P).transpose(2, 0, 1),
    }
    for name in ("ln_in_g", "ln_in_b", "ln_mix_g", "ln_mix_b", "ln_ffn_g", "ln_ffn_b", "q_norm_g", "kv_norm_g"):
        arrays[name] = w[name].reshape(1, -1)
    arrays = {k: np.ascontiguousarray(v) for k, v in arrays.items()}
    nc = bacc.Bacc("TRN2", target_bir_lowering=False, num_devices=1, dynamic_dma_scratch_size=512)
    a = {k: nc.dram_tensor(f"in_{k}", v.shape, F32, kind="ExternalInput").ap() for k, v in arrays.items()}
    out = nc.dram_tensor("out", (T, D), F32, kind="ExternalOutput").ap()
    build(nc, a, out)
    r = run_bass_kernel_spmd(nc, [{f"in_{k}": v for k, v in arrays.items()}], core_ids=[0])
    return r.results[0]["out"].reshape(w["x"].shape)
```

```python
import math
from contextlib import ExitStack

import numpy as np
import concourse.bass as bass
import concourse.mybir as mybir

F32 = mybir.dt.float32
F32R = mybir.dt.float32r
U32 = mybir.dt.uint32
ACT = mybir.ActivationFunctionType
ALU = mybir.AluOpType
AX_X = mybir.AxisListType.X

P = 128
T = 256
TT = T // P
D = 2048
KC = D // P
SSM = 1024
QL = 512
ROPE = 64
HEADS = 16
NOPE = 128
NKEY = 128
PH = 8
TOPK = 16
NE = NKEY * NKEY
SW = 2048
UW = SW // 2
STILES = 32
TH = 128
LN_EPS, RMS_EPS = 1e-5, 1e-6
ALPHA = 2.0 ** 0.25
SCALE = 1.0 / math.sqrt(NOPE + ROPE)
MASKED = -3.0e38
LOWEST = -3.4028235e38
BASE = 640
GELUS = NKEY // 2
GT = T // GELUS

STAGES = [("ssm_in", 8), ("gates", 32), ("latent", 9), ("glu", 4), ("proj_ssm", 8), ("q_nope", 4), ("q_rope", 2),
          ("k_nope", 4), ("value", 4), ("proj_attn", 16), ("out", 16), ("peer_q", 16),
          ("u", NKEY), ("v", NKEY)]
GROUPS = [("t_in", 8, "D"), ("t_bb", 4, "A"), ("ssm_in", 8, "D"), ("gates", 16, "A"), ("latent", 6, "A"),
          ("glu", 8, "D"), ("proj_ssm", 8, "D"), ("t_lat", 5, "D"), ("q_nope", 16, "D"), ("q_rope", 4, "A"),
          ("t_qr", 4, "A"), ("k_nope", 16, "D"), ("value", 8, "A"), ("attn", 16, "D"), ("proj_attn", 8, "D"),
          ("t_mix", 8, "D"), ("out", 8, "D"), ("t_h", 8, "D"), ("peer_q", 16, "D"), ("scores", 8, "A"),
          ("u", NKEY, "D"), ("v", 8, "D")]
COLUMN_FORM = ["ssm_in", "glu", "q_nope", "k_nope", "peer_q", "u"]
TRANSPOSED = ["t_in", "t_bb", "t_lat", "t_qr", "t_mix", "t_h"]
SPLIT_TRANSPOSED = ["t_in", "t_lat", "t_mix", "t_h"]


def starts(pairs):
    at, out = 0, {}
    for name, n in pairs:
        out[name] = at
        at += n
    return out, at


BLOCK0, NBLOCK = starts(STAGES)
GROUP0, _ = starts([(n, k) for n, k, _ in GROUPS])
SIZE = {n: k for n, k, _ in GROUPS}
EMPTIER = {n: e for n, _, e in GROUPS}
EMPTIED0 = {e: starts([(n, k) for n, k, x in GROUPS if x == e])[0] for e in "DA"}
TMP0, _ = starts([(n, SIZE[n]) for n in COLUMN_FORM])
TP0, _ = starts([(n, SIZE[n]) for n in TRANSPOSED])
TH0, _ = starts([(n, 4 if n == "t_lat" else SIZE[n]) for n in SPLIT_TRANSPOSED])
FLAT = [(n, k) for n, size, _ in GROUPS for k in range(size)]
NUNIT = 2 * NBLOCK


def build(nc, a, out):
    with ExitStack() as ctx:
        def sem(name):
            return ctx.enter_context(nc.semaphore(name))

        def at(name, kib, shape, dt=F32, more=0):
            return nc.alloc_sbuf_tensor_at(name, shape, dt, offset=BASE + int(kib * 1024) + more)

        bank = [ctx.enter_context(nc.psum_tensor(f"bank{i}", [P, 512], F32)) for i in range(8)]

        raw = [at(f"raw{i}", 4 * i, [P, UW]) for i in range(4)]
        hi = [at(f"hi{i}", 16 + 4 * i, [P, UW], F32R) for i in range(4)]
        lo = [at(f"lo{i}", 32 + 4 * i, [P, UW], F32R) for i in range(4)]
        actT = at("actT", 48, [P, KC, 2, T], F32R)
        glu_s = at("glu_s", 48, [P, 8, T])
        qr_rows = at("qr_rows", 48, [P, TT, 1024])
        qr_rot = at("qr_rot", 56, [P, TT, 1024])
        rope_m = at("rope_m", 64, [P, 2, 1024])
        ln_out_gb = at("ln_out_gb", 64, [P, 2, D])
        res_out = at("res_out", 48, [P, TT, D])
        res = at("res", 80, [P, TT, D])
        ln_in_gb = at("ln_in_gb", 112, [P, 2, D])
        gates = at("gates", 112, [P, 8, TT, 512])
        bb_rows = at("bb_rows", 128, [P, 2, 8, P])
        b_in = at("b_in", 136, [P, 2, STILES, 16])
        c_in = at("c_in", 140, [P, 2, STILES, 16])
        W = at("W", 80, [P, NKEY, T])
        table = at("table", 144, [P, STILES, 2, TH])
        yT = at("yT", 144, [P, 8, 2, T], F32R)
        ssmT = at("ssmT", 160, [P, 8, 2, T], F32R)
        qT = at("qT", 144, [P, HEADS, T])
        kT = at("kT", 160, [P, HEADS, T])
        uT = at("uT", 176, [P, 8, T])
        qrT = at("qrT", 176, [P, 8, T])
        keysT = at("keysT", 176, [P, 16, NKEY])
        bbT = at("bbT", 184, [P, 16, P])
        c_blk = at("c_blk", 192, [P, STILES, 2, 32])
        lat = at("lat", 184, [P, TT, 1088])
        latT = at("latT", 192.5, [P, 8, 2, T], F32R)
        kr_rows = at("kr_rows", 215, [P, TT, P])
        lat_g = at("lat_g", 208.5, [P, 2, QL])
        v0 = at("v0", 184, [P, D])
        v1 = at("v1", 208.5, [P, D])
        sm_p = [at(f"sm_p{i}", 193 + 1.5 * i, [P, 384]) for i in range(2)]
        sm_pT = [at(f"sm_pT{i}", 196 + 1.5 * i, [P, 384]) for i in range(2)]
        ln_mix_gb = at("ln_mix_gb", 184, [P, 2, D])
        s_all = at("s_all", 184, [P, 16, 2, NKEY])
        pqT = at("pqT", 200, [P, 16, T])
        rot_m = [at(f"rot_m{i}", 200 + 2 * i, [P, 2, T]) for i in range(2)]
        z = [at(f"z{i}", 204 + 2 * i, [P, 2, T]) for i in range(2)]
        xs = [at(f"xs{i}", 208 + 2 * i, [P, 2, T]) for i in range(2)]
        xs_m = at("xs_m", 212, [P, 2, T])
        prm = at("prm", 200, [P, 32, STILES])
        pw = at("pw", 212, [P, 8, 2, STILES])
        tab_m = [at(f"tab_m{i}", 204 + 4 * i, [P, 16, 64]) for i in range(2)]
        bb_m = [at(f"bb_m{i}", 184 + 2 * i, [P, STILES, 16]) for i in range(2)]
        tk_s = at("tk_s", 200, [P, 2, NKEY])
        tk_s2 = at("tk_s2", 201, [P, 2, NKEY])
        tk_cand = at("tk_cand", 202, [P, 16, 16])
        tk_cand2 = at("tk_cand2", 203, [P, 16, 16])
        tk_v = at("tk_v", 205, [P, 2, 16])
        tk_i = at("tk_i", 205, [P, 2, 16], U32, 128)
        tk_if = at("tk_if", 205, [P, 2, 16], F32, 256)
        tk_top = at("tk_top", 205, [P, 16], F32, 384)
        tk_pos = at("tk_pos", 205, [P, 16], U32, 448)
        tk_pu = at("tk_pu", 205, [P, 2, 16], U32, 512)
        tk_pf = at("tk_pf", 205, [P, 2, 16], F32, 640)
        tk_sel = at("tk_sel", 205, [P, 2, 16], F32, 768)
        tk_gate = at("tk_gate", 205, [P, 16], F32, 896)
        tk_eq = at("tk_eq", 202, [P, 2, 16, 16])
        picked = at("picked", 206, [P, 3, 16, 16])
        gsum = at("gsum", 209, [P, 4, 16])
        oneA = [at(f"oneA{i}", 208 + 2 * i, [P, GT, NKEY]) for i in range(2)]
        oneB = [at(f"oneB{i}", 212 + 2 * i, [P, GT, NKEY]) for i in range(2)]
        wh = [at(f"wh{i}", 208 + i, [P, T], F32R) for i in range(2)]
        wl = [at(f"wl{i}", 210 + i, [P, T], F32R) for i in range(2)]
        C0 = 216.5
        ident = at("ident", C0, [P, P])
        tmp = [at(f"tmp{i}", C0, [P, T], F32, 512 + 1024 * i) for i in range(2)]
        stats = at("stats", C0, [P, TT, 4, 6], F32, 2560)
        mv = at("mv", C0, [P, TT, 2], F32, 2752)
        rs = at("rs", C0, [P, 8], F32, 2784)
        iota16 = at("iota16", C0, [P, 16], F32, 2816)
        ini = at("ini", C0, [P, 8], F32, 2880)
        smx = [at(f"smx{i}", C0, [P, 8], F32, 2912 + 32 * i) for i in range(2)]
        tok = [at(f"tok{i}", C0, [P, 3, GT], F32, 2976 + 64 * i) for i in range(2)]
        tokP = [at(f"tokP{i}", C0, [P, GT], F32, 6720 + 32 * i) for i in range(2)]
        warm = at("warm", C0, [P, 2], F32, 3104)
        rope = at("rope", C0, [P, TT, 2, 32], F32, 3136)
        mag = at("mag", C0, [P, STILES], F32, 3648)
        wTH = at("wTH", C0, [P, 2, STILES], F32, 3776)
        dskip = at("dskip", C0, [P, 8], F32, 4032)
        krT = at("krT", C0, [P, T], F32, 4064)
        mask = at("mask", C0, [P, 384], F32, 5088)
        hkT = at("hkT", C0, [P, 3, T], F32, 3136)
        iota = at("iota", C0, [P, NKEY], F32, 6208)
        v01 = [v0, v1]

        s_raw = [sem(f"raw_landed{i}") for i in range(4)]
        s_hi, s_lo, s_mm = sem("hi_made"), sem("lo_made"), sem("unit_multiplied")
        s_ev = {"D": sem("bank_emptied_by_vector"), "A": sem("bank_emptied_by_scalar")}
        s_tmp = sem("second_half_copied")
        s_tp, s_th = sem("transposed"), sem("transposed_hi_made")
        s_x, s_par, s_gb, s_id = sem("x_landed"), sem("ssm_params_landed"), sem("ln_gb_landed"), sem("ident_landed")
        s_const = sem("constants_landed")
        s_dve, s_act, s_pool = sem("vector_step"), sem("scalar_step"), sem("pool_step")
        s_var, s_std = sem("variance_made"), sem("deviation_made")
        s_rows, s_rowfree = sem("rows_ready"), sem("norm_rows_used")
        s_prm, s_prmA = sem("ssm_prm_by_vector"), sem("ssm_prm_by_scalar")
        s_pw, s_tab, s_bb = sem("powers_ready"), sem("tables_ready"), sem("bb_ready")
        s_bu, s_bufree, s_z, s_xr, s_cy, s_y, s_gel = (sem("bu_made"), sem("bu_used"), sem("z_made"), sem("x_made"),
                                                       sem("cx_made"), sem("y_made"), sem("y_gelu"))
        s_yh, s_yl = sem("y_hi_made"), sem("y_lo_made")
        s_sig, s_glu, s_sh, s_sl = sem("glu_sigmoid"), sem("glu_product"), sem("ssm_hi_made"), sem("ssm_lo_made")
        s_sq, s_latg = sem("squares_made"), sem("latent_gain_landed")
        s_qr, s_krot = sem("q_rotated"), sem("k_rotated")
        s_S, s_P, s_E, s_Pn, s_PT, s_PTs, s_PV, s_pvh = (sem("scores_made"), sem("scores_masked"), sem("exp_made"),
                                                         sem("probs_ready"), sem("probs_transposed"),
                                                         sem("probsT_copied"), sem("head_multiplied"), sem("head_hi_made"))
        s_keys, s_topped, s_gexp, s_picked = sem("keys_landed"), sem("top_ready"), sem("gate_exp"), sem("picked_ready")
        s_hk, s_hkT, s_one, s_G, s_Gev = (sem("hk_transposed"), sem("hkT_copied"), sem("one_hots"),
                                                  sem("gate_matrix"), sem("gates_applied"))
        s_gel2, s_whm, s_wlm, s_tok = sem("expert_gelu"), sem("w_hi_made"), sem("w_lo_made"), sem("tokens_copied")
        s_oneB, s_ones, s_wmul, s_spill, s_back = (sem("second_one_hots"), sem("w_set_to_one"), sem("w_times_gelu"),
                                                   sem("residual_stored"), sem("residual_back"))
        s_warm = sem("table_warmed")
        s_top = sem("top_step")
        s_iota, s_outd = sem("iota_made"), sem("out_written")
        block = ctx.enter_context(nc.Block())

        def emptied(stage, k):
            e = EMPTIER[stage]
            return s_ev[e], EMPTIED0[e][stage] + k + 1

        def bank_of(stage, k):
            return bank[(GROUP0[stage] + k) % 4]

        def wait_bank_free(pe, stage, k):
            n = GROUP0[stage] + k
            if n >= 4:
                pe.wait_ge(*emptied(*FLAT[n - 4]))

        def unit0(stage):
            return 2 * BLOCK0[stage]

        class Chain:

            def __init__(self, eng, s):
                self.eng, self.s, self.n, self.extra = eng, s, 0, 0

            def __call__(self, ins):
                self.n += 1
                ins.then_inc(self.s, 1)
                self.eng.wait_ge(self.s, self.n + self.extra)

            def enter(self, i, per):
                self.at, self.per, self.extra = self.n, per, i * per

            def leave(self, count):
                assert self.n - self.at == self.per, (self.n - self.at, self.per)
                self.n, self.extra = self.at + self.per * count, 0

        @block.sync
        def _(sp):
            x_rows = a["x"].rearrange("(t p) d -> t p d", p=P)
            for t in range(TT):
                sp.dma_start(res[:, t, :], x_rows[t]).then_inc(s_x, 16)

            def load(u, i=None):
                n = u if i is None else i * 4 + u
                if u >= 4:
                    sp.wait_ge(s_lo, n - 3)
                sp.dma_start(raw[u % 4][:], a["stream"][n]).then_inc(s_raw[u % 4], 16)

            for u in range(4):
                load(u)
            loops = (NUNIT - 4) // 4
            with sp.Fori(0, loops) as i:
                for j in range(4):
                    load(4 + j, i)
            for u in range(4 + 4 * loops, NUNIT):
                load(u)
            for t in range(TT):
                sp.wait_ge(s_rows, 2 * TT + t + 1)
                sp.dma_start(out.rearrange("(t p) d -> t p d", p=P)[t], res_out[:, t, :]).then_inc(s_outd, 16)
            sp.wait_ge(s_outd, 16 * TT)

        @block.scalar
        def _(act):
            step = Chain(act, s_act)
            act.dma_start(prm[:, 0, :], a["lam_re"]).then_inc(s_par, 16)
            act.dma_start(prm[:, 1, :], a["lam_im"]).then_inc(s_par, 16)
            for g in range(2):
                act.dma_start(prm[64 * g:64 * g + 64, 2, :],
                               a["log_dt"][g:g + 1, :].broadcast_to([64, STILES])).then_inc(s_par, 16)
            act.dma_start(b_in[:, 0], a["b_re"]).then_inc(s_par, 16)
            act.dma_start(b_in[:, 1], a["b_im"]).then_inc(s_par, 16)
            act.dma_start(c_in[:, 0], a["c_re"]).then_inc(s_par, 16)
            act.dma_start(c_in[:, 1], a["c_im"]).then_inc(s_par, 16)
            act.dma_start(ident[:], a["ident"]).then_inc(s_id, 16)
            act.dma_start(ln_in_gb[:, 0, :], a["ln_in_g"].broadcast_to([P, D])).then_inc(s_gb, 16)
            act.dma_start(ln_in_gb[:, 1, :], a["ln_in_b"].broadcast_to([P, D])).then_inc(s_gb, 16)
            act.dma_start(rope[:], a["rope"]).then_inc(s_const, 16)
            act.dma_start(dskip[:], a["dskip"]).then_inc(s_const, 16)

            def split(u, i=None, per=0):
                n = u if i is None else i * per + u
                landed = 16 * (u // 4 + 1)
                act.wait_ge(s_raw[u % 4], landed if i is None else i * (4 * per) + landed)
                if u >= 4:
                    act.wait_ge(s_mm, n - 3)
                act.activation(hi[u % 4][:], raw[u % 4][:], ACT.Copy).then_inc(s_hi, 1)

            def second_half(stage, k):
                f = TMP0[stage] + k
                if f >= 2:
                    act.wait_ge(*emptied(*[(n, m) for n in COLUMN_FORM for m in range(SIZE[n])][f - 2]))
                act.activation(tmp[f % 2][:], bank_of(stage, k)[:, T:2 * T], ACT.Copy).then_inc(s_tmp, 1)

            def transposed_hi(stage, k, dst):
                act.wait_ge(s_tp, TP0[stage] + k + 1)
                src = bank_of(stage, k)[:].rearrange("p (c t) -> p c t", c=2)
                act.activation(dst, src, ACT.Copy).then_inc(s_th, 1)

            def deviation(n, count):
                act.wait_ge(s_var, n)
                act.activation(rs[:, 0:count], rs[:, 4:4 + count], ACT.Sqrt).then_inc(s_std, 1)

            act.wait_ge(s_par, 16 * 8)
            act.activation(prm[:, 2, :], prm[:, 2, :], ACT.Exp).then_inc(s_prmA, 1)
            act.wait_ge(s_prm, 1)
            act.activation(mag[:], prm[:, 3, :], ACT.Exp).then_inc(s_prmA, 1)
            act.activation(prm[:, 5, :], prm[:, 4, :], ACT.Sin).then_inc(s_prmA, 1)
            act.activation(prm[:, 6, :], prm[:, 4, :], ACT.Sin, scale=0.5).then_inc(s_prmA, 1)
            deviation(1, TT)
            for u in range(4):
                split(u)
            for k in range(8):
                transposed_hi("t_in", k, actT[:, 2 * k:2 * k + 2, 0, :])
            for k in range(4):
                act.wait_ge(s_tp, TP0["t_bb"] + k + 1)
                act.activation(bbT[:, 4 * k:4 * k + 4, :], bank_of("t_bb", k)[:].rearrange("p (c s) -> p c s", c=4),
                               ACT.Copy).then_inc(s_ev["A"], 1)
            for k in range(8):
                u = unit0("ssm_in") + 2 * k
                split(u + 4)
                split(u + 5)
                act.wait_ge(s_mm, u + 2)
                second_half("ssm_in", k)

            for b in range(32):
                u = unit0("gates") + 2 * b
                split(u + 4)
                split(u + 5)
                if b % 4 == 3:
                    act.wait_ge(s_mm, u + 2)
                    for t in range(TT):
                        g = 2 * (b // 4) + t
                        act.activation(gates[:, b // 4, t, :], bank_of("gates", g)[:],
                                       ACT.Sigmoid).then_inc(s_ev["A"], 1)
                if b >= 7 and b % 4 == 3:
                    q = (b - 7) // 4
                    act.wait_ge(s_y, q + 1)
                    act.activation(uT[:, q, :], uT[:, q, :], ACT.Gelu_apprx_tanh).then_inc(s_gel, 1)

            for b in range(9):
                u = unit0("latent") + 2 * b
                split(u + 4)
                split(u + 5)
                if b == 1:
                    act.wait_ge(s_y, 8)
                    act.activation(uT[:, 7, :], uT[:, 7, :], ACT.Gelu_apprx_tanh).then_inc(s_gel, 1)
                    act.wait_ge(s_gel, 8)
                    act.activation(yT[:, :, 0, :], uT[:], ACT.Copy).then_inc(s_yh, 1)
                    act.dma_start(lat_g[:, 0, :], a["q_norm_g"].broadcast_to([P, QL])).then_inc(s_latg, 16)
                    act.dma_start(lat_g[:, 1, :], a["kv_norm_g"].broadcast_to([P, QL])).then_inc(s_latg, 16)
                if b in (3, 7, 8):
                    act.wait_ge(s_mm, u + 2)
                    c = (3, 7, 8).index(b)
                    n = ROPE if c == 2 else QL
                    for t in range(TT):
                        g = 2 * c + t
                        act.activation(lat[:, t, QL * c:QL * c + n], bank_of("latent", g)[:, 0:n],
                                       ACT.Copy).then_inc(s_ev["A"], 1)
            act.wait_ge(*emptied("latent", 5))
            for n in range(4):
                t, c = n // 2, n % 2
                step(act.activation(rope_m[:, 0, 0:QL], lat[:, t, QL * c:QL * (c + 1)], ACT.Square,
                                    accum_out=mv[:, t, c:c + 1]))
            act.sem_inc(s_sq, 1)
            deviation(2, 4)

            for k in range(8):
                u = unit0("glu") + k
                split(u + 4)
                act.wait_ge(s_mm, u + 1)
                second_half("glu", k)
                act.wait_ge(*emptied("glu", k))
                act.activation(glu_s[:, k, :], glu_s[:, k, :], ACT.Sigmoid).then_inc(s_sig, 1)
            act.wait_ge(s_glu, 1)
            act.activation(ssmT[:, :, 0, :], glu_s[:], ACT.Copy).then_inc(s_sh, 1)
            for k in range(16):
                split(unit0("proj_ssm") + k + 4)
            for k in range(4):
                transposed_hi("t_lat", k, latT[:, 2 * k:2 * k + 2, 0, :])

            def heads_columns(stage):
                for m in range(8):
                    u = unit0(stage) + m
                    split(u + 4)
                    act.wait_ge(s_mm, u + 1)
                    for k in (2 * m, 2 * m + 1):
                        second_half(stage, k)

            heads_columns("q_nope")
            for b in range(2):
                u = unit0("q_rope") + 2 * b
                split(u + 4)
                split(u + 5)
                act.wait_ge(s_mm, u + 2)
                for t in range(TT):
                    act.activation(qr_rows[:, t, 512 * b:512 * (b + 1)], bank_of("q_rope", 2 * b + t)[:],
                                   ACT.Copy).then_inc(s_ev["A"], 1)
            for k in range(4):
                act.wait_ge(s_tp, TP0["t_qr"] + k + 1)
                act.activation(qrT[:, 2 * k:2 * k + 2, :], bank_of("t_qr", k)[:].rearrange("p (c t) -> p c t", c=2),
                               ACT.Copy).then_inc(s_ev["A"], 1)
            heads_columns("k_nope")
            for b in range(4):
                u = unit0("value") + 2 * b
                split(u + 4)
                split(u + 5)
                act.wait_ge(s_mm, u + 2)
                for t in range(TT):
                    act.activation(v01[t][:, 512 * b:512 * (b + 1)], bank_of("value", 2 * b + t)[:],
                                   ACT.Copy).then_inc(s_ev["A"], 1)
            for h in range(HEADS):
                act.wait_ge(s_P, h + 1)
                act.activation(sm_p[h % 2][:, 0:P], sm_p[h % 2][:, 0:P], ACT.Exp, bias=smx[h % 2][:, 0:1],
                               accum_out=smx[h % 2][:, 2:3])
                act.activation(sm_p[h % 2][:, P:384], sm_p[h % 2][:, P:384], ACT.Exp, bias=smx[h % 2][:, 1:2],
                               accum_out=smx[h % 2][:, 3:4]).then_inc(s_E, 1)
                act.wait_ge(s_PT, h + 1)
                act.activation(sm_pT[h % 2][:], bank[6 + h % 2][:, 0:384], ACT.Copy).then_inc(s_PTs, 1)
                act.wait_ge(s_PV, h + 1)
                act.activation(actT[:, h, 0, :], bank_of("attn", h)[:, 0:T], ACT.Copy).then_inc(s_pvh, 1)
            act.dma_start(ln_mix_gb[:, 0, :], a["ln_mix_g"].broadcast_to([P, D])).then_inc(s_gb, 16)
            act.dma_start(ln_mix_gb[:, 1, :], a["ln_mix_b"].broadcast_to([P, D])).then_inc(s_gb, 16)
            act.dma_start(keysT[:], a["keysT"]).then_inc(s_keys, 16)
            for k in range(32):
                split(unit0("proj_attn") + k + 4)
            for k in range(8):
                transposed_hi("t_mix", k, actT[:, 2 * k:2 * k + 2, 0, :])
            for k in range(32):
                split(unit0("out") + k + 4)
            deviation(3, TT)
            for k in range(8):
                transposed_hi("t_h", k, actT[:, 2 * k:2 * k + 2, 0, :])
            for k in range(16):
                u = unit0("peer_q") + 2 * k
                split(u + 4)
                split(u + 5)
                act.wait_ge(s_mm, u + 2)
                second_half("peer_q", k)
            for k in range(8):
                act.wait_ge(s_keys, 16 + k + 1)
                act.activation(s_all[:, 2 * k:2 * k + 2, :, :],
                               bank_of("scores", k)[:].rearrange("p (a c n) -> p a c n", a=2, c=2),
                               ACT.Copy).then_inc(s_ev["A"], 1)

            for t in range(TT):
                act.dma_start(a["spill"][t], res[:, t, :]).then_inc(s_spill, 16)
            act.wait_ge(s_spill, 16 * TT)
            act.wait_ge(*emptied("peer_q", 15))

            def warm_gelu():
                act.wait_ge(s_warm, 1)
                act.activation(warm[:, 1:2], warm[:, 0:1], ACT.Gelu_apprx_tanh)

            def expert_in(first, gates_beside):
                with act.Fori(0, GELUS // 4) as i:
                    warm_gelu()
                    for j in range(4):
                        k = first + j
                        u = unit0("u") + 2 * k
                        if gates_beside:
                            act.wait_ge(s_G, i * 4 + (j + 1))
                            act.activation(tok[j % 2][:], hkT[:, :, bass.ds(i * (4 * GT) + GT * j, GT)],
                                           ACT.Copy).then_inc(s_tok, 1)
                        split(u + 4, i, 8)
                        split(u + 5, i, 8)
                        act.wait_ge(s_mm, i * 8 + (u + 2))
                        if gates_beside:
                            act.wait_ge(s_wmul, i * 4 + (j + 1))
                        else:
                            act.wait_ge(s_gel2, i * 4 + (j + 1))
                        act.activation(tmp[j % 2][:], bank_of("u", k)[:, T:2 * T], ACT.Copy).then_inc(s_tmp, 1)
                        act.wait_ge(s_ev["D"], i * 4 + emptied("u", k)[1])
                        dst = tmp[j % 2][:] if gates_beside else W[:, bass.ds(i * 4 + j, 1), :]
                        act.activation(dst, tmp[j % 2][:] if gates_beside else tmp[j % 2][:].unsqueeze(1),
                                       ACT.Gelu_apprx_tanh).then_inc(s_gel2, 1)

            def w_hi(v, i=None):
                act.activation(wh[v % 2][:], W[:, v, :] if i is None else W[:, bass.ds(i * 4 + v, 1), :],
                               ACT.Copy).then_inc(s_whm, 1)

            def expert_out():
                act.wait_ge(s_Gev, 2 + GELUS)
                act.wait_ge(s_wmul, 2 + GELUS)
                for v in range(2):
                    w_hi(v)

                def steps(v, i=None):
                    u = unit0("v") + 2 * v
                    for q in range(2):
                        if i is not None or u + q + 4 < NUNIT:
                            split(u + q + 4, i, 8)
                    if i is not None or v + 2 < NKEY:
                        act.wait_ge(s_mm, (u + 2) if i is None else i * 8 + (u + 2))
                        w_hi(v + 2, i)

                with act.Fori(0, NKEY // 4 - 1) as i:
                    for j in range(4):
                        steps(j, i)
                for v in range(NKEY - 4, NKEY):
                    steps(v)

            act.sem_inc(s_gel2, 2)
            expert_in(0, False)
            act.wait_ge(s_gel2, 2 + GELUS)
            act.wait_ge(s_topped, 1)
            act.activation(picked[:, 0], picked[:, 0], ACT.Exp).then_inc(s_gexp, 1)
            for t in range(TT):
                act.wait_ge(s_hk, t + 1)
                act.activation(hkT[:, :, t * P:(t + 1) * P], bank[4 + t][:, 0:384].rearrange("p (a t) -> p a t", a=3),
                               ACT.Copy).then_inc(s_hkT, 1)
            act.wait_ge(s_hkT, TT)
            expert_in(GELUS, True)
            act.wait_ge(s_mm, unit0("v"))
            for t in range(TT):
                act.dma_start(res_out[:, t, :], a["spill"][t]).then_inc(s_back, 16)
            act.dma_start(ln_out_gb[:, 0, :], a["ln_ffn_g"].broadcast_to([P, D])).then_inc(s_gb, 16)
            act.dma_start(ln_out_gb[:, 1, :], a["ln_ffn_b"].broadcast_to([P, D])).then_inc(s_gb, 16)
            expert_out()
            deviation(4, TT)

        @block.gpsimd
        def _(pool):
            step = Chain(pool, s_pool)
            pool.iota(iota16[:], [[1, 16]], 0, 0, allow_small_or_imprecise_dtypes=True).then_inc(s_iota, 1)

            pool.memset(warm[:], 0.0).then_inc(s_warm, 1)
            pool.wait_ge(s_pw, 1)
            for half in range(2):
                st = slice(16 * half, 16 * half + 16)
                step(pool.memset(table[:, st, 0, 0:1], 1.0))
                step(pool.memset(table[:, st, 1, 0:1], 0.0))
                for k in range(7):
                    n = 1 << k
                    c, s = table[:, st, 0, 0:n], table[:, st, 1, 0:n]
                    pc = pw[:, k, 0, st].unsqueeze(2).broadcast_to([P, 16, n])
                    ps = pw[:, k, 1, st].unsqueeze(2).broadcast_to([P, 16, n])
                    m0, m1 = tab_m[0][:, :, 0:n], tab_m[1][:, :, 0:n]
                    pool.tensor_tensor(m0, c, pc, ALU.mult)
                    step(pool.tensor_tensor(m1, s, ps, ALU.mult))
                    step(pool.tensor_tensor(table[:, st, 0, n:2 * n], m0, m1, ALU.subtract))
                    pool.tensor_tensor(m0, c, ps, ALU.mult)
                    step(pool.tensor_tensor(m1, s, pc, ALU.mult))
                    step(pool.tensor_tensor(table[:, st, 1, n:2 * n], m0, m1, ALU.add))
            pool.sem_inc(s_tab, 1)

            for s in range(STILES):
                pool.wait_ge(s_z, s + 1)
                if s >= 1:
                    pool.wait_ge(s_xr, s)
                if s >= 2:
                    pool.wait_ge(s_cy, s - 1)
                x = xs[s % 2]
                for h in range(2):
                    tt = slice(TH * h, TH * h + TH)
                    c = table[:, s, 0:1, :].broadcast_to([P, 2, TH])
                    n = table[:, s, 1:2, :].broadcast_to([P, 2, TH])
                    pool.tensor_tensor(x[:, :, tt], z[s % 2][:, :, tt], c, ALU.mult)
                    last = pool.tensor_tensor(xs_m[:, :, tt], z[s % 2][:, :, tt], n, ALU.mult)
                step(last)
                pool.tensor_tensor(x[:, 0, :], x[:, 0, :], xs_m[:, 1, :], ALU.subtract)
                pool.tensor_tensor(x[:, 1, :], x[:, 1, :], xs_m[:, 0, :], ALU.add).then_inc(s_xr, 1)

            pool.wait_ge(s_ev["A"], emptied("scores", 7)[1])
            low = 184 - 80
            pool.memset(W[:, GELUS:low, :], 1.0)
            pool.iota(iota[:], [[1, NKEY]], 0, 0, allow_small_or_imprecise_dtypes=True).then_inc(s_iota, 1)
            pool.wait_ge(s_iota, 2)
            pool.wait_ge(s_hkT, TT)
            pool.memset(W[:, low:NKEY, :], 1.0).then_inc(s_ones, 1)
            with pool.Fori(0, GELUS // 4) as i:
                for j in range(4):
                    g = j % 2
                    pool.wait_ge(s_tok, i * 4 + (j + 1))
                    pool.tensor_tensor(tokP[g][:], tok[g][:, 0, :], tok[g][:, 2, :], ALU.mult)
                    for t in range(GT):
                        last = pool.tensor_scalar(oneB[g][:, t, :], iota[:], tok[g][:, 2, t:t + 1],
                                                  tok[g][:, 0, t:t + 1], ALU.is_equal, ALU.mult)
                    last.then_inc(s_oneB, 1)

        @block.vector
        def _(dve):
            step = Chain(dve, s_dve)

            def split(u, i=None, per=0):
                n = u if i is None else i * per + u
                dve.wait_ge(s_hi, n + 1)
                dve.tensor_tensor(lo[u % 4][:], raw[u % 4][:], hi[u % 4][:].bitcast(F32),
                                  ALU.subtract).then_inc(s_lo, 1)

            def add_halves(stage, k, dst, i=None, per=0):
                f = TMP0[stage] + k
                dve.wait_ge(s_tmp, f + 1 if i is None else i * per + (f + 1))
                dve.tensor_tensor(dst, bank_of(stage, k)[:, 0:T], tmp[f % 2][:], ALU.add).then_inc(s_ev["D"], 1)

            def transposed_lo(stage, k, dst_hi, dst_lo):
                dve.wait_ge(s_th, TH0[stage] + k + 1)
                src = bank_of(stage, k)[:].rearrange("p (c t) -> p c t", c=2)
                dve.tensor_tensor(dst_lo, src, dst_hi.bitcast(F32), ALU.subtract).then_inc(s_ev["D"], 1)

            def inverse_deviation(n, count):
                r, t, v = rs[:, 0:count], mv[:, :, :].rearrange("p a b -> p (a b)")[:, 0:count], rs[:, 4:4 + count]
                dve.wait_ge(s_std, n)
                step(dve.reciprocal(r, r))
                step(dve.tensor_tensor(ini[:, 0:count], r, r, ALU.mult))
                step(dve.tensor_tensor(ini[:, 0:count], ini[:, 0:count], v, ALU.mult))
                step(dve.tensor_scalar(ini[:, 0:count], ini[:, 0:count], -0.5, 1.5, ALU.mult, ALU.add))
                step(dve.tensor_tensor(r, r, ini[:, 0:count], ALU.mult))

            def layer_norm(n, nth, gb, x=res):
                for t in range(TT):
                    if nth == 1:
                        dve.wait_ge(s_x, 16 * TT)
                    for c in range(4):
                        last = dve.bn_stats(stats[:, t, c, :], x[:, t, 512 * c:512 * (c + 1)])
                    step(last)
                    step(dve.bn_aggr(mv[:, t, :], stats[:, t].rearrange("p c s -> p (c s)")))
                dve.tensor_scalar(rs[:, 4:4 + TT], mv[:, :, 1], LN_EPS, None, ALU.add).then_inc(s_var, 1)
                inverse_deviation(n, TT)
                dve.wait_ge(s_gb, 32 * nth)
                for t in range(TT):
                    step(dve.tensor_scalar(x[:, t, :], x[:, t, :], mv[:, t, 0:1], rs[:, t:t + 1],
                                           ALU.subtract, ALU.mult))
                    step(dve.tensor_tensor(x[:, t, :], x[:, t, :], gb[:, 0, :], ALU.mult))
                    dve.tensor_tensor(x[:, t, :], x[:, t, :], gb[:, 1, :], ALU.add).then_inc(s_rows, 1)

            (LR, LI, DT, LRDT, PHI, SIN, SINH, K2, DEN, NR, NI, CR, CI, M0, M1, COS) = range(16)

            def pr(n):
                return prm[:, n, :]

            def tt(o, x, y, op):
                step(dve.tensor_tensor(o, x, y, op))

            dve.memset(mask[:], 0.0)
            step(dve.memset(bb_rows[:], 0.0))
            step(dve.memset(c_blk[:], 0.0))
            step(dve.memset(mask[0:64, 64:128], MASKED))
            step(dve.memset(mask[0:64, 320:384], MASKED))
            dve.wait_ge(s_par, 16 * 8)
            dve.wait_ge(s_prmA, 1)
            tt(pr(PHI), pr(LI), pr(DT), ALU.mult)
            MAGIC = 12582912.0
            step(dve.tensor_scalar(pr(K2), pr(PHI), 1.0 / (2 * math.pi), MAGIC, ALU.mult, ALU.add))
            step(dve.tensor_scalar(pr(K2), pr(K2), MAGIC, None, ALU.subtract))
            for part in (6.28125, 0.0019350051879882812, 3.0199157663446332e-07):
                step(dve.scalar_tensor_tensor(pr(PHI), pr(K2), -part, pr(PHI), ALU.mult, ALU.add))
            step(dve.tensor_scalar(pr(PHI), pr(PHI), 3.1415925, -3.1415925, ALU.min, ALU.max))
            dve.tensor_tensor(pr(LRDT), pr(LR), pr(DT), ALU.mult).then_inc(s_prm, 1)
            dve.wait_ge(s_prmA, 4)
            tt(pr(M0), pr(SINH), pr(SINH), ALU.mult)
            step(dve.tensor_scalar(pr(COS), pr(M0), -2.0, 1.0, ALU.mult, ALU.add))
            step(dve.tensor_copy(pw[:, 0, 0, :], pr(COS)))
            step(dve.tensor_copy(pw[:, 0, 1, :], pr(SIN)))
            for k in range(7):
                c, s = pw[:, k, 0, :], pw[:, k, 1, :]
                tt(pr(M0), c, c, ALU.mult)
                tt(pr(M1), s, s, ALU.mult)
                tt(pw[:, k + 1, 0, :], pr(M0), pr(M1), ALU.subtract)
                step(dve.scalar_tensor_tensor(pw[:, k + 1, 1, :], c, 2.0, s, ALU.mult, ALU.mult))
            dve.tensor_copy(wTH[:], pw[:, 7]).then_inc(s_pw, 1)
            tt(pr(NR), mag[:], pr(COS), ALU.mult)
            step(dve.tensor_scalar(pr(NR), pr(NR), -1.0, None, ALU.add))
            tt(pr(NI), mag[:], pr(SIN), ALU.mult)
            tt(pr(M0), pr(LR), pr(LR), ALU.mult)
            tt(pr(M1), pr(LI), pr(LI), ALU.mult)
            tt(pr(DEN), pr(M0), pr(M1), ALU.add)
            step(dve.reciprocal(pr(DEN), pr(DEN)))
            for o, x, y, op in ((CR, NR, NI, ALU.add), (CI, NI, NR, ALU.subtract)):
                tt(pr(M0), pr(x), pr(LR), ALU.mult)
                tt(pr(M1), pr(y), pr(LI), ALU.mult)
                tt(pr(M0), pr(M0), pr(M1), op)
                tt(pr(o), pr(M0), pr(DEN), ALU.mult)
            cr, ci = (pr(x).unsqueeze(2).broadcast_to([P, STILES, 16]) for x in (CR, CI))
            mb = [bb_m[0][:], bb_m[1][:]]
            for ri, (x0, x1, op) in enumerate(((0, 1, ALU.subtract), (1, 0, ALU.add))):
                tt(mb[0], b_in[:, x0], cr, ALU.mult)
                tt(mb[1], b_in[:, x1], ci, ALU.mult)
                for g in range(2):
                    r = slice(64 * g, 64 * g + 64)
                    o = bb_rows[r, ri].rearrange("p q (j h) -> p (q j) h", h=32)[:, :, 16 * g:16 * g + 16]
                    tt(o, mb[0][r], mb[1][r], op)
            for ri, sign in ((0, 1.0), (1, -1.0)):
                for g in range(2):
                    r = slice(64 * g, 64 * g + 64)
                    last = dve.tensor_scalar(c_blk[r, :, ri, 16 * g:16 * g + 16], c_in[r, ri], sign, None, ALU.mult)
            last.then_inc(s_bb, 1)

            layer_norm(1, 1, ln_in_gb)
            for u in range(4):
                split(u)
            for k in range(8):
                c = slice(2 * k, 2 * k + 2)
                transposed_lo("t_in", k, actT[:, c, 0, :], actT[:, c, 1, :])
            for k in range(8):
                u = unit0("ssm_in") + 2 * k
                split(u + 4)
                split(u + 5)
                add_halves("ssm_in", k, uT[:, k, :])

            def scan_tile(s):
                m0, m1, zz = rot_m[0], rot_m[1], z[s % 2]
                if s == 0:
                    dve.wait_ge(s_tab, 1)
                else:
                    dve.wait_ge(s_z, s)
                dve.wait_ge(s_bu, s + 1)
                c = table[:, s, 0:1, :].broadcast_to([P, 2, TH])
                n = table[:, s, 1:2, :].broadcast_to([P, 2, TH])
                bu = bank[4 + s % 2][:].rearrange("p (a t) -> p a t", a=2)
                for h in range(2):
                    x = slice(TH * h, TH * h + TH)
                    dve.tensor_tensor(m0[:, :, x], bu[:, :, x], c, ALU.mult)
                    last = dve.tensor_tensor(m1[:, :, x], bu[:, :, x], n, ALU.mult)
                last.then_inc(s_bufree, 1)
                dve.wait_ge(s_bufree, s + 1)
                dve.tensor_tensor(m0[:, 0, :], m0[:, 0, :], m1[:, 1, :], ALU.add)
                step(dve.tensor_tensor(m0[:, 1, :], m0[:, 1, :], m1[:, 0, :], ALU.subtract))
                if s >= 2:
                    dve.wait_ge(s_xr, s - 1)
                r = mag[:, s:s + 1].broadcast_to([P, TH])
                dve.tensor_tensor_scan(zz[:, 0, 0:TH], r, m0[:, 0, 0:TH], 0.0, ALU.mult, ALU.add)
                step(dve.tensor_tensor_scan(zz[:, 1, 0:TH], r, m0[:, 1, 0:TH], 0.0, ALU.mult, ALU.add))
                zr, zi = zz[:, 0, TH - 1:TH], zz[:, 1, TH - 1:TH]
                wc, ws = wTH[:, 0, s:s + 1], wTH[:, 1, s:s + 1]
                dve.tensor_tensor(ini[:, 0:1], zi, ws, ALU.mult)
                step(dve.tensor_tensor(ini[:, 1:2], zr, ws, ALU.mult))
                dve.scalar_tensor_tensor(ini[:, 2:3], zr, wc, ini[:, 0:1], ALU.mult, ALU.subtract)
                step(dve.scalar_tensor_tensor(ini[:, 3:4], zi, wc, ini[:, 1:2], ALU.mult, ALU.add))
                dve.tensor_tensor_scan(zz[:, 0, TH:], r, m0[:, 0, TH:], ini[:, 2:3], ALU.mult, ALU.add)
                dve.tensor_tensor_scan(zz[:, 1, TH:], r, m0[:, 1, TH:], ini[:, 3:4], ALU.mult,
                                       ALU.add).then_inc(s_z, 1)

            def y_chunk(q):
                dve.wait_ge(s_cy, 4 * q + 4)
                dve.scalar_tensor_tensor(uT[:, q, :], uT[:, q, :], dskip[:, q:q + 1], bank[6 + q % 2][:, 0:T],
                                         ALU.mult, ALU.add).then_inc(s_y, 1)

            dve.wait_ge(s_const, 32)
            for b in range(32):
                u = unit0("gates") + 2 * b
                split(u + 4)
                split(u + 5)
                scan_tile(b)
                if b >= 6 and (b - 6) % 4 == 0:
                    y_chunk((b - 6) // 4)
            for b in range(9):
                u = unit0("latent") + 2 * b
                split(u + 4)
                split(u + 5)
                if b == 1:
                    y_chunk(7)
                if b == 2:
                    dve.wait_ge(s_yh, 1)
                    dve.tensor_tensor(yT[:, :, 1, :], uT[:], yT[:, :, 0, :].bitcast(F32),
                                      ALU.subtract).then_inc(s_yl, 1)
            dve.wait_ge(s_sq, 1)
            dve.tensor_scalar(rs[:, 4:8], mv[:].rearrange("p a b -> p (a b)"), 1.0 / QL, RMS_EPS,
                              ALU.mult, ALU.add).then_inc(s_var, 1)
            inverse_deviation(2, 4)
            dve.wait_ge(s_latg, 32)
            for t in range(TT):
                for c in range(2):
                    x = lat[:, t, QL * c:QL * (c + 1)]
                    n = 2 * t + c
                    dve.scalar_tensor_tensor(x, x, rs[:, n:n + 1], lat_g[:, c, :], ALU.mult, ALU.mult)
            cos, sin = rope[:, :, 0, :], rope[:, :, 1, :]
            x1, x2 = lat[:, :, 2 * QL:2 * QL + 32], lat[:, :, 2 * QL + 32:2 * QL + 64]
            km = [rope_m[:, 1, 64 * n:64 * n + 64].rearrange("p (a b) -> p a b", a=TT) for n in range(4)]
            dve.tensor_tensor(km[0], x1, cos, ALU.mult)
            dve.tensor_tensor(km[1], x2, sin, ALU.mult)
            dve.tensor_tensor(km[2], x1, sin, ALU.mult)
            step(dve.tensor_tensor(km[3], x2, cos, ALU.mult))
            for d in range(2):
                dve.tensor_tensor(kr_rows[:, :, 64 * d:64 * d + 32], km[0], km[1], ALU.subtract)
                last = dve.tensor_tensor(kr_rows[:, :, 64 * d + 32:64 * d + 64], km[2], km[3], ALU.add)
            last.then_inc(s_krot, 1)

            for k in range(8):
                split(unit0("glu") + k + 4)
                add_halves("glu", k, glu_s[:, k, :])
            dve.wait_ge(s_sig, 8)
            dve.tensor_tensor(glu_s[:], glu_s[:], uT[:], ALU.mult).then_inc(s_glu, 1)
            dve.wait_ge(s_sh, 1)
            dve.tensor_tensor(ssmT[:, :, 1, :], glu_s[:], ssmT[:, :, 0, :].bitcast(F32),
                              ALU.subtract).then_inc(s_sl, 1)
            for b in range(8):
                u = unit0("proj_ssm") + 2 * b
                split(u + 4)
                split(u + 5)
                if b % 2:
                    dve.wait_ge(s_mm, u + 2)
                    for t in range(TT):
                        g = gates[:, 4 + b // 2, t, :]
                        dve.tensor_tensor(g, g, bank_of("proj_ssm", b - 1 + t)[:], ALU.mult).then_inc(s_ev["D"], 1)
            for k in range(4):
                c = slice(2 * k, 2 * k + 2)
                transposed_lo("t_lat", k, latT[:, c, 0, :], latT[:, c, 1, :])
            dve.wait_ge(s_tp, TP0["t_lat"] + 5)
            dve.tensor_copy(krT[:], bank_of("t_lat", 4)[:, 0:T]).then_inc(s_ev["D"], 1)

            def heads_columns(stage, dst):
                for m in range(8):
                    split(unit0(stage) + m + 4)
                    for k in (2 * m, 2 * m + 1):
                        add_halves(stage, k, dst[:, k, :])

            heads_columns("q_nope", qT)
            for k in range(4):
                split(unit0("q_rope") + k + 4)
            dve.wait_ge(*emptied("q_rope", 3))
            for t in range(TT):
                rows = qr_rows[:, t, :].rearrange("p (h x) -> p h x", h=HEADS)
                rot = qr_rot[:, t, :].rearrange("p (h x) -> p h x", h=HEADS)
                m = [rope_m[:, n // 2, 512 * (n % 2):512 * (n % 2) + 512].rearrange("p (h x) -> p h x", h=HEADS)
                     for n in range(4)]
                cos = rope[:, t, 0:1, :].broadcast_to([P, HEADS, 32])
                sin = rope[:, t, 1:2, :].broadcast_to([P, HEADS, 32])
                dve.tensor_tensor(m[0], rows[:, :, 0:32], cos, ALU.mult)
                dve.tensor_tensor(m[1], rows[:, :, 32:64], sin, ALU.mult)
                dve.tensor_tensor(m[2], rows[:, :, 0:32], sin, ALU.mult)
                step(dve.tensor_tensor(m[3], rows[:, :, 32:64], cos, ALU.mult))
                dve.tensor_tensor(rot[:, :, 0:32], m[0], m[1], ALU.subtract)
                dve.tensor_tensor(rot[:, :, 32:64], m[2], m[3], ALU.add).then_inc(s_qr, 1)
                dve.wait_ge(s_qr, t + 1)
            heads_columns("k_nope", kT)
            for k in range(8):
                split(unit0("value") + k + 4)

            def mask_scores(h):
                p = sm_p[h % 2]
                dve.wait_ge(s_S, h + 1)
                if h >= 2:
                    dve.wait_ge(s_PT, h - 1)
                step(dve.scalar_tensor_tensor(p[:], bank[4 + h % 2][:, 0:384], SCALE, mask[:], ALU.mult, ALU.add))
                dve.tensor_reduce(smx[h % 2][:, 0:1], p[:, 0:P], AX_X, ALU.max, negate=True)
                dve.tensor_reduce(smx[h % 2][:, 1:2], p[:, P:384], AX_X, ALU.max, negate=True).then_inc(s_P, 1)

            mask_scores(0)
            for h in range(HEADS):
                if h + 1 < HEADS:
                    mask_scores(h + 1)
                p, mx = sm_p[h % 2], smx[h % 2]
                dve.wait_ge(s_E, h + 1)
                step(dve.reciprocal(mx[:, 4:6], mx[:, 2:4]))
                dve.tensor_scalar(p[:, 0:P], p[:, 0:P], mx[:, 4:5], None, ALU.mult)
                dve.tensor_scalar(p[:, P:384], p[:, P:384], mx[:, 5:6], None, ALU.mult).then_inc(s_Pn, 1)
                dve.wait_ge(s_pvh, h + 1)
                dve.tensor_tensor(actT[:, h, 1, :], bank_of("attn", h)[:, 0:T], actT[:, h, 0, :].bitcast(F32),
                                  ALU.subtract).then_inc(s_ev["D"], 1)
            for b in range(16):
                u = unit0("proj_attn") + 2 * b
                split(u + 4)
                split(u + 5)
                if b % 4 == 3:
                    dve.wait_ge(s_mm, u + 2)
                    for t in range(TT):
                        g, gs = gates[:, b // 4, t, :], gates[:, 4 + b // 4, t, :]
                        k = 2 * (b // 4) + t
                        dve.tensor_tensor(g, g, bank_of("proj_attn", k)[:], ALU.mult).then_inc(s_ev["D"], 1)
                        dve.wait_ge(*emptied("proj_attn", k))
                        step(dve.tensor_tensor(gs, gs, g, ALU.add))
            dve.sem_inc(s_picked, 1)
            for k in range(8):
                c = slice(2 * k, 2 * k + 2)
                transposed_lo("t_mix", k, actT[:, c, 0, :], actT[:, c, 1, :])
            for b in range(16):
                u = unit0("out") + 2 * b
                split(u + 4)
                split(u + 5)
                if b % 4 == 3:
                    dve.wait_ge(s_mm, u + 2)
                    for t in range(TT):
                        k = 2 * (b // 4) + t
                        r = res[:, t, 512 * (b // 4):512 * (b // 4 + 1)]
                        dve.scalar_tensor_tensor(r, r, ALPHA, bank_of("out", k)[:], ALU.mult,
                                                 ALU.add).then_inc(s_ev["D"], 1)
            dve.wait_ge(*emptied("out", 7))
            layer_norm(3, 2, ln_mix_gb)
            for k in range(8):
                c = slice(2 * k, 2 * k + 2)
                transposed_lo("t_h", k, actT[:, c, 0, :], actT[:, c, 1, :])
            for k in range(16):
                u = unit0("peer_q") + 2 * k
                split(u + 4)
                split(u + 5)
                add_halves("peer_q", k, pqT[:, k, :])
            dve.wait_ge(*emptied("scores", 7))

            LISTS = ((0, tk_s, tk_s2), (1, tk_s, tk_s2))
            cand, cand2 = (x[:].rearrange("p a b -> p (a b)") for x in (tk_cand, tk_cand2))
            eq = tk_eq[:]

            def top_stage(n, i):
                if n:
                    dve.wait_ge(s_top, n)
                if n == 0:
                    last = dve.tensor_copy(tk_s[:], s_all[:, bass.ds(i, 1)].rearrange("p o c n -> p (o c) n"))
                elif n == 1:
                    for c, x, _ in LISTS:
                        last = dve.max(tk_v[:, c, 0:8], x[:, c, :])
                elif n == 2:
                    for c, x, y in LISTS:
                        dve.max_index(tk_i[:, c, 0:8], tk_v[:, c, 0:8], x[:, c, :])
                        last = dve.match_replace(y[:, c, :], tk_v[:, c, 0:8], x[:, c, :], LOWEST)
                elif n == 3:
                    for c, _, y in LISTS:
                        last = dve.max(tk_v[:, c, 8:16], y[:, c, :])
                elif n == 4:
                    for c, _, y in LISTS:
                        last = dve.max_index(tk_i[:, c, 8:16], tk_v[:, c, 8:16], y[:, c, :])
                elif n == 5:
                    dve.tensor_copy(tk_if[:], tk_i[:])
                    last = dve.tensor_tensor(tk_cand[:], tk_v[:, 0, :].unsqueeze(2).broadcast_to([P, 16, 16]),
                                             tk_v[:, 1, :].unsqueeze(1).broadcast_to([P, 16, 16]), ALU.add)
                elif n == 6:
                    last = dve.max(tk_top[:, 0:8], cand)
                elif n == 7:
                    dve.max_index(tk_pos[:, 0:8], tk_top[:, 0:8], cand)
                    last = dve.match_replace(cand2, tk_top[:, 0:8], cand, LOWEST)
                elif n == 8:
                    last = dve.max(tk_top[:, 8:16], cand2)
                elif n == 9:
                    last = dve.max_index(tk_pos[:, 8:16], tk_top[:, 8:16], cand2)
                elif n == 10:
                    dve.tensor_scalar(tk_pu[:, 0, :], tk_pos[:], 4, None, ALU.logical_shift_right)
                    dve.tensor_scalar(tk_pu[:, 1, :], tk_pos[:], 15, None, ALU.bitwise_and)
                    last = dve.tensor_scalar(tk_gate[:], tk_top[:], tk_top[:, 0:1], None, ALU.subtract)
                elif n == 11:
                    last = dve.tensor_copy(tk_pf[:], tk_pu[:])
                elif n in (12, 13, 14):
                    for c in range(2):
                        e = eq[:, c]
                        if n == 12:
                            last = dve.tensor_tensor(e, tk_pf[:, c, :].unsqueeze(2).broadcast_to([P, 16, 16]),
                                                     iota16[:].unsqueeze(1).broadcast_to([P, 16, 16]), ALU.is_equal)
                        elif n == 13:
                            last = dve.tensor_tensor(e, e, tk_if[:, c, :].unsqueeze(1).broadcast_to([P, 16, 16]),
                                                     ALU.mult)
                        else:
                            last = dve.tensor_reduce(tk_sel[:, c, :], e, AX_X, ALU.add)
                else:
                    dve.tensor_copy(picked[:, 0, bass.ds(i, 1), :].rearrange("p o k -> p (o k)"), tk_gate[:])
                    last = dve.tensor_copy(picked[:, 1:3, bass.ds(i, 1), :].rearrange("p a o k -> p (a o) k"),
                                           tk_sel[:])
                last.then_inc(s_top, 1)

            def add_expert(k, i):
                dve.wait_ge(s_tmp, i * 4 + (TMP0["u"] + k + 1))
                dve.tensor_tensor(tmp[k % 2][:], bank_of("u", k)[:, 0:T], tmp[k % 2][:],
                                  ALU.add).then_inc(s_ev["D"], 1)

            with dve.Fori(0, GELUS // 4) as i:
                for j in range(4):
                    u = unit0("u") + 2 * j
                    split(u + 4, i, 8)
                    top_stage(4 * j, i)
                    split(u + 5, i, 8)
                    top_stage(4 * j + 1, i)
                    add_expert(j, i)
                    top_stage(4 * j + 2, i)
                    top_stage(4 * j + 3, i)
                dve.wait_ge(s_top, 16)
                dve.sem_clear(s_top)
            dve.sem_inc(s_topped, 1)
            dve.wait_ge(s_gexp, 1)
            step(dve.tensor_reduce(gsum[:, 0, :], picked[:, 0], AX_X, ALU.add))
            step(dve.reciprocal(gsum[:, 1, :], gsum[:, 0, :]))
            dve.tensor_tensor(picked[:, 0], picked[:, 0], gsum[:, 1, :].unsqueeze(2).broadcast_to([P, 16, 16]),
                              ALU.mult).then_inc(s_picked, 1)

            dve.wait_ge(s_hkT, TT)
            dve.wait_ge(s_iota, 2)
            dve.wait_ge(s_ones, 1)
            dve.sem_inc(s_wmul, 2)
            dve.sem_inc(s_Gev, 2)
            with dve.Fori(0, GELUS // 4) as i:
                for j in range(4):
                    k, g = GELUS + j, j % 2
                    u = unit0("u") + 2 * k
                    dve.wait_ge(s_tok, i * 4 + (j + 1))
                    for t in range(GT):
                        last = dve.tensor_scalar(oneA[g][:, t, :], iota[:], tok[g][:, 1, t:t + 1], None, ALU.is_equal)
                    last.then_inc(s_one, 1)
                    split(u + 4, i, 8)
                    split(u + 5, i, 8)
                    add_expert(k, i)
                    dve.wait_ge(s_G, i * 4 + (j + 3))
                    if j:
                        dve.wait_ge(s_wmul, i * 4 + (j + 2))
                    else:
                        dve.wait_ge(s_wmul, i * 4 + 2)
                    w = W[:, :, bass.ds(i * (4 * GT) + GT * j, GT)]
                    dve.tensor_tensor(w, w, bank[4 + g][:].rearrange("p (t n) -> p n t", t=GT),
                                      ALU.mult).then_inc(s_Gev, 1)
                    dve.wait_ge(s_gel2, i * 4 + (2 + k + 1))
                    dve.wait_ge(s_Gev, i * 4 + (j + 3))
                    w = W[:, bass.ds(i * 4 + k, 1), :].rearrange("p o t -> p (o t)")
                    dve.tensor_tensor(w, w, tmp[k % 2][:], ALU.mult).then_inc(s_wmul, 1)

            def w_lo(v, i=None):
                dve.wait_ge(s_whm, v + 1 if i is None else i * 4 + (v + 1))
                w = W[:, v, :] if i is None else W[:, bass.ds(i * 4 + v, 1), :].rearrange("p o t -> p (o t)")
                dve.tensor_tensor(wl[v % 2][:], w, wh[v % 2][:].bitcast(F32), ALU.subtract).then_inc(s_wlm, 1)

            for v in range(2):
                w_lo(v)

            def out_steps(v, i=None):
                u = unit0("v") + 2 * v
                for q in range(2):
                    if i is not None or u + q + 4 < NUNIT:
                        split(u + q + 4, i, 8)
                if i is not None or v + 2 < NKEY:
                    w_lo(v + 2, i)

            with dve.Fori(0, NKEY // 4 - 1) as i:
                for j in range(4):
                    out_steps(j, i)
            for v in range(NKEY - 4, NKEY):
                out_steps(v)
            dve.wait_ge(s_back, 16 * TT)
            dve.wait_ge(s_mm, NUNIT)
            for k in range(8):
                t, c = k // 4, k % 4
                r = res_out[:, t, 512 * c:512 * (c + 1)]
                dve.scalar_tensor_tensor(r, r, ALPHA, bank[k][:], ALU.mult, ALU.add).then_inc(s_ev["D"], 1)
            dve.wait_ge(*emptied("v", 7))
            layer_norm(4, 3, ln_out_gb, res_out)

        @block.tensor
        def _(pe):
            def mm_done(ins):
                ins.then_inc(s_mm, 1)

            def wait_unit(u, i=None, per=0):
                pe.wait_ge(s_lo, u + 1 if i is None else i * per + (u + 1))

            def columns(dst, u, first, x, n, kc0, start, stop):
                for k in range(n):
                    w = slice((first + k) * P, (first + k + 1) * P)
                    pe.matmul(dst[:, :], hi[u % 4][:, w], x[:, kc0 + k, :, :].rearrange("p a t -> p (a t)"),
                              start=start and k == 0, stop=False)
                    last = pe.matmul(dst[:, 0:T], lo[u % 4][:, w], x[:, kc0 + k, 0, :], start=False,
                                     stop=stop and k == n - 1)
                return last

            def rows(dsts, u, x, kc0, start, stop, nk=2, width=512, tiles=range(TT)):
                for t in tiles:
                    tok_ = slice(t * P, (t + 1) * P)
                    for k in range(nk):
                        w = slice(k * width, (k + 1) * width)
                        o = dsts[t][:, 0:width]
                        pe.matmul(o, x[:, kc0 + k, 0, tok_], hi[u % 4][:, w], start=start and k == 0, stop=False)
                        pe.matmul(o, x[:, kc0 + k, 0, tok_], lo[u % 4][:, w], start=False, stop=False)
                        last = pe.matmul(o, x[:, kc0 + k, 1, tok_], hi[u % 4][:, w], start=False,
                                         stop=stop and k == nk - 1)
                return last

            def transposes(stage, k, sources):
                wait_bank_free(pe, stage, k)
                b = bank_of(stage, k)
                for n, src in enumerate(sources):
                    last = pe.transpose(b[:, n * P:(n + 1) * P], src, ident[:])
                last.then_inc(s_tp, 1)

            def row_chunk(src, k):
                return [src[:, t, c * P:(c + 1) * P] for c in (2 * k, 2 * k + 1) for t in range(TT)]

            def row_stage(stage, x, kcs, between=None):
                per = kcs // 2
                units = 2 * dict(STAGES)[stage]
                for n in range(units):
                    c, k = n // per, n % per
                    if k == 0:
                        for t in range(TT):
                            wait_bank_free(pe, stage, 2 * c + t)
                    wait_unit(unit0(stage) + n)
                    mm_done(rows([bank_of(stage, 2 * c + t) for t in range(TT)], unit0(stage) + n, x, 2 * k,
                                 k == 0, k == per - 1))
                    if between is not None:
                        between(n)

            pe.wait_ge(s_id, 16)
            pe.wait_ge(s_rows, TT)
            for k in range(8):
                transposes("t_in", k, row_chunk(res, k))
            pe.wait_ge(s_bb, 1)
            for k in range(4):
                transposes("t_bb", k, [bb_rows[:, ri, q, :] for q in (2 * k, 2 * k + 1) for ri in range(2)])
            pe.wait_ge(*emptied("t_in", 7))
            for k in range(8):
                u = unit0("ssm_in") + 2 * k
                wait_bank_free(pe, "ssm_in", k)
                for q in range(2):
                    wait_unit(u + q)
                    mm_done(columns(bank_of("ssm_in", k), u + q, 0, actT, 8, 8 * q, q == 0, q == 1))
            pe.wait_ge(*emptied("ssm_in", 7))
            pe.wait_ge(*emptied("t_bb", 3))

            def bu_tile(s):
                q, r = s // 4, slice(32 * (s % 4), 32 * (s % 4) + 32)
                if s >= 2:
                    pe.wait_ge(s_bufree, s - 1)
                for ri in range(2):
                    last = pe.matmul(bank[4 + s % 2][:, T * ri:T * ri + T], bbT[r, 2 * q + ri, :], uT[r, q, :],
                                     start=True, stop=True)
                last.then_inc(s_bu, 1)

            def cx_tile(s):
                q, r = s // 4, slice(32 * (s % 4), 32 * (s % 4) + 32)
                pe.wait_ge(s_xr, s + 1)
                if s % 4 == 0 and q >= 2:
                    pe.wait_ge(s_y, q - 1)
                for ri in range(2):
                    last = pe.matmul(bank[6 + q % 2][r, 0:T], c_blk[:, s, ri, :], xs[s % 2][:, ri, :],
                                     start=(ri == 0), stop=(ri == 1))
                last.then_inc(s_cy, 1)

            def ssm_beside(n):
                if n % 2:
                    bu_tile(n // 2)
                    if n // 2 >= 2:
                        cx_tile(n // 2 - 2)

            row_stage("gates", actT, KC, ssm_beside)

            for c in range(2):
                for n in range(8):
                    u = unit0("latent") + 8 * c + n
                    if n == 0:
                        for t in range(TT):
                            wait_bank_free(pe, "latent", 2 * c + t)
                    wait_unit(u)
                    mm_done(rows([bank_of("latent", 2 * c + t) for t in range(TT)], u, actT, 2 * n, n == 0, n == 7))
                    if c == 0 and n in (1, 3):
                        cx_tile(STILES - 2 + n // 2)
            for t in range(TT):
                wait_bank_free(pe, "latent", 4 + t)
            u = unit0("latent") + 16
            wait_unit(u)
            mm_done(rows([bank_of("latent", 4 + t) for t in range(TT)], u, actT, 0, True, True, nk=KC, width=ROPE))
            wait_unit(u + 1)
            pe.wait_ge(s_yl, 1)
            for k in range(8):
                if k == 0:
                    wait_bank_free(pe, "glu", k)
                    mm_done(pe.matmul(bank_of("glu", k)[:, 0:T], hi[(u + 1) % 4][:, 0:P], yT[:, 0, 0, :],
                                      start=True, stop=True))
                wait_bank_free(pe, "glu", k)
                wait_unit(unit0("glu") + k)
                mm_done(columns(bank_of("glu", k), unit0("glu") + k, 0, yT, 8, 0, True, True))
            pe.wait_ge(s_sl, 1)
            row_stage("proj_ssm", ssmT, 8)

            pe.wait_ge(s_krot, 1)
            for k in range(4):
                transposes("t_lat", k, row_chunk(lat, k))
            transposes("t_lat", 4, [kr_rows[:, t, :] for t in range(TT)])
            pe.wait_ge(*emptied("t_lat", 3))

            def heads_columns(stage, kc0):
                for m in range(8):
                    wait_unit(unit0(stage) + m)
                    for k in (2 * m, 2 * m + 1):
                        wait_bank_free(pe, stage, k)
                        last = columns(bank_of(stage, k), unit0(stage) + m, 4 * (k % 2), latT, 4, kc0, True, True)
                    mm_done(last)

            heads_columns("q_nope", 0)
            row_stage("q_rope", latT, 4)
            pe.wait_ge(s_qr, TT)
            for k in range(4):
                transposes("t_qr", k, row_chunk(qr_rot, k))
            heads_columns("k_nope", 4)
            lat_kv = latT[:, 4:8]
            for n in range(8):
                b, k = n // 2, n % 2
                if k == 0:
                    for t in range(TT):
                        wait_bank_free(pe, "value", 2 * b + t)
                wait_unit(unit0("value") + n)
                mm_done(rows([bank_of("value", 2 * b + t) for t in range(TT)], unit0("value") + n, latT, 4 + 2 * k,
                             k == 0, k == 1))

            def head_scores(h):
                if h >= 2:
                    pe.wait_ge(s_P, h - 1)
                r = slice(64 * (h % 2), 64 * (h % 2) + 64)
                for t, cols, keys in ((0, slice(0, P), slice(0, P)), (1, slice(P, 384), slice(0, T))):
                    q = slice(t * P, (t + 1) * P)
                    pe.matmul(bank[4 + h % 2][:, cols], qT[:, h, q], kT[:, h, keys], start=True, stop=False)
                    last = pe.matmul(bank[4 + h % 2][:, cols], qrT[r, h // 2, q], krT[r, keys],
                                     start=False, stop=True)
                last.then_inc(s_S, 1)

            pe.wait_ge(*emptied("k_nope", 15))
            pe.wait_ge(*emptied("value", 7))
            head_scores(0)
            for h in range(HEADS):
                if h + 1 < HEADS:
                    head_scores(h + 1)
                pe.wait_ge(s_Pn, h + 1)
                if h >= 2:
                    pe.wait_ge(s_PTs, h - 1)
                for n in range(3):
                    last = pe.transpose(bank[6 + h % 2][:, n * P:(n + 1) * P], sm_p[h % 2][:, n * P:(n + 1) * P],
                                        ident[:])
                last.then_inc(s_PT, 1)
                pe.wait_ge(s_PTs, h + 1)
                wait_bank_free(pe, "attn", h)
                hd = slice(h * P, (h + 1) * P)
                pe.matmul(bank_of("attn", h)[:, 0:T], v0[:, hd], sm_pT[h % 2][:, 0:T], start=True, stop=False)
                pe.matmul(bank_of("attn", h)[:, P:T], v1[:, hd], sm_pT[h % 2][:, T:384], start=False,
                          stop=True).then_inc(s_PV, 1)
            pe.wait_ge(*emptied("attn", 15))
            row_stage("proj_attn", actT, KC)
            pe.wait_ge(s_picked, 1)
            for k in range(8):
                transposes("t_mix", k, [gates[:, 4 + c // 4, t, (c % 4) * P:(c % 4 + 1) * P]
                                        for c in (2 * k, 2 * k + 1) for t in range(TT)])
            pe.wait_ge(*emptied("t_mix", 7))
            row_stage("out", actT, KC)
            pe.wait_ge(s_rows, 2 * TT)
            for k in range(8):
                transposes("t_h", k, row_chunk(res, k))
            pe.wait_ge(*emptied("t_h", 7))
            for k in range(16):
                wait_bank_free(pe, "peer_q", k)
                for q in range(2):
                    u = unit0("peer_q") + 2 * k + q
                    wait_unit(u)
                    mm_done(columns(bank_of("peer_q", k), u, 0, actT, 8, 8 * q, q == 0, q == 1))
            pe.wait_ge(*emptied("peer_q", 15))
            pe.wait_ge(s_keys, 16)
            for k in range(8):
                wait_bank_free(pe, "scores", k)
                for n in range(4):
                    t, hc = k // 4, 4 * (k % 4) + n
                    last = pe.matmul(bank_of("scores", k)[:, n * P:(n + 1) * P], pqT[:, hc, t * P:(t + 1) * P],
                                     keysT[:, hc, :], start=True, stop=True)
                last.then_inc(s_keys, 1)

            def expert_in(first, gates_beside):
                with pe.Fori(0, GELUS // 4) as i:
                    for j in range(4):
                        k = first + j
                        pe.wait_ge(s_ev["D"], i * 4 + (emptied("u", k)[1] - 4))
                        for q in range(2):
                            u = unit0("u") + 2 * k + q
                            wait_unit(u, i, 8)
                            mm_done(columns(bank_of("u", k), u, 0, actT, 8, 8 * q, q == 0, q == 1))
                        if gates_beside:
                            g = j % 2
                            pe.wait_ge(s_Gev, i * 4 + (j + 1))
                            pe.wait_ge(s_one, i * 4 + (j + 1))
                            pe.wait_ge(s_oneB, i * 4 + (j + 1))
                            for t in range(GT):
                                last = pe.matmul(bank[4 + g][:, P * t:P * (t + 1)], oneA[g][:, t, :],
                                                 oneB[g][:, t, :], start=True, stop=True)
                            last.then_inc(s_G, 1)

            pe.wait_ge(*emptied("scores", 7))
            expert_in(0, False)
            pe.wait_ge(s_picked, 2)
            for t in range(TT):
                for n in range(3):
                    last = pe.transpose(bank[4 + t][:, n * P:(n + 1) * P],
                                        picked[:, n, 8 * t:8 * t + 8, :].rearrange("p h k -> p (h k)"), ident[:])
                last.then_inc(s_hk, 1)
            pe.wait_ge(s_hkT, TT)
            pe.sem_inc(s_G, 2)
            expert_in(GELUS, True)

            def out_steps(v, i=None):
                pe.wait_ge(s_wlm, v + 1 if i is None else i * 4 + (v + 1))
                for q in range(2):
                    u = unit0("v") + 2 * v + q
                    wait_unit(u, i, 8)
                    for t in range(TT):
                        ts_ = slice(t * P, (t + 1) * P)
                        for w, v_ in ((wh, hi), (wh, lo), (wl, hi)):
                            for c in range(2):
                                last = pe.matmul(bank[4 * t + 2 * q + c][:], w[v % 2][:, ts_],
                                                 v_[u % 4][:, 512 * c:512 * (c + 1)],
                                                 start=v == 0 and i is None and w is wh and v_ is hi,
                                                 stop=v == NKEY - 1 and w is wl)
                    mm_done(last)

            pe.wait_ge(*emptied("u", NKEY - 1))
            pe.wait_ge(s_Gev, 2 + GELUS)
            for v in range(4):
                out_steps(v)
            with pe.Fori(0, NKEY // 4 - 2) as i:
                for j in range(4):
                    out_steps(4 + j, i)
            for v in range(NKEY - 4, NKEY):
                out_steps(v)


def row_blocks(w):
    k, n = w.shape
    return w.reshape(k // 512, 4, P, n // 512, 512).transpose(3, 0, 2, 1, 4).reshape(-1, P, SW)


def column_blocks(w):
    k, m = w.shape
    kc = k // P
    return w.reshape(kc, P, m // P, P).transpose(2, 1, 0, 3).reshape(m // P // (16 // kc), 16 // kc, P, kc * P) \
        .transpose(0, 2, 1, 3).reshape(-1, P, SW)


def stream(w):
    w_in, w_uq, w_ukv = w["w_in"][0], w["w_uq"][0], w["w_ukv"][0]
    o_q = SSM
    o_kv, o_kr = o_q + QL, o_q + 2 * QL
    o_g = o_kr + ROPE
    kr = np.zeros((1, P, SW), np.float32)
    kr[0, :, :KC * ROPE] = w_in[:, o_kr:o_g].reshape(KC, P, ROPE).transpose(1, 0, 2).reshape(P, -1)
    uq = w_uq.reshape(QL, HEADS, NOPE + ROPE)
    ukv = w_ukv.reshape(QL, HEADS, 2 * NOPE)
    u = w["peer_u"][0].reshape(NKEY, NKEY, KC, P).transpose(1, 3, 2, 0).reshape(NKEY, P, SW)
    v = w["peer_v"][0].reshape(NKEY, NKEY, D).transpose(1, 0, 2)
    parts = [column_blocks(w_in[:, :SSM]), row_blocks(w_in[:, o_g:]), row_blocks(w_in[:, o_q:o_kr]), kr,
             column_blocks(w["w_glu"][0]), row_blocks(w["w_proj_ssm"][0]),
             column_blocks(uq[:, :, :NOPE].reshape(QL, -1)), row_blocks(uq[:, :, NOPE:].reshape(QL, -1)),
             column_blocks(ukv[:, :, :NOPE].reshape(QL, -1)), row_blocks(ukv[:, :, NOPE:].reshape(QL, -1)),
             row_blocks(w["w_proj_attn"][0]), row_blocks(w["w_out"][0]), column_blocks(w["w_peer_q"][0]),
             u, v]
    return np.concatenate(parts).reshape(-1, P, 2, UW).transpose(0, 2, 1, 3).reshape(-1, P, UW)


def kernel(**inputs):
    import concourse.bacc as bacc
    from concourse.bass_utils import run_bass_kernel_spmd

    w = {k: np.asarray(v) for k, v in inputs.items()}
    half = ROPE // 2
    ang = np.arange(T, dtype=np.float32)[:, None] * (1.0 / (10000.0 ** (np.arange(half, dtype=np.float32) / half)))
    rope = np.stack([np.cos(ang), np.sin(ang)], 1).astype(np.float32)
    arrays = {
        "x": w["x"].reshape(T, D),
        "stream": stream(w),
        "rope": rope.reshape(TT, P, 2, half).transpose(1, 0, 2, 3),
        "ident": np.eye(P, dtype=np.float32),
        "lam_re": w["ssm_lam_re"][0].reshape(STILES, P).T,
        "lam_im": w["ssm_lam_im"][0].reshape(STILES, P).T,
        "log_dt": w["ssm_log_dt"][0].reshape(STILES, 2).T,
        "b_re": w["ssm_b_re"][0].reshape(STILES, P, 16).transpose(1, 0, 2),
        "b_im": w["ssm_b_im"][0].reshape(STILES, P, 16).transpose(1, 0, 2),
        "c_re": w["ssm_c_re"][0].reshape(STILES, 2, 16, 64).transpose(1, 3, 0, 2).reshape(P, STILES, 16),
        "c_im": w["ssm_c_im"][0].reshape(STILES, 2, 16, 64).transpose(1, 3, 0, 2).reshape(P, STILES, 16),
        "dskip": w["ssm_d"][0].reshape(8, P).T,
        "keysT": w["peer_sub_keys"][0].reshape(16, NKEY, P).transpose(2, 0, 1),
    }
    for name in ("ln_in_g", "ln_in_b", "ln_mix_g", "ln_mix_b", "ln_ffn_g", "ln_ffn_b", "q_norm_g", "kv_norm_g"):
        arrays[name] = w[name].reshape(1, -1)
    arrays = {k: np.ascontiguousarray(v) for k, v in arrays.items()}
    nc = bacc.Bacc("TRN2", target_bir_lowering=False, num_devices=1, dynamic_dma_scratch_size=512)
    a = {k: nc.dram_tensor(f"in_{k}", v.shape, F32, kind="ExternalInput").ap() for k, v in arrays.items()}
    a["spill"] = nc.dram_tensor("residual_spill", (TT, P, D), F32).ap()
    out = nc.dram_tensor("out", (T, D), F32, kind="ExternalOutput").ap()
    build(nc, a, out)
    r = run_bass_kernel_spmd(nc, [{f"in_{k}": v for k, v in arrays.items()}], core_ids=[0])
    return r.results[0]["out"].reshape(w["x"].shape)
```

```python
import math
from contextlib import ExitStack

import numpy as np
import concourse.bass as bass
import concourse.mybir as mybir

F32 = mybir.dt.float32
F32R = mybir.dt.float32r
U32 = mybir.dt.uint32
ACT = mybir.ActivationFunctionType
ALU = mybir.AluOpType
AX_X = mybir.AxisListType.X

P = 128
T = 256
TT = T // P
D = 2048
KC = D // P
SSM = 1024
QL = 512
ROPE = 64
HEADS = 16
NOPE = 128
NKEY = 128
PH = 8
SW = 2048
UW = SW // 2
STILES = 32
TH = 128
LN_EPS, RMS_EPS = 1e-5, 1e-6
ALPHA = 2.0 ** 0.25
SCALE = 1.0 / math.sqrt(NOPE + ROPE)
MASKED = -3.0e38
LOWEST = -3.4028235e38
BASE = 640
GELUS = NKEY // 2
GT = T // GELUS

STAGES = [("ssm_in", 16), ("latent", 17), ("gates", 64), ("glu", 8), ("q_rope", 4), ("q_nope", 8), ("k_nope", 8),
          ("value", 8), ("proj_ssm", 16), ("proj_attn", 32), ("out", 32), ("peer_q", 32),
          ("u", 2 * NKEY), ("v", 2 * NKEY)]
GROUPS = [("ssm_in", 8, "D"), ("latent", 4, "A"), ("k_rope", 1, "D"), ("t_krows", 1, "A"), ("gates", 16, "A"),
          ("glu", 8, "D"), ("q_rope", 4, "A"), ("q_nope", 16, "D"), ("k_nope", 16, "D"), ("t_kr", 1, "D"), ("t_qr", 4, "A"), ("value", 8, "A"),
          ("proj_ssm", 8, "D"), ("proj_attn", 8, "D"), ("out", 8, "D"), ("peer_q", 16, "D"),
          ("u", NKEY, "D"), ("v", 8, "D")]
SPLIT_TRANSPOSED = [("t_in", 8), ("t_lat", 4), ("t_mix", 8), ("t_h", 8)]
COLUMN_FORM = ["ssm_in", "glu", "q_nope", "k_nope", "peer_q", "u"]


def starts(pairs):
    at, out = 0, {}
    for name, n in pairs:
        out[name] = at
        at += n
    return out, at


UNIT0, NUNIT = starts(STAGES)
GROUP0, _ = starts([(n, k) for n, k, _ in GROUPS])
SIZE = {n: k for n, k, _ in GROUPS}
EMPTIER = {n: e for n, _, e in GROUPS}
EMPTIED0 = {e: starts([(n, k) for n, k, x in GROUPS if x == e])[0] for e in "DA"}
TMP0, _ = starts([(n, SIZE[n]) for n in COLUMN_FORM])
TH0, _ = starts(SPLIT_TRANSPOSED)
FLAT = [(n, k) for n, size, _ in GROUPS for k in range(size)]
TILE_BLOCK = 5


def build(nc, a, out):
    with ExitStack() as ctx:
        def sem(name):
            return ctx.enter_context(nc.semaphore(name))

        def at(name, kib, shape, dt=F32, more=0):
            return nc.alloc_sbuf_tensor_at(name, shape, dt, offset=BASE + int(kib * 1024) + more)

        bank = [ctx.enter_context(nc.psum_tensor(f"bank{i}", [P, 512], F32)) for i in range(8)]

        raw = [at(f"raw{i}", 4 * i, [P, UW]) for i in range(4)]
        hi = [at(f"hi{i}", 16 + 4 * i, [P, UW], F32R) for i in range(4)]
        lo = [at(f"lo{i}", 32 + 4 * i, [P, UW], F32R) for i in range(4)]
        actT = at("actT", 48, [P, KC, 2, T], F32R)
        glu_s = at("glu_s", 48, [P, 8, T])
        qr_rows = at("qr_rows", 72, [P, TT, 1024])
        qr_rot = at("qr_rot", 56, [P, TT, 1024])
        rope_m = at("rope_m", 64, [P, 2, 1024])
        ln_out_gb = at("ln_out_gb", 64, [P, 2, D])
        res_out = at("res_out", 48, [P, TT, D])
        res = at("res", 80, [P, TT, D])
        ln_in_gb = at("ln_in_gb", 112, [P, 2, D])
        gates = at("gates", 112, [P, 8, TT, 512])
        bb_rows = at("bb_rows", 128, [P, 2, 8, P])
        b_in = at("b_in", 136, [P, 2, STILES, 16])
        c_in = at("c_in", 140, [P, 2, STILES, 16])
        W = at("W", 80, [P, NKEY, T])
        table = at("table", 144, [P, STILES, 2, TH])
        yT = at("yT", 144, [P, 8, 2, T], F32R)
        ssmT = at("ssmT", 96, [P, 8, 2, T], F32R)
        qT = at("qT", 144, [P, HEADS, T])
        kT = at("kT", 160, [P, HEADS, T])
        uT = at("uT", 176, [P, 8, T])
        qrT = at("qrT", 176, [P, 8, T])
        keysT = at("keysT", 176, [P, 16, NKEY])
        bbT = at("bbT", 184, [P, 16, P])
        c_blk = at("c_blk", 192, [P, STILES, 2, 32])
        mixT = at("mixT", 144, [P, KC, 2, T], F32R)
        lat = at("lat", 96, [P, TT, 1088])
        latT = at("latT", 192.5, [P, 8, 2, T], F32R)
        kr_rows = at("kr_rows", 214, [P, TT, P])
        lat_g = at("lat_g", 104.5, [P, 2, QL])
        lat_m = at("lat_m", 109.5, [P, QL])
        kr_sum = at("kr_sum", 108.5, [ROPE, T])
        v0 = at("v0", 184, [P, D])
        v1 = at("v1", 208.5, [P, D])
        sm_p = [at(f"sm_p{i}", 193 + 1.5 * i, [P, 384]) for i in range(2)]
        sm_pT = [at(f"sm_pT{i}", 196 + 1.5 * i, [P, 384]) for i in range(2)]
        ln_mix_gb = at("ln_mix_gb", 184, [P, 2, D])
        s_all = at("s_all", 184, [P, 16, 2, NKEY])
        pqT = at("pqT", 200, [P, 16, T])
        rot_m = [at(f"rot_m{i}", 200 + 2 * i, [P, 2, T]) for i in range(2)]
        z = [at(f"z{i}", 204 + 2 * i, [P, 2, T]) for i in range(2)]
        xs = [at(f"xs{i}", 208 + 2 * i, [P, 2, T]) for i in range(2)]
        xs_m = at("xs_m", 212, [P, 2, T])
        prm = at("prm", 200, [P, 32, STILES])
        pw = at("pw", 214, [P, 8, 2, STILES])
        tab_m = [at(f"tab_m{i}", 120 + 4 * i, [P, 16, 64]) for i in range(2)]
        bb_m = [at(f"bb_m{i}", 184 + 2 * i, [P, STILES, 16]) for i in range(2)]
        tk_s = at("tk_s", 208, [P, 2, NKEY])
        tk_s2 = at("tk_s2", 209, [P, 2, NKEY])
        tk_cand = at("tk_cand", 210, [P, 16, 16])
        tk_cand2 = at("tk_cand2", 211, [P, 16, 16])
        tk_v = at("tk_v", 212, [P, 2, 16])
        tk_i = at("tk_i", 212, [P, 2, 16], U32, 128)
        tk_if = at("tk_if", 212, [P, 2, 16], F32, 256)
        tk_top = at("tk_top", 212, [P, 16], F32, 384)
        tk_pos = at("tk_pos", 212, [P, 16], U32, 448)
        tk_pu = at("tk_pu", 212, [P, 2, 16], U32, 512)
        tk_pf = at("tk_pf", 212, [P, 2, 16], F32, 640)
        tk_sel = at("tk_sel", 212, [P, 2, 16], F32, 768)
        tk_gate = at("tk_gate", 212, [P, 16], F32, 896)
        tk_eq = at("tk_eq", 210, [P, 2, 16, 16])
        picked = at("picked", 213, [P, 3, 16, 16])
        gsum = at("gsum", 216, [P, 4, 16])
        oneA = [at(f"oneA{i}", 208 + 2 * i, [P, GT, NKEY]) for i in range(2)]
        oneB = [at(f"oneB{i}", 212 + 2 * i, [P, GT, NKEY]) for i in range(2)]
        wh = [at(f"wh{i}", 208 + i, [P, T], F32R) for i in range(2)]
        wl = [at(f"wl{i}", 210 + i, [P, T], F32R) for i in range(2)]
        C0 = 216.5
        ident = at("ident", C0, [P, P])
        tmp = [at(f"tmp{i}", C0, [P, T], F32, 512 + 1024 * i) for i in range(2)]
        stats = at("stats", C0, [P, TT, 4, 6], F32, 2560)
        mv = at("mv", C0, [P, TT, 2], F32, 2752)
        rs = at("rs", C0, [P, 8], F32, 2784)
        iota16 = at("iota16", C0, [P, 16], F32, 2816)
        ini = at("ini", C0, [P, 8], F32, 2880)
        smx = [at(f"smx{i}", C0, [P, 8], F32, 2912 + 32 * i) for i in range(2)]
        tok = [at(f"tok{i}", C0, [P, 3, GT], F32, 2976 + 64 * i) for i in range(2)]
        tok_m = [at(f"tok_m{i}", C0, [P, GT], F32, 6720 + 32 * i) for i in range(2)]
        warm = at("warm", C0, [P, 2], F32, 3104)
        rope = at("rope", C0, [P, TT, 2, 32], F32, 3136)
        mag = at("mag", C0, [P, STILES], F32, 3648)
        wTH = at("wTH", C0, [P, 2, STILES], F32, 3776)
        dskip = at("dskip", C0, [P, 8], F32, 4032)
        krT = at("krT", C0, [P, T], F32, 4064)
        mask = at("mask", C0, [P, 384], F32, 5088)
        hkT = at("hkT", C0, [P, 3, T], F32, 3136)
        iota = at("iota", C0, [P, NKEY], F32, 6208)
        v01 = [v0, v1]

        s_raw = [sem(f"raw_landed{i}") for i in range(4)]
        s_hi, s_lo, s_mm = sem("hi_made"), sem("lo_made"), sem("unit_multiplied")
        s_ev = {"D": sem("bank_emptied_by_vector"), "A": sem("bank_emptied_by_scalar")}
        s_tmp = sem("second_half_copied")
        s_tp, s_th, s_tl = sem("transposed"), sem("transposed_hi_made"), sem("transposed_lo_made")
        s_sc, s_scored = sem("key_scores_made"), sem("key_scores_copied")
        s_krh, s_krt, s_gsig = sem("k_rope_half_copied"), sem("k_rope_rows_made"), sem("gates_sigmoid")
        s_nmr, s_xn, s_rows1, s_lastc = (sem("mean_over_deviation"), sem("rows_normalised"), sem("second_tile_ready"),
                                         sem("last_chunk_ready"))
        s_tr, s_mix = sem("rotary_part_transposed"), sem("mixed_chunks")
        s_x = [sem(f"x_landed{t}") for t in range(TT)]
        s_par, s_gb, s_id = sem("ssm_params_landed"), sem("ln_gb_landed"), sem("ident_landed")
        s_const = sem("constants_landed")
        s_dve, s_act, s_pool = sem("vector_step"), sem("scalar_step"), sem("pool_step")
        s_var, s_std = sem("variance_made"), sem("deviation_made")
        s_rows = sem("rows_ready")
        s_prm, s_prmA = sem("ssm_prm_by_vector"), sem("ssm_prm_by_scalar")
        s_pw, s_tab, s_bb = sem("powers_ready"), sem("tables_ready"), sem("bb_ready")
        s_bu, s_bufree, s_z, s_xr, s_cy, s_y, s_gel = (sem("bu_made"), sem("bu_used"), sem("z_made"), sem("x_made"),
                                                       sem("cx_made"), sem("y_made"), sem("y_gelu"))
        s_yh, s_yl = sem("y_hi_made"), sem("y_lo_made")
        s_sig, s_glu, s_sh, s_sl = sem("glu_sigmoid"), sem("glu_product"), sem("ssm_hi_made"), sem("ssm_lo_made")
        s_sq, s_latg = sem("squares_made"), sem("latent_gain_landed")
        s_qr, s_krot = sem("q_rotated"), sem("k_rotated")
        s_S, s_P, s_E, s_Pn, s_PT, s_PTs, s_PV, s_pvh = (sem("scores_made"), sem("scores_masked"), sem("exp_made"),
                                                         sem("probs_ready"), sem("probs_transposed"),
                                                         sem("probsT_copied"), sem("head_multiplied"), sem("head_hi_made"))
        s_pvl, s_bbT, s_bbTc = sem("head_lo_made"), sem("bb_transposed"), sem("bbT_copied")
        s_keys, s_topped, s_gexp, s_picked = sem("keys_landed"), sem("top_ready"), sem("gate_exp"), sem("picked_ready")
        s_hk, s_hkT, s_one, s_G, s_Gev = (sem("hk_transposed"), sem("hkT_copied"), sem("one_hots"),
                                                  sem("gate_matrix"), sem("gates_applied"))
        s_gel2, s_whm, s_wlm, s_tok = sem("expert_gelu"), sem("w_hi_made"), sem("w_lo_made"), sem("tokens_copied")
        s_oneB, s_ones, s_wmul, s_spill, s_back = (sem("second_one_hots"), sem("w_set_to_one"), sem("w_times_gelu"),
                                                   sem("residual_stored"), sem("residual_back"))
        s_warm, s_lo0 = sem("table_warmed"), sem("first_lo_made")
        s_top = sem("top_step")
        s_iota, s_outd = sem("iota_made"), sem("out_written")
        block = ctx.enter_context(nc.Block())

        def emptied(stage, k):
            e = EMPTIER[stage]
            return s_ev[e], EMPTIED0[e][stage] + k + 1

        def bank_of(stage, k):
            return bank[(GROUP0[stage] + k) % 4]

        def wait_bank_free(pe, stage, k):
            n = GROUP0[stage] + k
            if n >= 4:
                pe.wait_ge(*emptied(*FLAT[n - 4]))

        def unit0(stage):
            return UNIT0[stage]

        class Chain:

            def __init__(self, eng, s):
                self.eng, self.s, self.n = eng, s, 0

            def __call__(self, ins):
                self.n += 1
                ins.then_inc(self.s, 1)
                self.eng.wait_ge(self.s, self.n)

        @block.sync
        def _(sp):
            x_rows = a["x"].rearrange("(t p) d -> t p d", p=P)
            for t in range(TT):
                sp.dma_start(res[:, t, :], x_rows[t]).then_inc(s_x[t], 16)

            def load(u, i=None):
                n = u if i is None else i * 4 + u
                if 4 <= u < 8:
                    sp.wait_ge(s_lo0, u - 3)
                elif u >= 8:
                    sp.wait_ge(s_lo, n - 3)
                sp.dma_start(raw[u % 4][:], a["stream"][n]).then_inc(s_raw[u % 4], 16)

            for u in range(8):
                load(u)
            loops = (NUNIT - 8) // 4
            with sp.Fori(0, loops) as i:
                for j in range(4):
                    load(8 + j, i)
            for u in range(8 + 4 * loops, NUNIT):
                load(u)
            for n in range(8):
                c, t = slice(512 * (n // 2), 512 * (n // 2 + 1)), n % 2
                if n == 7:
                    sp.wait_ge(s_lastc, 1)
                else:
                    sp.wait_ge(s_rows1 if t else s_rows, 8 + n // 2 + 1)
                sp.dma_start(out.rearrange("(t p) d -> t p d", p=P)[t, :, c], res_out[:, t, c]).then_inc(s_outd, 16)
            sp.wait_ge(s_outd, 16 * 8)

        @block.scalar
        def _(act):
            step = Chain(act, s_act)
            act.dma_start(ln_in_gb[:, 0, :], a["ln_in_g"].broadcast_to([P, D])).then_inc(s_gb, 16)
            act.dma_start(ln_in_gb[:, 1, :], a["ln_in_b"].broadcast_to([P, D])).then_inc(s_gb, 16)
            act.dma_start(ident[:], a["ident"]).then_inc(s_id, 16)
            act.dma_start(prm[:, 0, :], a["lam_re"]).then_inc(s_par, 16)
            act.dma_start(prm[:, 1, :], a["lam_im"]).then_inc(s_par, 16)
            for g in range(2):
                act.dma_start(prm[64 * g:64 * g + 64, 2, :],
                               a["log_dt"][g:g + 1, :].broadcast_to([64, STILES])).then_inc(s_par, 16)
            act.dma_start(b_in[:, 0], a["b_re"]).then_inc(s_par, 16)
            act.dma_start(b_in[:, 1], a["b_im"]).then_inc(s_par, 16)
            act.dma_start(c_in[:, 0], a["c_re"]).then_inc(s_par, 16)
            act.dma_start(c_in[:, 1], a["c_im"]).then_inc(s_par, 16)
            act.dma_start(rope[:], a["rope"]).then_inc(s_const, 16)
            act.dma_start(dskip[:], a["dskip"]).then_inc(s_const, 16)

            def split(u, i=None, per=0):
                n = u if i is None else i * per + u
                landed = 16 * (u // 4 + 1)
                act.wait_ge(s_raw[u % 4], landed if i is None else i * (4 * per) + landed)
                if u >= 4:
                    act.wait_ge(s_mm, n - 3)
                act.activation(hi[u % 4][:], raw[u % 4][:], ACT.Copy).then_inc(s_hi, 1)

            def second_half(stage, k):
                f = TMP0[stage] + k
                if f >= 2:
                    act.wait_ge(*emptied(*[(n, m) for n in COLUMN_FORM for m in range(SIZE[n])][f - 2]))
                act.activation(tmp[f % 2][:], bank_of(stage, k)[:, T:2 * T], ACT.Copy).then_inc(s_tmp, 1)

            def transposed_hi(stage, k, dst):
                f = TH0[stage] + k
                act.wait_ge(s_tp, f + 1)
                src = bank[4 + f % 4][:].rearrange("p (c t) -> p c t", c=2)
                act.activation(dst, src, ACT.Copy).then_inc(s_th, 1)

            def normalise(nth, x, chunks):
                act.wait_ge(s_nmr, nth - 1)
                for c in range(chunks):
                    w = slice(512 * c, 512 * (c + 1))
                    act.activation(x[:, 1, w], x[:, 1, w], ACT.Identity, bias=ini[:, 4:5],
                                   scale=rs[:, 1:2]).then_inc(s_xn, 1)

            def deviation(n, count):
                act.wait_ge(s_var, n)
                act.activation(rs[:, 0:count], rs[:, 4:4 + count], ACT.Sqrt).then_inc(s_std, 1)

            deviation(1, TT)
            for u in range(4):
                split(u)
            for k in range(8):
                transposed_hi("t_in", k, actT[:, 2 * k:2 * k + 2, 0, :])
            for k in range(8):
                u = unit0("ssm_in") + 2 * k
                split(u + 4)
                split(u + 5)
                if k == 0:
                    act.wait_ge(s_par, 16 * 8)
                    act.activation(prm[:, 2, :], prm[:, 2, :], ACT.Exp).then_inc(s_prmA, 1)
                    act.wait_ge(s_prm, 1)
                    act.activation(mag[:], prm[:, 3, :], ACT.Exp).then_inc(s_prmA, 1)
                    act.activation(prm[:, 5, :], prm[:, 4, :], ACT.Sin).then_inc(s_prmA, 1)
                    act.activation(prm[:, 6, :], prm[:, 4, :], ACT.Sin, scale=0.5).then_inc(s_prmA, 1)
                act.wait_ge(s_mm, u + 2)
                second_half("ssm_in", k)

            def y_beside(block):
                s = block - TILE_BLOCK
                if s >= 7 and s % 4 == 3:
                    q = s // 4 - 1
                    act.wait_ge(s_y, q + 1)
                    act.activation(uT[:, q, :], uT[:, q, :], ACT.Gelu_apprx_tanh).then_inc(s_gel, 1)
                    act.wait_ge(s_gel, q + 1)
                    act.activation(yT[:, q, 0, :], uT[:, q, :], ACT.Copy).then_inc(s_yh, 1)

            act.dma_start(lat_g[:, 0, :], a["q_norm_g"].broadcast_to([P, QL])).then_inc(s_latg, 16)
            act.dma_start(lat_g[:, 1, :], a["kv_norm_g"].broadcast_to([P, QL])).then_inc(s_latg, 16)
            for b in range(9):
                u = unit0("latent") + 2 * b
                split(u + 4)
                if b < 8:
                    split(u + 5)
                if b == 3:
                    for k in range(4):
                        act.wait_ge(s_bbT, k + 1)
                        act.activation(bbT[:, 4 * k:4 * k + 4, :], bank[4 + k][:].rearrange("p (c s) -> p c s", c=4),
                                       ACT.Copy).then_inc(s_bbTc, 1)
                if b in (3, 7):
                    act.wait_ge(s_mm, u + 2)
                    c = b // 4
                    for t in range(TT):
                        act.activation(lat[:, t, QL * c:QL * c + QL], bank_of("latent", 2 * c + t)[:],
                                       ACT.Copy).then_inc(s_ev["A"], 1)
                if b == 8:
                    act.wait_ge(s_mm, u + 1)
                    act.wait_ge(*emptied("ssm_in", 7))
                    act.activation(tmp[0][0:ROPE, :], bank_of("k_rope", 0)[0:ROPE, T:2 * T],
                                   ACT.Copy).then_inc(s_krh, 1)
                y_beside(b)

            for b in range(32):
                u = unit0("gates") + 2 * b
                y_beside(9 + b)
                split(u + 4)
                split(u + 5)
                if b == 0:
                    act.wait_ge(*emptied("latent", 3))
                    for n in range(4):
                        t, c = n // 2, n % 2
                        step(act.activation(lat_m[:], lat[:, t, QL * c:QL * (c + 1)], ACT.Square,
                                            accum_out=mv[:, t, c:c + 1]))
                    act.sem_inc(s_sq, 1)
                if b == 1:
                    deviation(2, 4)
                if b == 2:
                    act.wait_ge(s_krt, 1)
                    act.activation(lat[:, :, 2 * QL:2 * QL + ROPE],
                                   bank_of("t_krows", 0)[:, 0:P].rearrange("p (t f) -> p t f", t=TT),
                                   ACT.Copy).then_inc(s_ev["A"], 1)
                if b == 11:
                    act.wait_ge(s_tab, 2)
                if b % 4 == 3:
                    act.wait_ge(s_mm, u + 2)
                    for t in range(TT):
                        g = 2 * (b // 4) + t
                        act.activation(gates[:, b // 4, t, :], bank_of("gates", g)[:],
                                       ACT.Copy).then_inc(s_ev["A"], 1)
            for k in range(4):
                transposed_hi("t_lat", k, latT[:, 2 * k:2 * k + 2, 0, :])

            for k in range(8):
                u = unit0("glu") + k
                act.wait_ge(s_mm, u + 1)
                second_half("glu", k)
                split(u + 4)
                if k:
                    act.wait_ge(s_glu, k)
                    act.activation(ssmT[:, k - 1, 0, :], glu_s[:, k - 1, :], ACT.Copy).then_inc(s_sh, 1)
                act.wait_ge(*emptied("glu", k))
                act.activation(glu_s[:, k, :], glu_s[:, k, :], ACT.Sigmoid).then_inc(s_sig, 1)
            act.wait_ge(s_glu, 8)
            act.activation(ssmT[:, 7, 0, :], glu_s[:, 7, :], ACT.Copy).then_inc(s_sh, 1)

            def gate_sigmoid(c):
                for t in range(TT):
                    act.activation(gates[:, c, t, :], gates[:, c, t, :], ACT.Sigmoid).then_inc(s_gsig, 1)

            act.wait_ge(*emptied("gates", 15))

            def heads_columns(stage):
                for m in range(8):
                    u = unit0(stage) + m
                    act.wait_ge(s_mm, u + 1)
                    for k in (2 * m, 2 * m + 1):
                        second_half(stage, k)
                    split(u + 4)
                    if stage == "k_nope":
                        gate_sigmoid(m)

            for b in range(2):
                u = unit0("q_rope") + 2 * b
                split(u + 4)
                split(u + 5)
                act.wait_ge(s_mm, u + 2)
                for t in range(TT):
                    act.activation(qr_rows[:, t, 512 * b:512 * (b + 1)], bank_of("q_rope", 2 * b + t)[:],
                                   ACT.Copy).then_inc(s_ev["A"], 1)
            heads_columns("q_nope")
            heads_columns("k_nope")
            for k in range(4):
                act.wait_ge(s_tr, k + 2)
                act.activation(qrT[:, 2 * k:2 * k + 2, :], bank_of("t_qr", k)[:].rearrange("p (c t) -> p c t", c=2),
                               ACT.Copy).then_inc(s_ev["A"], 1)
            for b in range(4):
                u = unit0("value") + 2 * b
                split(u + 4)
                split(u + 5)
                act.wait_ge(s_mm, u + 2)
                for t in range(TT):
                    act.activation(v01[t][:, 512 * b:512 * (b + 1)], bank_of("value", 2 * b + t)[:],
                                   ACT.Copy).then_inc(s_ev["A"], 1)
            def exp_scores(h):
                act.wait_ge(s_P, h + 1)
                act.activation(sm_p[h % 2][:, 0:P], sm_p[h % 2][:, 0:P], ACT.Exp, bias=smx[h % 2][:, 0:1],
                               accum_out=smx[h % 2][:, 2:3])
                act.activation(sm_p[h % 2][:, P:384], sm_p[h % 2][:, P:384], ACT.Exp, bias=smx[h % 2][:, 1:2],
                               accum_out=smx[h % 2][:, 3:4]).then_inc(s_E, 1)

            exp_scores(0)
            for h in range(HEADS):
                act.wait_ge(s_PT, h + 1)
                act.activation(sm_pT[h % 2][:], bank[6][:, 0:384], ACT.Copy).then_inc(s_PTs, 1)
                if h + 1 < HEADS:
                    exp_scores(h + 1)
                split(unit0("proj_ssm") + h + 4)
                act.wait_ge(s_PV, h + 1)
                act.activation(actT[:, h, 0, :], bank[7][:, 0:T], ACT.Copy).then_inc(s_pvh, 1)
            act.dma_start(ln_mix_gb[:, 0, :], a["ln_mix_g"].broadcast_to([P, D])).then_inc(s_gb, 16)
            act.dma_start(ln_mix_gb[:, 1, :], a["ln_mix_b"].broadcast_to([P, D])).then_inc(s_gb, 16)
            act.dma_start(keysT[:], a["keysT"]).then_inc(s_keys, 16)
            for n in range(32):
                split(unit0("proj_attn") + n + 4)
                if n % 8 == 5 and n > 8:
                    for k in (2 * (n // 8) - 2, 2 * (n // 8) - 1):
                        transposed_hi("t_mix", k, mixT[:, 2 * k:2 * k + 2, 0, :])
            for k in (6, 7):
                transposed_hi("t_mix", k, mixT[:, 2 * k:2 * k + 2, 0, :])
            for k in range(32):
                split(unit0("out") + k + 4)
            deviation(3, TT)
            normalise(2, res, 4)
            for k in range(8):
                transposed_hi("t_h", k, actT[:, 2 * k:2 * k + 2, 0, :])
            act.wait_ge(s_rows, 8)
            act.wait_ge(s_rows1, 8)
            for t in range(TT):
                act.dma_start(a["spill"][t], res[:, t, :]).then_inc(s_spill, 16)

            def copy_scores(h):
                act.wait_ge(s_sc, h + 1)
                act.activation(s_all[:, h::PH, :, :], bank[4 + h % 4][:].rearrange("p (t c n) -> p t c n", t=TT, c=2),
                               ACT.Copy).then_inc(s_scored, 1)

            for k in range(16):
                u = unit0("peer_q") + 2 * k
                split(u + 4)
                split(u + 5)
                act.wait_ge(s_mm, u + 2)
                second_half("peer_q", k)
                if k > 3 and k % 2:
                    copy_scores(k // 2 - 2)
            copy_scores(6)
            copy_scores(7)

            act.wait_ge(s_spill, 16 * TT)
            act.wait_ge(*emptied("peer_q", 15))

            def warm_gelu():
                act.wait_ge(s_warm, 1)
                act.activation(warm[:, 1:2], warm[:, 0:1], ACT.Gelu_apprx_tanh)

            def expert_hi(k, i):
                u = unit0("u") + 2 * k
                split(u + 4, i, 8)
                split(u + 5, i, 8)
                act.wait_ge(s_mm, i * 8 + (u + 2))

            def expert_half(k):
                act.activation(tmp[k % 2][:], bank_of("u", k)[:, T:2 * T], ACT.Copy).then_inc(s_tmp, 1)

            def expert_gelu(k, i, dst):
                act.wait_ge(s_ev["D"], i * 4 + emptied("u", k)[1])
                act.activation(dst, tmp[k % 2][:], ACT.Gelu_apprx_tanh).then_inc(s_gel2, 1)

            def w_hi(v, i=None):
                act.activation(wh[v % 2][:], W[:, v, :] if i is None else W[:, bass.ds(i * 4 + v, 1), :],
                               ACT.Copy).then_inc(s_whm, 1)

            def expert_out():
                act.wait_ge(s_wmul, 1 + GELUS)

                def steps(v, i=None):
                    u = unit0("v") + 2 * v
                    for q in range(2):
                        if i is not None or u + q + 4 < NUNIT:
                            split(u + q + 4, i, 8)
                    if i is not None or v + 2 < NKEY:
                        act.wait_ge(s_mm, (u + 2) if i is None else i * 8 + (u + 2))
                        w_hi(v + 2, i)

                with act.Fori(0, NKEY // 4 - 1) as i:
                    for j in range(4):
                        steps(j, i)
                for v in range(NKEY - 4, NKEY):
                    if v == NKEY - 4:
                        act.dma_start(res_out[:, 1, :], a["spill"][1]).then_inc(s_back, 16)
                    elif v < NKEY - 1:
                        n = v - (NKEY - 3)
                        act.dma_start(ln_out_gb[:, n, :],
                                      a[("ln_ffn_g", "ln_ffn_b")[n]].broadcast_to([P, D])).then_inc(s_gb, 16)
                    steps(v)

            act.sem_inc(s_gel2, 2)
            with act.Fori(0, GELUS // 4) as i:
                warm_gelu()
                for j in range(4):
                    expert_hi(j, i)
                    act.wait_ge(s_gel2, i * 4 + (j + 1))
                    expert_half(j)
                    expert_gelu(j, i, W[:, bass.ds(i * 4 + j, 1), :].rearrange("p o t -> p (o t)"))
            act.wait_ge(s_gel2, 2 + GELUS)
            act.wait_ge(s_topped, 1)
            act.activation(picked[:, 0], picked[:, 0], ACT.Exp).then_inc(s_gexp, 1)
            expert_hi(GELUS, 0)
            expert_half(GELUS)
            expert_gelu(GELUS, 0, tmp[GELUS % 2][:])
            for t in range(TT):
                act.wait_ge(s_hk, t + 1)
                act.activation(hkT[:, :, t * P:(t + 1) * P], bank[4 + t][:, 0:384].rearrange("p (a t) -> p a t", a=3),
                               ACT.Copy).then_inc(s_hkT, 1)
            def gated_block(j, i):
                k = GELUS + 1 + j
                expert_hi(k, i)
                act.wait_ge(s_wmul, i * 4 + (j + 1))
                expert_half(k)

            with act.Fori(0, GELUS // 4 - 1) as i:
                warm_gelu()
                for j in range(4):
                    gated_block(j, i)
                    expert_gelu(GELUS + 1 + j, i, tmp[(GELUS + 1 + j) % 2][:])
            last_turn = GELUS // 4 - 1
            for j in range(2):
                gated_block(j, last_turn)
                expert_gelu(GELUS + 1 + j, last_turn, tmp[(GELUS + 1 + j) % 2][:])
            split(unit0("u") + 2 * (NKEY - 1) + 4)
            act.wait_ge(s_Gev, 2 + GELUS)
            for v in range(2):
                w_hi(v)
            split(unit0("u") + 2 * (NKEY - 1) + 5)
            act.wait_ge(s_mm, unit0("v"))
            act.wait_ge(s_wmul, GELUS - 1)
            expert_half(NKEY - 1)
            expert_gelu(GELUS + 3, last_turn, tmp[(NKEY - 1) % 2][:])
            act.wait_ge(s_mm, unit0("v"))
            act.dma_start(res_out[:, 0, :], a["spill"][0]).then_inc(s_back, 16)
            expert_out()
            deviation(4, TT)
            normalise(3, res_out, 3)

        @block.gpsimd
        def _(pool):
            step = Chain(pool, s_pool)
            pool.iota(iota16[:], [[1, 16]], 0, 0, allow_small_or_imprecise_dtypes=True).then_inc(s_iota, 1)

            pool.memset(warm[:], 0.0).then_inc(s_warm, 1)
            for u in range(4):
                pool.wait_ge(s_hi, u + 1)
                pool.tensor_tensor(lo[u][:], raw[u][:], hi[u][:].bitcast(F32), ALU.subtract).then_inc(s_lo0, 1)
            pool.wait_ge(s_pw, 1)
            def table_doubling(first, count, k):
                st, n = slice(first, first + count), 1 << k
                c, s = table[:, st, 0, 0:n], table[:, st, 1, 0:n]
                pc = pw[:, k, 0, st].unsqueeze(2).broadcast_to([P, count, n])
                ps = pw[:, k, 1, st].unsqueeze(2).broadcast_to([P, count, n])
                m0, m1 = tab_m[0][:, 0:count, 0:n], tab_m[1][:, 0:count, 0:n]
                pool.tensor_tensor(m0, c, pc, ALU.mult)
                step(pool.tensor_tensor(m1, s, ps, ALU.mult))
                step(pool.tensor_tensor(table[:, st, 0, n:2 * n], m0, m1, ALU.subtract))
                pool.tensor_tensor(m0, c, ps, ALU.mult)
                step(pool.tensor_tensor(m1, s, pc, ALU.mult))
                step(pool.tensor_tensor(table[:, st, 1, n:2 * n], m0, m1, ALU.add))

            step(pool.memset(table[:, :, 0, 0:1], 1.0))
            step(pool.memset(table[:, :, 1, 0:1], 0.0))
            for k in range(7):
                table_doubling(0, 16, k)
            pool.sem_inc(s_tab, 1)

            def table_beside(s):
                if s == 0:
                    for k in range(3):
                        table_doubling(16, 16, k)
                elif s in (1, 2):
                    table_doubling(16, 16, s + 2)
                elif s in (3, 5):
                    table_doubling(4 * s + 4, 8, 5)
                elif 6 <= s < 14 and s % 2 == 0:
                    table_doubling(2 * s + 4, 4, 6)
                elif s == 14:
                    pool.sem_inc(s_tab, 1)

            def finish_rows(x, gb, chunks, before):
                for c in range(chunks):
                    w = slice(512 * c, 512 * (c + 1))
                    pool.wait_ge(s_xn, before + c + 1)
                    step(pool.tensor_tensor(x[:, 1, w], x[:, 1, w], gb[:, 0, w], ALU.mult))
                    pool.tensor_tensor(x[:, 1, w], x[:, 1, w], gb[:, 1, w], ALU.add).then_inc(s_rows1, 1)

            for s in range(STILES):
                pool.wait_ge(s_z, s + 1)
                if s >= 1:
                    pool.wait_ge(s_xr, s)
                if s >= 2:
                    pool.wait_ge(s_cy, s - 1)
                x = xs[s % 2]
                c = table[:, s, 0:1, :].broadcast_to([P, 4, TH])
                n = table[:, s, 1:2, :].broadcast_to([P, 4, TH])
                zf, xf, mf = (b[:].rearrange("p a (h t) -> p (a h) t", h=2) for b in (z[s % 2], x, xs_m))
                pool.tensor_tensor(xf, zf, c, ALU.mult)
                step(pool.tensor_tensor(mf, zf, n, ALU.mult))
                pool.tensor_tensor(x[:, 0, :], x[:, 0, :], xs_m[:, 1, :], ALU.subtract)
                pool.tensor_tensor(x[:, 1, :], x[:, 1, :], xs_m[:, 0, :], ALU.add).then_inc(s_xr, 1)
                table_beside(s)

            pool.wait_ge(*emptied("q_rope", 3))
            for t in range(TT):
                rows = qr_rows[:, t, :].rearrange("p (h x) -> p h x", h=HEADS)
                rot = qr_rot[:, t, :].rearrange("p (h x) -> p h x", h=HEADS)
                m = [rope_m[:, n // 2, 512 * (n % 2):512 * (n % 2) + 512].rearrange("p (h x) -> p h x", h=HEADS)
                     for n in range(4)]
                cos = rope[:, t, 0:1, :].broadcast_to([P, HEADS, 32])
                sin = rope[:, t, 1:2, :].broadcast_to([P, HEADS, 32])
                pool.tensor_tensor(m[0], rows[:, :, 0:32], cos, ALU.mult)
                pool.tensor_tensor(m[1], rows[:, :, 32:64], sin, ALU.mult)
                pool.tensor_tensor(m[2], rows[:, :, 0:32], sin, ALU.mult)
                step(pool.tensor_tensor(m[3], rows[:, :, 32:64], cos, ALU.mult))
                pool.tensor_tensor(rot[:, :, 0:32], m[0], m[1], ALU.subtract)
                pool.tensor_tensor(rot[:, :, 32:64], m[2], m[3], ALU.add).then_inc(s_qr, 1)
                pool.wait_ge(s_qr, t + 1)

            pool.wait_ge(s_gb, 64)
            finish_rows(res, ln_mix_gb, 4, 0)
            pool.wait_ge(s_scored, PH)
            pool.iota(iota[:], [[1, NKEY]], 0, 0, allow_small_or_imprecise_dtypes=True).then_inc(s_iota, 1)
            low, high = 184 - 80, 200 - 80
            pool.memset(W[:, GELUS:low, :], 1.0)
            pool.memset(W[:, high:NKEY, :], 1.0)
            pool.wait_ge(*emptied("u", GELUS - 4))
            pool.memset(W[:, low:high, :], 1.0).then_inc(s_ones, 1)
            pool.wait_ge(s_iota, 2)
            pool.wait_ge(s_hkT, TT)
            def copy_tokens(g, i):
                pool.wait_ge(s_G, i * 4 + (g + 1))
                pool.tensor_copy(tok[g % 2][:], hkT[:, :, bass.ds(i * (4 * GT) + GT * g, GT)]).then_inc(s_tok, 1)

            def second_one_hots(g, i):
                copy_tokens(g, i)
                pool.wait_ge(s_tok, i * 4 + (g + 1))
                pool.tensor_tensor(tok_m[g % 2][:], tok[g % 2][:, 0, :], tok[g % 2][:, 2, :], ALU.mult)
                for t in range(GT):
                    last = pool.tensor_scalar(oneB[g % 2][:, t, :], iota[:], tok[g % 2][:, 2, t:t + 1],
                                              tok[g % 2][:, 0, t:t + 1], ALU.is_equal, ALU.mult)
                last.then_inc(s_oneB, 1)

            copy_tokens(0, 0)
            with pool.Fori(0, GELUS // 4 - 1) as i:
                for j in range(4):
                    second_one_hots(1 + j, i)
            for j in range(3):
                second_one_hots(1 + j, GELUS // 4 - 1)
            pool.wait_ge(s_gb, 96)
            finish_rows(res_out, ln_out_gb, 3, 4)

        @block.vector
        def _(dve):
            step = Chain(dve, s_dve)

            def split(u, i=None, per=0):
                n = u if i is None else i * per + u
                dve.wait_ge(s_hi, n + 1)
                dve.tensor_tensor(lo[u % 4][:], raw[u % 4][:], hi[u % 4][:].bitcast(F32),
                                  ALU.subtract).then_inc(s_lo, 1)

            def add_halves(stage, k, dst, i=None, per=0):
                f = TMP0[stage] + k
                dve.wait_ge(s_tmp, f + 1 if i is None else i * per + (f + 1))
                dve.tensor_tensor(dst, bank_of(stage, k)[:, 0:T], tmp[f % 2][:], ALU.add).then_inc(s_ev["D"], 1)

            def transposed_lo(stage, k, dst):
                f = TH0[stage] + k
                dve.wait_ge(s_th, f + 1)
                src = bank[4 + f % 4][:].rearrange("p (c t) -> p c t", c=2)
                dve.tensor_tensor(dst[:, 2 * k:2 * k + 2, 1, :], src, dst[:, 2 * k:2 * k + 2, 0, :].bitcast(F32),
                                  ALU.subtract).then_inc(s_tl, 1)

            def inverse_deviation(n, count):
                r, t, v = rs[:, 0:count], mv[:, :, :].rearrange("p a b -> p (a b)")[:, 0:count], rs[:, 4:4 + count]
                dve.wait_ge(s_std, n)
                step(dve.reciprocal(r, r))
                step(dve.tensor_tensor(ini[:, 0:count], r, r, ALU.mult))
                step(dve.tensor_tensor(ini[:, 0:count], ini[:, 0:count], v, ALU.mult))
                step(dve.tensor_scalar(ini[:, 0:count], ini[:, 0:count], -0.5, 1.5, ALU.mult, ALU.add))
                step(dve.tensor_tensor(r, r, ini[:, 0:count], ALU.mult))

            def row_stats(x, t, c):
                return dve.bn_stats(stats[:, t, c, :], x[:, t, 512 * c:512 * (c + 1)])

            def layer_norm(n, nth, gb, x=res, after=None):
                for t in range(TT):
                    last = dve.bn_aggr(mv[:, t, :], stats[:, t].rearrange("p c s -> p (c s)"))
                step(last)
                dve.tensor_scalar(rs[:, 4:4 + TT], mv[:, :, 1], LN_EPS, None, ALU.add).then_inc(s_var, 1)
                inverse_deviation(n, TT)
                if nth > 1:
                    dve.scalar_tensor_tensor(ini[:, 4:5], mv[:, 1, 0:1], -1.0, rs[:, 1:2], ALU.mult,
                                             ALU.mult).then_inc(s_nmr, 1)
                dve.wait_ge(s_gb, 32 * nth)
                for c in range(4):
                    w = slice(512 * c, 512 * (c + 1))
                    tiles = range(TT) if nth == 1 or (nth == 3 and c == 3) else range(1)
                    for t in tiles:
                        last = dve.scalar_tensor_tensor(x[:, t, w], x[:, t, w], mv[:, t, 0:1], gb[:, 0, w],
                                                        ALU.subtract, ALU.mult)
                    step(last)
                    for t in tiles:
                        ready = s_rows if t == 0 else s_rows1 if nth == 1 else s_lastc
                        dve.scalar_tensor_tensor(x[:, t, w], x[:, t, w], rs[:, t:t + 1], gb[:, 1, w],
                                                 ALU.mult, ALU.add).then_inc(ready, 1)
                    if after is not None and c:
                        after(2 * c - 2)
                        after(2 * c - 1)
                if after is not None:
                    after(6)
                    after(7)

            def lo_of(stage):
                def after(k):
                    transposed_lo(stage, k, actT)
                return after

            (LR, LI, DT, LRDT, PHI, SIN, SINH, K2, DEN, NR, NI, CR, CI, M0, M1, COS) = range(16)

            def pr(n):
                return prm[:, n, :]

            def tt(o, x, y, op):
                step(dve.tensor_tensor(o, x, y, op))

            dve.memset(mask[:], 0.0)
            step(dve.memset(bb_rows[:], 0.0))
            step(dve.memset(c_blk[:], 0.0))
            step(dve.memset(mask[0:64, 64:128], MASKED))
            step(dve.memset(mask[0:64, 320:384], MASKED))
            cr, ci = (pr(x).unsqueeze(2).broadcast_to([P, STILES, 16]) for x in (CR, CI))
            mb = [bb_m[0][:], bb_m[1][:]]

            def ssm_params(part):
                if part == 0:
                    dve.wait_ge(s_par, 16 * 8)
                    dve.wait_ge(s_prmA, 1)
                    tt(pr(PHI), pr(LI), pr(DT), ALU.mult)
                    magic = 12582912.0
                    step(dve.tensor_scalar(pr(K2), pr(PHI), 1.0 / (2 * math.pi), magic, ALU.mult, ALU.add))
                    step(dve.tensor_scalar(pr(K2), pr(K2), magic, None, ALU.subtract))
                    for c in (6.28125, 0.0019350051879882812, 3.0199157663446332e-07):
                        step(dve.scalar_tensor_tensor(pr(PHI), pr(K2), -c, pr(PHI), ALU.mult, ALU.add))
                    step(dve.tensor_scalar(pr(PHI), pr(PHI), 3.1415925, -3.1415925, ALU.min, ALU.max))
                    dve.tensor_tensor(pr(LRDT), pr(LR), pr(DT), ALU.mult).then_inc(s_prm, 1)
                elif part == 1:
                    dve.wait_ge(s_prmA, 4)
                    tt(pr(M0), pr(SINH), pr(SINH), ALU.mult)
                    step(dve.tensor_scalar(pr(COS), pr(M0), -2.0, 1.0, ALU.mult, ALU.add))
                    dve.tensor_copy(pw[:, 0, 0, :], pr(COS))
                    step(dve.tensor_copy(pw[:, 0, 1, :], pr(SIN)))
                if part in (1, 2):
                    for k in range(3) if part == 1 else range(3, 7):
                        c, s = pw[:, k, 0, :], pw[:, k, 1, :]
                        dve.tensor_tensor(pr(M0), c, c, ALU.mult)
                        dve.scalar_tensor_tensor(pw[:, k + 1, 1, :], c, 2.0, s, ALU.mult, ALU.mult)
                        tt(pr(M1), s, s, ALU.mult)
                        tt(pw[:, k + 1, 0, :], pr(M0), pr(M1), ALU.subtract)
                    if part == 2:
                        dve.tensor_copy(wTH[:], pw[:, 7]).then_inc(s_pw, 1)
                elif part == 3:
                    tt(pr(NR), mag[:], pr(COS), ALU.mult)
                    dve.tensor_scalar(pr(NR), pr(NR), -1.0, None, ALU.add)
                    dve.tensor_tensor(pr(NI), mag[:], pr(SIN), ALU.mult)
                    dve.tensor_tensor(pr(M0), pr(LR), pr(LR), ALU.mult)
                    tt(pr(M1), pr(LI), pr(LI), ALU.mult)
                    tt(pr(DEN), pr(M0), pr(M1), ALU.add)
                    step(dve.reciprocal(pr(DEN), pr(DEN)))
                    for o, x, y, op in ((CR, NR, NI, ALU.add), (CI, NI, NR, ALU.subtract)):
                        dve.tensor_tensor(pr(M0), pr(x), pr(LR), ALU.mult)
                        tt(pr(M1), pr(y), pr(LI), ALU.mult)
                        tt(pr(M0), pr(M0), pr(M1), op)
                        tt(pr(o), pr(M0), pr(DEN), ALU.mult)
                elif part in (4, 5):
                    ri, x0, x1, op = ((0, 0, 1, ALU.subtract), (1, 1, 0, ALU.add))[part - 4]
                    dve.tensor_tensor(mb[0], b_in[:, x0], cr, ALU.mult)
                    tt(mb[1], b_in[:, x1], ci, ALU.mult)
                    for g in range(2):
                        r = slice(64 * g, 64 * g + 64)
                        o = bb_rows[r, ri].rearrange("p q (j h) -> p (q j) h", h=32)[:, :, 16 * g:16 * g + 16]
                        tt(o, mb[0][r], mb[1][r], op)
                elif part == 6:
                    for ri, sign in ((0, 1.0), (1, -1.0)):
                        for g in range(2):
                            r = slice(64 * g, 64 * g + 64)
                            last = dve.tensor_scalar(c_blk[r, :, ri, 16 * g:16 * g + 16], c_in[r, ri], sign, None,
                                                     ALU.mult)
                    last.then_inc(s_bb, 1)

            dve.sem_inc(s_lo, 4)
            for t in range(TT):
                dve.wait_ge(s_x[t], 16)
                for c in range(4):
                    last = row_stats(res, t, c)
            step(last)
            layer_norm(1, 1, ln_in_gb, after=lo_of("t_in"))
            for k in range(8):
                u = unit0("ssm_in") + 2 * k
                split(u + 4)
                split(u + 5)
                ssm_params(k)
                add_halves("ssm_in", k, uT[:, k, :])

            def scan_tile(s, u):
                m0, m1, zz = rot_m[0], rot_m[1], z[s % 2]
                dve.wait_ge(s_tab, 1 if s < 16 else 2)
                if s:
                    dve.wait_ge(s_z, s)
                dve.wait_ge(s_bu, s + 1)
                c = table[:, s, 0:1, :].broadcast_to([P, 4, TH])
                n = table[:, s, 1:2, :].broadcast_to([P, 4, TH])
                bu = bank[4 + s % 2][:].rearrange("p (f t) -> p f t", f=4)
                dve.tensor_tensor(m0[:].rearrange("p a (h t) -> p (a h) t", h=2), bu, c, ALU.mult)
                last = dve.tensor_tensor(m1[:].rearrange("p a (h t) -> p (a h) t", h=2), bu, n, ALU.mult)
                last.then_inc(s_bufree, 1)
                if u is not None:
                    split(u)
                dve.wait_ge(s_bufree, s + 1)
                dve.tensor_tensor(m0[:, 0, :], m0[:, 0, :], m1[:, 1, :], ALU.add)
                step(dve.tensor_tensor(m0[:, 1, :], m0[:, 1, :], m1[:, 0, :], ALU.subtract))
                if s >= 2:
                    dve.wait_ge(s_xr, s - 1)
                r = mag[:, s:s + 1].broadcast_to([P, TH])
                dve.tensor_tensor_scan(zz[:, 0, 0:TH], r, m0[:, 0, 0:TH], 0.0, ALU.mult, ALU.add)
                step(dve.tensor_tensor_scan(zz[:, 1, 0:TH], r, m0[:, 1, 0:TH], 0.0, ALU.mult, ALU.add))
                zr, zi = zz[:, 0, TH - 1:TH], zz[:, 1, TH - 1:TH]
                wc, ws = wTH[:, 0, s:s + 1], wTH[:, 1, s:s + 1]
                dve.tensor_tensor(ini[:, 0:1], zi, ws, ALU.mult)
                step(dve.tensor_tensor(ini[:, 1:2], zr, ws, ALU.mult))
                dve.scalar_tensor_tensor(ini[:, 2:3], zr, wc, ini[:, 0:1], ALU.mult, ALU.subtract)
                step(dve.scalar_tensor_tensor(ini[:, 3:4], zi, wc, ini[:, 1:2], ALU.mult, ALU.add))
                dve.tensor_tensor_scan(zz[:, 0, TH:], r, m0[:, 0, TH:], ini[:, 2:3], ALU.mult, ALU.add)
                dve.tensor_tensor_scan(zz[:, 1, TH:], r, m0[:, 1, TH:], ini[:, 3:4], ALU.mult,
                                       ALU.add).then_inc(s_z, 1)

            def y_chunk(q):
                dve.wait_ge(s_cy, 4 * q + 4)
                dve.scalar_tensor_tensor(uT[:, q, :], uT[:, q, :], dskip[:, q:q + 1], bank[6 + q % 2][:, 0:T],
                                         ALU.mult, ALU.add).then_inc(s_y, 1)

            def ssm_beside(block, u):
                s = block - TILE_BLOCK
                if 0 <= s < STILES:
                    scan_tile(s, u)
                elif u is not None:
                    split(u)
                q = (s - 6) // 4
                if s >= 6 and s % 4 == 2 and q < 8:
                    y_chunk(q)
                    if q:
                        y_lo(q - 1)

            def y_lo(q):
                dve.wait_ge(s_yh, q + 1)
                dve.tensor_tensor(yT[:, q, 1, :], uT[:, q, :], yT[:, q, 0, :].bitcast(F32),
                                  ALU.subtract).then_inc(s_yl, 1)

            dve.wait_ge(s_const, 32)
            for b in range(9):
                u = unit0("latent") + 2 * b
                split(u + 4)
                ssm_beside(b, u + 5 if b < 8 else None)
            dve.wait_ge(s_krh, 1)
            dve.tensor_tensor(kr_sum[:], bank_of("k_rope", 0)[0:ROPE, 0:T], tmp[0][0:ROPE, :],
                              ALU.add).then_inc(s_ev["D"], 1)

            cos, sin = rope[:, :, 0, :], rope[:, :, 1, :]
            x1, x2 = lat[:, :, 2 * QL:2 * QL + 32], lat[:, :, 2 * QL + 32:2 * QL + 64]
            km = [lat_m[:, 64 * n:64 * n + 64].rearrange("p (a b) -> p a b", a=TT) for n in range(4)]
            for b in range(32):
                u = unit0("gates") + 2 * b
                split(u + 4)
                ssm_beside(9 + b, u + 5)
                if b == 1:
                    dve.wait_ge(s_sq, 1)
                    dve.tensor_scalar(rs[:, 4:8], mv[:].rearrange("p a b -> p (a b)"), 1.0 / QL, RMS_EPS,
                                      ALU.mult, ALU.add).then_inc(s_var, 1)
                elif b == 2:
                    inverse_deviation(2, 4)
                    dve.wait_ge(s_latg, 32)
                elif b in (3, 4):
                    t = b - 3
                    for c in range(2):
                        x = lat[:, t, QL * c:QL * (c + 1)]
                        n = 2 * t + c
                        dve.scalar_tensor_tensor(x, x, rs[:, n:n + 1], lat_g[:, c, :], ALU.mult, ALU.mult)
                elif b == 31:
                    y_lo(7)
                elif b == 8:
                    dve.wait_ge(*emptied("t_krows", 0))
                    dve.tensor_tensor(km[0], x1, cos, ALU.mult)
                    dve.tensor_tensor(km[1], x2, sin, ALU.mult)
                    dve.tensor_tensor(km[2], x1, sin, ALU.mult)
                    step(dve.tensor_tensor(km[3], x2, cos, ALU.mult))
                    for d in range(2):
                        dve.tensor_tensor(kr_rows[:, :, 64 * d:64 * d + 32], km[0], km[1], ALU.subtract)
                        last = dve.tensor_tensor(kr_rows[:, :, 64 * d + 32:64 * d + 64], km[2], km[3], ALU.add)
                    last.then_inc(s_krot, 1)
            for k in range(4):
                transposed_lo("t_lat", k, latT)

            def glu_product(k):
                dve.wait_ge(s_sig, k + 1)
                dve.tensor_tensor(glu_s[:, k, :], glu_s[:, k, :], uT[:, k, :], ALU.mult).then_inc(s_glu, 1)

            def glu_lo(k):
                dve.wait_ge(s_sh, k + 1)
                dve.tensor_tensor(ssmT[:, k, 1, :], glu_s[:, k, :], ssmT[:, k, 0, :].bitcast(F32),
                                  ALU.subtract).then_inc(s_sl, 1)

            for k in range(8):
                if k:
                    glu_product(k - 1)
                add_halves("glu", k, glu_s[:, k, :])
                split(unit0("glu") + k + 4)
                if k > 1:
                    glu_lo(k - 2)
            glu_product(7)
            glu_lo(6)
            for k in range(4):
                split(unit0("q_rope") + k + 4)
            glu_lo(7)

            def heads_columns(stage, dst):
                for m in range(8):
                    for k in (2 * m, 2 * m + 1):
                        add_halves(stage, k, dst[:, k, :])
                    split(unit0(stage) + m + 4)

            heads_columns("q_nope", qT)
            heads_columns("k_nope", kT)
            dve.wait_ge(s_tr, 1)
            dve.tensor_copy(krT[:], bank_of("t_kr", 0)[:, 0:T]).then_inc(s_ev["D"], 1)
            for k in range(8):
                split(unit0("value") + k + 4)

            def mask_scores(h):
                p = sm_p[h % 2]
                dve.wait_ge(s_S, h + 1)
                if h >= 2:
                    dve.wait_ge(s_PT, h - 1)
                step(dve.scalar_tensor_tensor(p[:], bank[4 + h % 2][:, 0:384], SCALE, mask[:], ALU.mult, ALU.add))
                dve.tensor_reduce(smx[h % 2][:, 0:1], p[:, 0:P], AX_X, ALU.max, negate=True)
                dve.tensor_reduce(smx[h % 2][:, 1:2], p[:, P:384], AX_X, ALU.max, negate=True).then_inc(s_P, 1)

            def normalise_scores(h):
                p, mx = sm_p[h % 2], smx[h % 2]
                dve.wait_ge(s_E, h + 1)
                step(dve.reciprocal(mx[:, 4:6], mx[:, 2:4]))
                dve.tensor_scalar(p[:, 0:P], p[:, 0:P], mx[:, 4:5], None, ALU.mult)
                dve.tensor_scalar(p[:, P:384], p[:, P:384], mx[:, 5:6], None, ALU.mult).then_inc(s_Pn, 1)

            dve.wait_ge(s_gsig, 16)
            mask_scores(0)
            normalise_scores(0)
            for h in range(HEADS):
                if h + 1 < HEADS:
                    mask_scores(h + 1)
                    normalise_scores(h + 1)
                u = unit0("proj_ssm") + h
                split(u + 4)
                dve.wait_ge(s_pvh, h + 1)
                dve.tensor_tensor(actT[:, h, 1, :], bank[7][:, 0:T], actT[:, h, 0, :].bitcast(F32),
                                  ALU.subtract).then_inc(s_pvl, 1)
                if h % 4 == 3:
                    c = h // 4
                    dve.wait_ge(s_mm, u + 1)
                    for t in range(TT):
                        g = gates[:, 4 + c, t, :]
                        dve.tensor_tensor(g, g, bank_of("proj_ssm", 2 * c + t)[:], ALU.mult).then_inc(s_ev["D"], 1)
            for b in range(16):
                u = unit0("proj_attn") + 2 * b
                split(u + 4)
                if b < 15:
                    split(u + 5)
                if b % 4 == 3:
                    dve.wait_ge(s_mm, u + 2)
                    for t in range(TT):
                        g = gates[:, b // 4, t, :]
                        k = 2 * (b // 4) + t
                        dve.tensor_tensor(g, g, bank_of("proj_attn", k)[:], ALU.mult).then_inc(s_ev["D"], 1)
                    dve.wait_ge(*emptied("proj_attn", 2 * (b // 4) + 1))
                    for t in range(TT):
                        g, gs = gates[:, b // 4, t, :], gates[:, 4 + b // 4, t, :]
                        last = dve.tensor_tensor(gs, gs, g, ALU.add)
                    last.then_inc(s_mix, 1)
                if b == 15:
                    split(u + 5)
                if b % 4 == 3 and b > 4:
                    for k in (2 * (b // 4) - 2, 2 * (b // 4) - 1):
                        transposed_lo("t_mix", k, mixT)
            for k in (6, 7):
                transposed_lo("t_mix", k, mixT)
            for b in range(16):
                u = unit0("out") + 2 * b
                split(u + 4)
                if b < 15:
                    split(u + 5)
                if b % 4 == 3:
                    dve.wait_ge(s_mm, u + 2)
                    for t in range(TT):
                        k = 2 * (b // 4) + t
                        r = res[:, t, 512 * (b // 4):512 * (b // 4 + 1)]
                        dve.scalar_tensor_tensor(r, r, ALPHA, bank_of("out", k)[:], ALU.mult,
                                                 ALU.add).then_inc(s_ev["D"], 1)
                    dve.wait_ge(*emptied("out", 2 * (b // 4) + 1))
                    for t in range(TT):
                        last = row_stats(res, t, b // 4)
                    step(last)
            layer_norm(3, 2, ln_mix_gb, after=lo_of("t_h"))
            split(unit0("peer_q") + 3)
            for k in range(16):
                u = unit0("peer_q") + 2 * k
                split(u + 4)
                split(u + 5)
                add_halves("peer_q", k, pqT[:, k, :])
            dve.wait_ge(s_scored, PH)

            cand, cand2 = (x[:].rearrange("p a b -> p (a b)") for x in (tk_cand, tk_cand2))
            eq = tk_eq[:]

            def top_stage(n, i):
                if n:
                    dve.wait_ge(s_top, n)
                if n == 0:
                    last = dve.tensor_copy(tk_s[:], s_all[:, bass.ds(i, 1)].rearrange("p o c n -> p (o c) n"))
                elif n == 1:
                    for c in range(2):
                        last = dve.max(tk_v[:, c, 0:8], tk_s[:, c, :])
                elif n == 2:
                    for c in range(2):
                        dve.max_index(tk_i[:, c, 0:8], tk_v[:, c, 0:8], tk_s[:, c, :])
                        last = dve.match_replace(tk_s2[:, c, :], tk_v[:, c, 0:8], tk_s[:, c, :], LOWEST)
                elif n == 3:
                    for c in range(2):
                        last = dve.max(tk_v[:, c, 8:16], tk_s2[:, c, :])
                elif n == 4:
                    for c in range(2):
                        last = dve.max_index(tk_i[:, c, 8:16], tk_v[:, c, 8:16], tk_s2[:, c, :])
                elif n == 5:
                    dve.tensor_copy(tk_if[:], tk_i[:])
                    last = dve.tensor_tensor(tk_cand[:], tk_v[:, 0, :].unsqueeze(2).broadcast_to([P, 16, 16]),
                                             tk_v[:, 1, :].unsqueeze(1).broadcast_to([P, 16, 16]), ALU.add)
                elif n == 6:
                    last = dve.max(tk_top[:, 0:8], cand)
                elif n == 7:
                    dve.max_index(tk_pos[:, 0:8], tk_top[:, 0:8], cand)
                    last = dve.match_replace(cand2, tk_top[:, 0:8], cand, LOWEST)
                elif n == 8:
                    last = dve.max(tk_top[:, 8:16], cand2)
                elif n == 9:
                    last = dve.max_index(tk_pos[:, 8:16], tk_top[:, 8:16], cand2)
                elif n == 10:
                    dve.tensor_scalar(tk_pu[:, 0, :], tk_pos[:], 4, None, ALU.logical_shift_right)
                    dve.tensor_scalar(tk_pu[:, 1, :], tk_pos[:], 15, None, ALU.bitwise_and)
                    last = dve.tensor_scalar(tk_gate[:], tk_top[:], tk_top[:, 0:1], None, ALU.subtract)
                elif n == 11:
                    last = dve.tensor_copy(tk_pf[:], tk_pu[:])
                elif n in (12, 13, 14):
                    for c in range(2):
                        e = eq[:, c]
                        if n == 12:
                            last = dve.tensor_tensor(e, tk_pf[:, c, :].unsqueeze(2).broadcast_to([P, 16, 16]),
                                                     iota16[:].unsqueeze(1).broadcast_to([P, 16, 16]), ALU.is_equal)
                        elif n == 13:
                            last = dve.tensor_tensor(e, e, tk_if[:, c, :].unsqueeze(1).broadcast_to([P, 16, 16]),
                                                     ALU.mult)
                        else:
                            last = dve.tensor_reduce(tk_sel[:, c, :], e, AX_X, ALU.add)
                else:
                    dve.tensor_copy(picked[:, 0, bass.ds(i, 1), :].rearrange("p o k -> p (o k)"), tk_gate[:])
                    last = dve.tensor_copy(picked[:, 1:3, bass.ds(i, 1), :].rearrange("p a o k -> p (a o) k"),
                                           tk_sel[:])
                last.then_inc(s_top, 1)

            def add_expert(k, i):
                dve.wait_ge(s_tmp, i * 4 + (TMP0["u"] + k + 1))
                dve.tensor_tensor(tmp[k % 2][:], bank_of("u", k)[:, 0:T], tmp[k % 2][:],
                                  ALU.add).then_inc(s_ev["D"], 1)

            with dve.Fori(0, GELUS // 4) as i:
                for j in range(4):
                    u = unit0("u") + 2 * j
                    split(u + 4, i, 8)
                    top_stage(4 * j, i)
                    split(u + 5, i, 8)
                    add_expert(j, i)
                    top_stage(4 * j + 1, i)
                    top_stage(4 * j + 2, i)
                    top_stage(4 * j + 3, i)
                dve.wait_ge(s_top, 16)
                dve.sem_clear(s_top)
            dve.sem_inc(s_topped, 1)
            dve.wait_ge(s_gexp, 1)
            step(dve.tensor_reduce(gsum[:, 0, :], picked[:, 0], AX_X, ALU.add))
            step(dve.reciprocal(gsum[:, 1, :], gsum[:, 0, :]))
            dve.tensor_tensor(picked[:, 0], picked[:, 0], gsum[:, 1, :].unsqueeze(2).broadcast_to([P, 16, 16]),
                              ALU.mult).then_inc(s_picked, 1)

            def first_one_hots(g, i):
                dve.wait_ge(s_tok, i * 4 + (g + 1))
                for t in range(GT):
                    last = dve.tensor_scalar(oneA[g % 2][:, t, :], iota[:], tok[g % 2][:, 1, t:t + 1], None, ALU.is_equal)
                last.then_inc(s_one, 1)

            def apply_gates(g, i):
                dve.wait_ge(s_G, i * 4 + (g + 3))
                dve.wait_ge(s_wmul, i * 4 + (g + 2))
                w = W[:, :, bass.ds(i * (4 * GT) + GT * g, GT)]
                dve.tensor_tensor(w, w, bank[4 + g % 2][:].rearrange("p (t n) -> p n t", t=GT),
                                  ALU.mult).then_inc(s_Gev, 1)

            def times_gelu(k, i, laid):
                dve.wait_ge(s_gel2, i * 4 + (2 + k + 1))
                dve.wait_ge(s_Gev, i * 4 + laid)
                w = W[:, bass.ds(i * 4 + k, 1), :].rearrange("p o t -> p (o t)")
                dve.tensor_tensor(w, w, tmp[k % 2][:], ALU.mult).then_inc(s_wmul, 1)

            def expert_lo(k, i, q):
                split(unit0("u") + 2 * k + 4 + q, i, 8)

            dve.sem_inc(s_wmul, 1)
            dve.sem_inc(s_Gev, 2)
            expert_lo(GELUS, 0, 0)
            expert_lo(GELUS, 0, 1)
            add_expert(GELUS, 0)
            dve.wait_ge(s_ones, 1)
            times_gelu(GELUS, 0, 2)
            dve.wait_ge(s_iota, 2)
            dve.wait_ge(s_hkT, TT)
            dve.wait_ge(s_tok, 1)
            for t in range(GT):
                dve.tensor_scalar(oneB[0][:, t, :], iota[:], tok[0][:, 2, t:t + 1], tok[0][:, 0, t:t + 1],
                                  ALU.is_equal, ALU.mult)
            first_one_hots(0, 0)

            def gated_block(j, i):
                k = GELUS + 1 + j
                first_one_hots(j + 1, i)
                expert_lo(k, i, 0)
                expert_lo(k, i, 1)
                add_expert(k, i)
                apply_gates(j, i)
                times_gelu(k, i, j + 3)

            with dve.Fori(0, GELUS // 4 - 1) as i:
                for j in range(4):
                    gated_block(j, i)
            last_turn = GELUS // 4 - 1
            for j in range(2):
                gated_block(j, last_turn)
            first_one_hots(3, last_turn)
            expert_lo(GELUS + 3, last_turn, 0)
            apply_gates(2, last_turn)
            dve.wait_ge(s_Gev, 2 + GELUS - 1)
            dve.wait_ge(s_G, 2 + GELUS)
            dve.tensor_tensor(W[:, :, T - GT:T], W[:, :, T - GT:T], bank[5][:].rearrange("p (t n) -> p n t", t=GT),
                              ALU.mult).then_inc(s_Gev, 1)

            def w_lo(v, i=None):
                dve.wait_ge(s_whm, v + 1 if i is None else i * 4 + (v + 1))
                w = W[:, v, :] if i is None else W[:, bass.ds(i * 4 + v, 1), :].rearrange("p o t -> p (o t)")
                dve.tensor_tensor(wl[v % 2][:], w, wh[v % 2][:].bitcast(F32), ALU.subtract).then_inc(s_wlm, 1)

            for v in range(2):
                w_lo(v)
            expert_lo(GELUS + 3, last_turn, 1)
            add_expert(GELUS + 3, last_turn)
            times_gelu(GELUS + 3, last_turn, GELUS + 2 - 4 * last_turn)

            def out_steps(v, i=None):
                u = unit0("v") + 2 * v
                for q in range(2):
                    if i is not None or u + q + 4 < NUNIT:
                        split(u + q + 4, i, 8)
                if i is not None or v + 2 < NKEY:
                    w_lo(v + 2, i)

            with dve.Fori(0, NKEY // 4 - 1) as i:
                for j in range(4):
                    out_steps(j, i)
            for v in range(NKEY - 4, NKEY):
                out_steps(v)
            dve.wait_ge(s_back, 16 * TT)
            for n, (q, t, c) in enumerate((q, t, c) for q in range(2) for t in range(TT) for c in (2 * q, 2 * q + 1)):
                if n % 4 == 0:
                    dve.wait_ge(s_mm, NUNIT - 1 + q)
                x = res_out[:, t, 512 * c:512 * (c + 1)]
                dve.scalar_tensor_tensor(x, x, ALPHA, bank[4 * t + c][:], ALU.mult, ALU.add).then_inc(s_ev["D"], 1)
                if n:
                    dve.wait_ge(*emptied("v", n - 1))
                    row_stats(res_out, *done)
                done = t, c
            dve.wait_ge(*emptied("v", 7))
            step(row_stats(res_out, *done))
            layer_norm(4, 3, ln_out_gb, res_out)

        @block.tensor
        def _(pe):
            def mm_done(ins):
                ins.then_inc(s_mm, 1)

            def wait_unit(u, i=None, per=0):
                if i is None and u < 4:
                    pe.wait_ge(s_lo0, u + 1)
                else:
                    pe.wait_ge(s_lo, u + 1 if i is None else i * per + (u + 1))

            def columns(dst, u, first, x, n, kc0, start, stop):
                for k in range(n):
                    w = slice((first + k) * P, (first + k + 1) * P)
                    pe.matmul(dst[:, :], hi[u % 4][:, w], x[:, kc0 + k, :, :].rearrange("p a t -> p (a t)"),
                              start=start and k == 0, stop=False)
                    last = pe.matmul(dst[:, 0:T], lo[u % 4][:, w], x[:, kc0 + k, 0, :], start=False,
                                     stop=stop and k == n - 1)
                return last

            def rows(dsts, u, x, kc0, start, stop, nk=2, width=512, tiles=range(TT)):
                for t in tiles:
                    tok_ = slice(t * P, (t + 1) * P)
                    for k in range(nk):
                        w = slice(k * width, (k + 1) * width)
                        o = dsts[t][:, 0:width]
                        pe.matmul(o, x[:, kc0 + k, 0, tok_], hi[u % 4][:, w], start=start and k == 0, stop=False)
                        pe.matmul(o, x[:, kc0 + k, 0, tok_], lo[u % 4][:, w], start=False, stop=False)
                        last = pe.matmul(o, x[:, kc0 + k, 1, tok_], hi[u % 4][:, w], start=False,
                                         stop=stop and k == nk - 1)
                return last

            def transposes(dst, sources, signal):
                for n, src in enumerate(sources):
                    last = pe.transpose(dst[:, n * P:(n + 1) * P], src, ident[:])
                last.then_inc(signal, 1)

            def split_transposes(stage, k, sources):
                f = TH0[stage] + k
                if f >= 4:
                    pe.wait_ge(s_tl, f - 3)
                transposes(bank[4 + f % 4], sources, s_tp)

            def row_chunk(src, k):
                return [src[:, t, c * P:(c + 1) * P] for c in (2 * k, 2 * k + 1) for t in range(TT)]

            def row_stage(stage, x, kcs, between=None, chunks=None):
                per = kcs // 2
                units = dict(STAGES)[stage]
                for n in range(units):
                    c, k = n // per, n % per
                    if k == 0:
                        for t in range(TT):
                            wait_bank_free(pe, stage, 2 * c + t)
                    if c == 0 and chunks is not None:
                        pe.wait_ge(s_tl, TH0[chunks] + k + 1)
                    wait_unit(unit0(stage) + n)
                    mm_done(rows([bank_of(stage, 2 * c + t) for t in range(TT)], unit0(stage) + n, x, 2 * k,
                                 k == 0, k == per - 1))
                    if between is not None:
                        between(n)

            pe.wait_ge(s_id, 16)
            def first_columns(stage, transposed, chunks_before, beside=None):
                for q in range(2):
                    for k in range(4 * q, 4 * q + 4):
                        pe.wait_ge(s_rows, chunks_before + k // 2 + 1)
                        pe.wait_ge(s_rows1, chunks_before + k // 2 + 1)
                        split_transposes(transposed, k, row_chunk(res, k))
                for k in range(SIZE[stage]):
                    wait_bank_free(pe, stage, k)
                    if beside is not None:
                        beside(k)
                    for q in range(2):
                        u = unit0(stage) + 2 * k + q
                        if k == 0:
                            pe.wait_ge(s_tl, TH0[transposed] + 4 * q + 4)
                        wait_unit(u)
                        mm_done(columns(bank_of(stage, k), u, 0, actT, 8, 8 * q, q == 0, q == 1))

            first_columns("ssm_in", "t_in", 0)

            def bu_tile(s):
                q, r = s // 4, slice(32 * (s % 4), 32 * (s % 4) + 32)
                if s >= 2:
                    pe.wait_ge(s_bufree, s - 1)
                for ri in range(2):
                    last = pe.matmul(bank[4 + s % 2][:, T * ri:T * ri + T], bbT[r, 2 * q + ri, :], uT[r, q, :],
                                     start=True, stop=True)
                last.then_inc(s_bu, 1)

            def cx_tile(s):
                q, r = s // 4, slice(32 * (s % 4), 32 * (s % 4) + 32)
                pe.wait_ge(s_xr, s + 1)
                if s % 4 == 0 and q >= 2:
                    pe.wait_ge(s_y, q - 1)
                for ri in range(2):
                    last = pe.matmul(bank[6 + q % 2][r, 0:T], c_blk[:, s, ri, :], xs[s % 2][:, ri, :],
                                     start=(ri == 0), stop=(ri == 1))
                last.then_inc(s_cy, 1)

            def bu_beside(block):
                s = block - TILE_BLOCK
                if s == 0:
                    pe.wait_ge(s_bbTc, 4)
                    pe.wait_ge(*emptied("ssm_in", 7))
                if 0 <= s < STILES:
                    bu_tile(s)

            def ssm_beside(block):
                s = block - TILE_BLOCK
                if block == 2:
                    pe.wait_ge(s_bb, 1)
                    for k in range(4):
                        for n, (q, ri) in enumerate([(q, ri) for q in (2 * k, 2 * k + 1) for ri in range(2)]):
                            last = pe.transpose(bank[4 + k][:, n * P:(n + 1) * P], bb_rows[:, ri, q, :], ident[:])
                        last.then_inc(s_bbT, 1)
                if block == 10:
                    wait_bank_free(pe, "t_krows", 0)
                    pe.wait_ge(*emptied("k_rope", 0))
                    for t in range(TT):
                        last = pe.transpose(bank_of("t_krows", 0)[:, ROPE * t:ROPE * (t + 1)],
                                            kr_sum[:, t * P:(t + 1) * P], ident[0:ROPE, 0:ROPE])
                    last.then_inc(s_krt, 1)
                if block == 40:
                    pe.wait_ge(s_krot, 1)
                    pe.wait_ge(s_y, 8)
                    for k in range(4):
                        split_transposes("t_lat", k, row_chunk(lat, k))
                if 0 <= s - 2 < STILES:
                    cx_tile(s - 2)

            for c in range(2):
                for n in range(8):
                    u = unit0("latent") + 8 * c + n
                    if n == 0:
                        for t in range(TT):
                            wait_bank_free(pe, "latent", 2 * c + t)
                    wait_unit(u)
                    mm_done(rows([bank_of("latent", 2 * c + t) for t in range(TT)], u, actT, 2 * n, n == 0, n == 7))
                    (ssm_beside if n % 2 else bu_beside)((8 * c + n) // 2)
            wait_bank_free(pe, "k_rope", 0)
            u = unit0("latent") + 16
            wait_unit(u)
            b = bank_of("k_rope", 0)
            for k in range(KC):
                w = slice(ROPE * k, ROPE * (k + 1))
                pe.matmul(b[0:ROPE, :], hi[u % 4][:, w], actT[:, k, :, :].rearrange("p a t -> p (a t)"),
                          start=k == 0, stop=False)
                last = pe.matmul(b[0:ROPE, 0:T], lo[u % 4][:, w], actT[:, k, 0, :], start=False, stop=k == KC - 1)
            mm_done(last)
            bu_beside(8)
            ssm_beside(8)
            row_stage("gates", actT, KC, lambda n: (ssm_beside if n % 2 else bu_beside)(9 + n // 2))

            pe.wait_ge(s_yl, 8)
            for k in range(8):
                wait_bank_free(pe, "glu", k)
                wait_unit(unit0("glu") + k)
                mm_done(columns(bank_of("glu", k), unit0("glu") + k, 0, yT, 8, 0, True, True))
            pe.wait_ge(s_tl, TH0["t_lat"] + 4)

            def heads_columns(stage, kc0):
                for m in range(8):
                    wait_unit(unit0(stage) + m)
                    for k in (2 * m, 2 * m + 1):
                        wait_bank_free(pe, stage, k)
                        last = columns(bank_of(stage, k), unit0(stage) + m, 4 * (k % 2), latT, 4, kc0, True, True)
                    mm_done(last)

            row_stage("q_rope", latT, 4)
            heads_columns("q_nope", 0)
            heads_columns("k_nope", 4)
            wait_bank_free(pe, "t_kr", 0)
            transposes(bank_of("t_kr", 0), [kr_rows[:, t, :] for t in range(TT)], s_tr)
            pe.wait_ge(s_qr, TT)
            for k in range(4):
                wait_bank_free(pe, "t_qr", k)
                transposes(bank_of("t_qr", k), row_chunk(qr_rot, k), s_tr)
            for n in range(8):
                b, k = n // 2, n % 2
                if k == 0:
                    for t in range(TT):
                        wait_bank_free(pe, "value", 2 * b + t)
                wait_unit(unit0("value") + n)
                mm_done(rows([bank_of("value", 2 * b + t) for t in range(TT)], unit0("value") + n, latT, 4 + 2 * k,
                             k == 0, k == 1))

            def head_scores(h):
                if h >= 2:
                    pe.wait_ge(s_P, h - 1)
                r = slice(64 * (h % 2), 64 * (h % 2) + 64)
                for t, cols, keys in ((0, slice(0, P), slice(0, P)), (1, slice(P, 384), slice(0, T))):
                    q = slice(t * P, (t + 1) * P)
                    pe.matmul(bank[4 + h % 2][:, cols], qT[:, h, q], kT[:, h, keys], start=True, stop=False)
                    last = pe.matmul(bank[4 + h % 2][:, cols], qrT[r, h // 2, q], krT[r, keys],
                                     start=False, stop=True)
                last.then_inc(s_S, 1)

            pe.wait_ge(*emptied("k_nope", 15))
            pe.wait_ge(*emptied("value", 7))
            def head_out(h):
                pe.wait_ge(s_PTs, h + 1)
                if h >= 1:
                    pe.wait_ge(s_pvl, h)
                hd = slice(h * P, (h + 1) * P)
                pe.matmul(bank[7][:, 0:T], v0[:, hd], sm_pT[h % 2][:, 0:T], start=True, stop=False)
                pe.matmul(bank[7][:, P:T], v1[:, hd], sm_pT[h % 2][:, T:384], start=False,
                          stop=True).then_inc(s_PV, 1)

            def attention_beside(h):
                if h + 1 < HEADS:
                    head_scores(h + 1)
                head_transposes(h)

            def head_transposes(h):
                pe.wait_ge(s_Pn, h + 1)
                if h >= 1:
                    pe.wait_ge(s_PTs, h)
                for n in range(3):
                    last = pe.transpose(bank[6][:, n * P:(n + 1) * P], sm_p[h % 2][:, n * P:(n + 1) * P], ident[:])
                last.then_inc(s_PT, 1)

            pe.wait_ge(s_sl, 8)
            head_scores(0)
            attention_beside(0)
            for h in range(HEADS):
                c, k = h // 4, h % 4
                if k == 0:
                    for t in range(TT):
                        wait_bank_free(pe, "proj_ssm", 2 * c + t)
                u = unit0("proj_ssm") + h
                wait_unit(u)
                mm_done(rows([bank_of("proj_ssm", 2 * c + t) for t in range(TT)], u, ssmT, 2 * k, k == 0, k == 3))
                head_out(h)
                if h + 1 < HEADS:
                    attention_beside(h + 1)
            pe.wait_ge(s_pvl, HEADS)

            def mix_transposes(c):
                pe.wait_ge(s_mix, c + 1)
                for k in (2 * c, 2 * c + 1):
                    split_transposes("t_mix", k, [gates[:, 4 + x // 4, t, (x % 4) * P:(x % 4 + 1) * P]
                                                  for x in (2 * k, 2 * k + 1) for t in range(TT)])

            row_stage("proj_attn", actT, KC, lambda n: mix_transposes(n // 8 - 1) if n % 8 == 4 and n > 8 else None)
            mix_transposes(3)
            row_stage("out", mixT, KC, chunks="t_mix")
            def head_key_scores(h):
                pe.wait_ge(s_keys, 16)
                pe.wait_ge(*emptied("peer_q", 2 * h + 1))
                if h >= 4:
                    pe.wait_ge(s_scored, h - 3)
                for n in range(4):
                    t, hc = n // 2, 2 * h + n % 2
                    last = pe.matmul(bank[4 + h % 4][:, n * P:(n + 1) * P], pqT[:, hc, t * P:(t + 1) * P],
                                     keysT[:, hc, :], start=True, stop=True)
                last.then_inc(s_sc, 1)

            first_columns("peer_q", "t_h", 4, lambda k: head_key_scores(k // 2 - 2) if k > 3 and k % 2 == 0 else None)
            head_key_scores(6)

            def expert_unit(k, i, q):
                u = unit0("u") + 2 * k + q
                if q == 0:
                    pe.wait_ge(s_ev["D"], i * 4 + (emptied("u", k)[1] - 4))
                wait_unit(u, i, 8)
                mm_done(columns(bank_of("u", k), u, 0, actT, 8, 8 * q, q == 0, q == 1))

            def expert_block(k, i):
                expert_unit(k, i, 0)
                expert_unit(k, i, 1)

            def gate_matrices(g, i):
                pe.wait_ge(s_Gev, i * 4 + (g + 1))
                pe.wait_ge(s_one, i * 4 + (g + 1))
                pe.wait_ge(s_oneB, i * 4 + g)
                for t in range(GT):
                    last = pe.matmul(bank[4 + g % 2][:, P * t:P * (t + 1)], oneA[g % 2][:, t, :],
                                     oneB[g % 2][:, t, :], start=True, stop=True)
                last.then_inc(s_G, 1)

            head_key_scores(7)
            with pe.Fori(0, GELUS // 4) as i:
                for j in range(4):
                    expert_block(j, i)
            expert_block(GELUS, 0)
            expert_unit(GELUS + 1, 0, 0)
            pe.wait_ge(s_picked, 1)
            for t in range(TT):
                for n in range(3):
                    last = pe.transpose(bank[4 + t][:, n * P:(n + 1) * P],
                                        picked[:, n, 8 * t:8 * t + 8, :].rearrange("p h k -> p (h k)"), ident[:])
                last.then_inc(s_hk, 1)
            pe.sem_inc(s_G, 2)
            with pe.Fori(0, GELUS // 4 - 1) as i:
                for j in range(4):
                    expert_unit(GELUS + 1 + j, i, 1)
                    gate_matrices(j, i)
                    expert_unit(GELUS + 2 + j, i, 0)
            last_turn = GELUS // 4 - 1
            expert_unit(GELUS + 1, last_turn, 1)
            gate_matrices(0, last_turn)
            expert_block(GELUS + 2, last_turn)
            gate_matrices(1, last_turn)
            gate_matrices(2, last_turn)
            expert_unit(GELUS + 3, last_turn, 0)
            gate_matrices(3, last_turn)
            expert_unit(GELUS + 3, last_turn, 1)

            def out_steps(v, i=None):
                pe.wait_ge(s_wlm, v + 1 if i is None else i * 4 + (v + 1))
                for q in range(2):
                    u = unit0("v") + 2 * v + q
                    if i is None and v == 0:
                        pe.wait_ge(*emptied("u", NKEY - 2 + q))
                    wait_unit(u, i, 8)
                    for t in range(TT):
                        ts_ = slice(t * P, (t + 1) * P)
                        for w, v_ in ((wh, hi), (wh, lo), (wl, hi)):
                            for c in range(2):
                                last = pe.matmul(bank[4 * t + 2 * q + c][:], w[v % 2][:, ts_],
                                                 v_[u % 4][:, 512 * c:512 * (c + 1)],
                                                 start=v == 0 and i is None and w is wh and v_ is hi,
                                                 stop=v == NKEY - 1 and w is wl)
                    mm_done(last)

            pe.wait_ge(s_Gev, 2 + GELUS)
            for v in range(4):
                out_steps(v)
            with pe.Fori(0, NKEY // 4 - 2) as i:
                for j in range(4):
                    out_steps(4 + j, i)
            for v in range(NKEY - 4, NKEY):
                out_steps(v)


def row_blocks(w):
    k, n = w.shape
    return w.reshape(k // 512, 4, P, n // 512, 512).transpose(3, 0, 2, 1, 4).reshape(-1, P, SW)


def column_blocks(w):
    k, m = w.shape
    kc = k // P
    return w.reshape(kc, P, m // P, P).transpose(2, 1, 0, 3).reshape(m // P // (16 // kc), 16 // kc, P, kc * P) \
        .transpose(0, 2, 1, 3).reshape(-1, P, SW)


def stream(w):
    w_in, w_uq, w_ukv = w["w_in"][0], w["w_uq"][0], w["w_ukv"][0]
    o_q = SSM
    o_kv, o_kr = o_q + QL, o_q + 2 * QL
    o_g = o_kr + ROPE
    kr = w_in[:, o_kr:o_g].reshape(KC, P, ROPE).transpose(1, 0, 2).reshape(1, P, UW)
    uq = w_uq.reshape(QL, HEADS, NOPE + ROPE)
    ukv = w_ukv.reshape(QL, HEADS, 2 * NOPE)
    u = w["peer_u"][0].reshape(NKEY, NKEY, KC, P).transpose(1, 3, 2, 0).reshape(NKEY, P, SW)
    v = w["peer_v"][0].reshape(NKEY, NKEY, D).transpose(1, 0, 2)

    def units(blocks):
        return blocks.reshape(-1, P, 2, UW).transpose(0, 2, 1, 3).reshape(-1, P, UW)

    parts = [units(column_blocks(w_in[:, :SSM])), units(row_blocks(w_in[:, o_q:o_kr])), kr,
             units(row_blocks(w_in[:, o_g:])), units(column_blocks(w["w_glu"][0])),
             units(row_blocks(uq[:, :, NOPE:].reshape(QL, -1))), units(column_blocks(uq[:, :, :NOPE].reshape(QL, -1))),
             units(column_blocks(ukv[:, :, :NOPE].reshape(QL, -1))), units(row_blocks(ukv[:, :, NOPE:].reshape(QL, -1))),
             units(row_blocks(w["w_proj_ssm"][0])), units(row_blocks(w["w_proj_attn"][0])),
             units(row_blocks(w["w_out"][0])), units(column_blocks(w["w_peer_q"][0])), units(u), units(v)]
    return np.concatenate(parts)


def kernel(**inputs):
    import concourse.bacc as bacc
    from concourse.bass_utils import run_bass_kernel_spmd

    w = {k: np.asarray(v) for k, v in inputs.items()}
    half = ROPE // 2
    ang = np.arange(T, dtype=np.float32)[:, None] * (1.0 / (10000.0 ** (np.arange(half, dtype=np.float32) / half)))
    rope = np.stack([np.cos(ang), np.sin(ang)], 1).astype(np.float32)
    arrays = {
        "x": w["x"].reshape(T, D),
        "stream": stream(w),
        "rope": rope.reshape(TT, P, 2, half).transpose(1, 0, 2, 3),
        "ident": np.eye(P, dtype=np.float32),
        "lam_re": w["ssm_lam_re"][0].reshape(STILES, P).T,
        "lam_im": w["ssm_lam_im"][0].reshape(STILES, P).T,
        "log_dt": w["ssm_log_dt"][0].reshape(STILES, 2).T,
        "b_re": w["ssm_b_re"][0].reshape(STILES, P, 16).transpose(1, 0, 2),
        "b_im": w["ssm_b_im"][0].reshape(STILES, P, 16).transpose(1, 0, 2),
        "c_re": w["ssm_c_re"][0].reshape(STILES, 2, 16, 64).transpose(1, 3, 0, 2).reshape(P, STILES, 16),
        "c_im": w["ssm_c_im"][0].reshape(STILES, 2, 16, 64).transpose(1, 3, 0, 2).reshape(P, STILES, 16),
        "dskip": w["ssm_d"][0].reshape(8, P).T,
        "keysT": w["peer_sub_keys"][0].reshape(16, NKEY, P).transpose(2, 0, 1),
    }
    for name in ("ln_in_g", "ln_in_b", "ln_mix_g", "ln_mix_b", "ln_ffn_g", "ln_ffn_b", "q_norm_g", "kv_norm_g"):
        arrays[name] = w[name].reshape(1, -1)
    arrays = {k: np.ascontiguousarray(v) for k, v in arrays.items()}
    nc = bacc.Bacc("TRN2", target_bir_lowering=False, num_devices=1, dynamic_dma_scratch_size=512)
    a = {k: nc.dram_tensor(f"in_{k}", v.shape, F32, kind="ExternalInput").ap() for k, v in arrays.items()}
    a["spill"] = nc.dram_tensor("residual_spill", (TT, P, D), F32).ap()
    out = nc.dram_tensor("out", (T, D), F32, kind="ExternalOutput").ap()
    build(nc, a, out)
    r = run_bass_kernel_spmd(nc, [{f"in_{k}": v for k, v in arrays.items()}], core_ids=[0])
    return r.results[0]["out"].reshape(w["x"].shape)
```
